# Optimizing a Trainium2 kernel written in Bass

```python
import jax, jax.numpy as jnp
from jax import lax
import numpy as np
import jax
import jax.numpy as jnp

D_MODEL = 1024
BATCH = 1
SEQ = 256
DEPTH = 1

D_CONV = D_MODEL // 2
D_POOL = D_MODEL // 2
D_SC = D_MODEL // 2
CONV_A_K = 31
SC_K = 3
POOL_WINDOWS = (2, 4, 8, 16)
N_POOL_GROUPS = len(POOL_WINDOWS)
POOL_GROUP_DIM = D_POOL // N_POOL_GROUPS
POOL_OUT_DIM = D_MODEL // N_POOL_GROUPS
MAX_WINDOW = max(POOL_WINDOWS)
N_BRANCH = 3
PROJ_SPLITS = (D_CONV, 2 * D_CONV, 2 * D_CONV + D_POOL, 2 * D_CONV + D_POOL + D_SC,
               2 * D_CONV + D_POOL + 2 * D_SC, 2 * D_CONV + D_POOL + 3 * D_SC)
D_IN_PROJ = 2 * D_CONV + D_POOL + 3 * D_SC + N_BRANCH * D_MODEL
N_MEM = 256
XATTN_HEADS = 4
XATTN_HEAD_DIM = D_MODEL // XATTN_HEADS
MOE_GROUPS = 4
EXPERTS_PER_GROUP = 4
N_EXPERTS = MOE_GROUPS * EXPERTS_PER_GROUP
EXPERT_TOP_K = 2
D_EXPERT = D_MODEL // 4
EPS = 1e-6


def rmsnorm(x, g):
    xf = x.astype(jnp.float32)
    y = xf * lax.rsqrt(jnp.mean(xf * xf, axis=-1, keepdims=True) + EPS)
    return (y * g.astype(jnp.float32)).astype(x.dtype)

def layernorm(x, g, b):
    xf = x.astype(jnp.float32)
    mu = jnp.mean(xf, axis=-1, keepdims=True)
    var = jnp.mean(jnp.square(xf - mu), axis=-1, keepdims=True)
    y = (xf - mu) * lax.rsqrt(var + EPS)
    return (y * g.astype(jnp.float32) + b.astype(jnp.float32)).astype(x.dtype)

def causal_dwconv(u, w):
    k = w.shape[0]
    u_pad = jnp.pad(u, ((0, 0), (k - 1, 0), (0, 0)))
    return lax.conv_general_dilated(
        u_pad, w[:, None, :].astype(u.dtype), window_strides=(1,), padding='VALID',
        dimension_numbers=('NWC', 'WIO', 'NWC'), feature_group_count=u.shape[-1])

def multiscale_pool_minus_token(u):
    s = u.shape[1]
    uf = u.astype(jnp.float32)
    cs = jnp.cumsum(uf, axis=1)
    cs_pad = jnp.pad(cs, ((0, 0), (MAX_WINDOW, 0), (0, 0)))
    t = jnp.arange(s, dtype=jnp.int32)
    outs = []
    for i, w in enumerate(POOL_WINDOWS):
        c0, c1 = i * POOL_GROUP_DIM, (i + 1) * POOL_GROUP_DIM
        prev = cs_pad[:, MAX_WINDOW - w:MAX_WINDOW - w + s, c0:c1]
        cnt = jnp.minimum(t + 1, w).astype(jnp.float32)[None, :, None]
        outs.append((cs[:, :, c0:c1] - prev) / cnt - uf[:, :, c0:c1])
    return jnp.concatenate(outs, axis=-1).astype(u.dtype)

def gated_branch_mixer(h, w_in, conv_a_w, conv_a_b, ln_a_g, ln_a_b, w_a_out,
                       w_pool_grp, pool_scale, conv_c_w, w_c_out, w_o):
    bsz, s, _ = h.shape
    proj = h @ w_in
    a_val, a_gate, u_pool, c_x, c_b, c_c, g = jnp.split(proj, PROJ_SPLITS, axis=-1)
    a = a_val * jax.nn.sigmoid(a_gate)
    a = causal_dwconv(a, conv_a_w) + conv_a_b
    a = jax.nn.silu(layernorm(a, ln_a_g, ln_a_b)) @ w_a_out
    p = multiscale_pool_minus_token(u_pool).reshape(bsz, s, N_POOL_GROUPS, POOL_GROUP_DIM)
    p = jnp.einsum('bsgc,gco->bsgo', p, w_pool_grp).reshape(bsz, s, D_MODEL) * pool_scale
    c = (c_b * causal_dwconv(c_c * c_x, conv_c_w)) @ w_c_out
    gates = jax.nn.sigmoid(g).reshape(bsz, s, N_BRANCH, D_MODEL)
    merged = gates[:, :, 0] * a + gates[:, :, 1] * p + gates[:, :, 2] * c
    return merged @ w_o

def memory_cross_attention(h, mem_n, w_xq, w_xkv, w_xo):
    bsz, s, _ = h.shape
    q = (h @ w_xq).reshape(bsz, s, XATTN_HEADS, XATTN_HEAD_DIM)
    k, v = jnp.split(mem_n @ w_xkv, 2, axis=-1)
    k = k.reshape(bsz, N_MEM, XATTN_HEADS, XATTN_HEAD_DIM)
    v = v.reshape(bsz, N_MEM, XATTN_HEADS, XATTN_HEAD_DIM)
    scores = jnp.einsum('bshd,bmhd->bhsm', q, k).astype(jnp.float32) * (XATTN_HEAD_DIM ** -0.5)
    probs = jax.nn.softmax(scores, axis=-1).astype(v.dtype)
    o = jnp.einsum('bhsm,bmhd->bshd', probs, v).reshape(bsz, s, D_MODEL)
    return o @ w_xo

def hierarchical_moe(h, w_rg, b_rg, w_re, b_re, w_e_gate, w_e_up, w_e_down):
    bsz, s, d = h.shape
    t = h.reshape(-1, d)
    n = t.shape[0]
    p_grp = jax.nn.softmax((t @ w_rg + b_rg).astype(jnp.float32), axis=-1)
    g_val, g_idx = lax.top_k(p_grp, 1)
    le = (t @ w_re + b_re).astype(jnp.float32).reshape(n, MOE_GROUPS, EXPERTS_PER_GROUP)
    le_sel = jnp.take_along_axis(le, g_idx[:, :, None], axis=1)[:, 0]
    p_exp = jax.nn.softmax(le_sel, axis=-1)
    e_val, e_idx = lax.top_k(p_exp, EXPERT_TOP_K)
    e_val = e_val / jnp.sum(e_val, axis=-1, keepdims=True)
    weight = g_val * e_val
    eid = g_idx * EXPERTS_PER_GROUP + e_idx
    gate = jnp.sum(jax.nn.one_hot(eid, N_EXPERTS, dtype=jnp.float32) * weight[..., None], axis=1)
    act = jax.nn.silu(jnp.einsum('nd,edf->nef', t, w_e_gate)) * jnp.einsum('nd,edf->nef', t, w_e_up)
    act = act * gate[:, :, None].astype(act.dtype)
    out = jnp.einsum('nef,efd->nd', act, w_e_down)
    return out.reshape(bsz, s, d)

def first_inputs(seed: int = 0) -> dict:
    key = jax.random.key(seed)
    ks = jax.random.split(key, 32)
    f32 = jnp.float32

    def nrm(k, shape, scale):
        return jax.random.normal(k, shape, f32) * scale

    def gain(k, shape):
        return 1.0 + 0.02 * jax.random.normal(k, shape, f32)

    L = DEPTH
    return {
        "x": nrm(ks[0], (BATCH, SEQ, D_MODEL), 1.0),
        "mem": nrm(ks[1], (BATCH, N_MEM, D_MODEL), 1.0),
        "norm_mix_g": gain(ks[2], (L, D_MODEL)),
        "w_in": nrm(ks[3], (L, D_MODEL, D_IN_PROJ), D_MODEL ** -0.5),
        "conv_a_w": nrm(ks[4], (L, CONV_A_K, D_CONV), CONV_A_K ** -0.5),
        "conv_a_b": nrm(ks[5], (L, D_CONV), 0.02),
        "ln_a_g": gain(ks[6], (L, D_CONV)),
        "ln_a_b": nrm(ks[7], (L, D_CONV), 0.02),
        "w_a_out": nrm(ks[8], (L, D_CONV, D_MODEL), D_CONV ** -0.5),
        "w_pool_grp": nrm(ks[9], (L, N_POOL_GROUPS, POOL_GROUP_DIM, POOL_OUT_DIM), POOL_GROUP_DIM ** -0.5),
        "pool_scale": gain(ks[10], (L, D_MODEL)),
        "conv_c_w": nrm(ks[11], (L, SC_K, D_SC), SC_K ** -0.5),
        "w_c_out": nrm(ks[12], (L, D_SC, D_MODEL), D_SC ** -0.5),
        "w_o": nrm(ks[13], (L, D_MODEL, D_MODEL), D_MODEL ** -0.5),
        "norm_x_g": gain(ks[14], (L, D_MODEL)),
        "norm_mem_g": gain(ks[15], (L, D_MODEL)),
        "w_xq": nrm(ks[16], (L, D_MODEL, D_MODEL), D_MODEL ** -0.5),
        "w_xkv": nrm(ks[17], (L, D_MODEL, 2 * D_MODEL), D_MODEL ** -0.5),
        "w_xo": nrm(ks[18], (L, D_MODEL, D_MODEL), D_MODEL ** -0.5),
        "norm_ffn_g": gain(ks[19], (L, D_MODEL)),
        "w_rg": nrm(ks[20], (L, D_MODEL, MOE_GROUPS), D_MODEL ** -0.5),
        "b_rg": nrm(ks[21], (L, MOE_GROUPS), 0.01),
        "w_re": nrm(ks[22], (L, D_MODEL, N_EXPERTS), D_MODEL ** -0.5),
        "b_re": nrm(ks[23], (L, N_EXPERTS), 0.01),
        "w_e_gate": nrm(ks[24], (L, N_EXPERTS, D_MODEL, D_EXPERT), D_MODEL ** -0.5),
        "w_e_up": nrm(ks[25], (L, N_EXPERTS, D_MODEL, D_EXPERT), D_MODEL ** -0.5),
        "w_e_down": nrm(ks[26], (L, N_EXPERTS, D_EXPERT, D_MODEL), D_EXPERT ** -0.5),
        "norm_f_g": gain(ks[27], (D_MODEL,)),
    }

def first_block(x, mem, norm_mix_g, w_in, conv_a_w, conv_a_b, ln_a_g, ln_a_b, w_a_out,
              w_pool_grp, pool_scale, conv_c_w, w_c_out, w_o, norm_x_g, norm_mem_g,
              w_xq, w_xkv, w_xo, norm_ffn_g, w_rg, b_rg, w_re, b_re,
              w_e_gate, w_e_up, w_e_down, norm_f_g):
    for l in range(DEPTH):
        h = rmsnorm(x, norm_mix_g[l])
        x = x + gated_branch_mixer(h, w_in[l], conv_a_w[l], conv_a_b[l], ln_a_g[l], ln_a_b[l],
                                   w_a_out[l], w_pool_grp[l], pool_scale[l], conv_c_w[l],
                                   w_c_out[l], w_o[l])
        x = x + memory_cross_attention(rmsnorm(x, norm_x_g[l]), rmsnorm(mem, norm_mem_g[l]),
                                       w_xq[l], w_xkv[l], w_xo[l])
        x = x + hierarchical_moe(rmsnorm(x, norm_ffn_g[l]), w_rg[l], b_rg[l], w_re[l], b_re[l],
                                 w_e_gate[l], w_e_up[l], w_e_down[l])
    return rmsnorm(x, norm_f_g)


GRID_W = 64

ATT_HEADS = 8
ATT_KV_HEADS = 2
ATT_HEAD_DIM = 64
ATT_Q_DIM = ATT_HEADS * ATT_HEAD_DIM
ATT_KV_DIM = ATT_KV_HEADS * ATT_HEAD_DIM
ATT_BLOCK = 128
ROPE_THETA = 10000.0
ROPE_PAIRS_PER_AXIS = ATT_HEAD_DIM // 4

HG_HEADS = 4
HG_HEAD_K = 128
HG_HEAD_V = 128
HG_KEY_DIM = HG_HEADS * HG_HEAD_K
HG_VAL_DIM = HG_HEADS * HG_HEAD_V
HG_CHUNK = 32

MIX_WIDTH = ATT_Q_DIM + HG_VAL_DIM
IN_SPLITS = (ATT_Q_DIM, ATT_KV_DIM, ATT_KV_DIM, HG_KEY_DIM, HG_KEY_DIM, HG_KEY_DIM, HG_VAL_DIM, HG_VAL_DIM)
N_IN = ATT_Q_DIM + 2 * ATT_KV_DIM + 3 * HG_KEY_DIM + 2 * HG_VAL_DIM

X_HEADS = 4
X_HEAD_DIM = D_MODEL // X_HEADS

D_FF = 2816
CONV_W = 3


def rmsnorm_2(x, g):
    xf = x.astype(jnp.float32)
    y = xf * lax.rsqrt(jnp.mean(xf * xf, axis=-1, keepdims=True) + EPS)
    return (y * g.astype(jnp.float32)).astype(x.dtype)

def split_columns(p, sizes):
    idx = np.cumsum(np.array(sizes))[:-1].tolist()
    return jnp.split(p, idx, axis=-1)

def axial_rope_tables(n):
    rows = n // GRID_W
    r, c = jnp.meshgrid(jnp.arange(rows), jnp.arange(GRID_W), indexing="ij")
    inv = jnp.power(ROPE_THETA, -jnp.arange(ROPE_PAIRS_PER_AXIS, dtype=jnp.float32) / ROPE_PAIRS_PER_AXIS)
    ang = jnp.concatenate([r.reshape(-1, 1).astype(jnp.float32) * inv,
                           c.reshape(-1, 1).astype(jnp.float32) * inv], axis=-1)
    return jnp.cos(ang), jnp.sin(ang)

def apply_rope(x, cos, sin):
    b, n, h, d = x.shape
    xp = x.reshape(b, n, h, d // 2, 2)
    x0, x1 = xp[..., 0], xp[..., 1]
    c = cos[None, :, None, :].astype(x.dtype)
    s = sin[None, :, None, :].astype(x.dtype)
    return jnp.stack([x0 * c - x1 * s, x0 * s + x1 * c], axis=-1).reshape(b, n, h, d)

def axial_gqa_attention(q, k, v):
    b, n = q.shape[0], q.shape[1]
    grp = ATT_HEADS // ATT_KV_HEADS
    nb = n // ATT_BLOCK
    qb = jnp.moveaxis(q.reshape(b, nb, ATT_BLOCK, ATT_KV_HEADS, grp, ATT_HEAD_DIM), 1, 0)
    scale = ATT_HEAD_DIM ** -0.5

    def one_block(qblk):
        s = jnp.einsum("bqhgd,bkhd->bhgqk", qblk, k).astype(jnp.float32) * scale
        p = jax.nn.softmax(s, axis=-1).astype(v.dtype)
        return jnp.einsum("bhgqk,bkhd->bqhgd", p, v)

    o = lax.map(one_block, qb)
    return jnp.moveaxis(o, 0, 1).reshape(b, n, ATT_Q_DIM)

def bidirectional_gated_scan(q, logf_fwd, logf_bwd, v):
    b, n, h, kd = q.shape
    vd = v.shape[-1]
    nc = n // HG_CHUNK

    def flip(a):
        return a[:, ::-1]

    qs = jnp.stack([q, flip(q)])
    lf = jnp.stack([logf_fwd, flip(logf_bwd)])
    vs = jnp.stack([v, flip(v)])
    ks = -jnp.expm1(lf)

    def to_chunks(a):
        a = a.reshape(2, b, nc, HG_CHUNK, h, a.shape[-1])
        return jnp.transpose(a, (2, 0, 1, 4, 3, 5))

    tri = jnp.tril(jnp.ones((HG_CHUNK, HG_CHUNK), dtype=bool))[:, :, None]

    def step(S, xs):
        qx, kx, vx, lx = xs
        bcum = jnp.cumsum(lx, axis=-2)
        diff = bcum[..., :, None, :] - bcum[..., None, :, :]
        dec = jnp.exp(jnp.where(tri, diff, -jnp.inf))
        a = jnp.einsum("...tk,...sk,...tsk->...ts", qx, kx, dec)
        o_intra = jnp.einsum("...ts,...sv->...tv", a, vx)
        o_inter = jnp.einsum("...tk,...kv->...tv", qx * jnp.exp(bcum), S)
        b_last = bcum[..., -1:, :]
        k_dec = kx * jnp.exp(b_last - bcum)
        S_new = jnp.exp(b_last[..., 0, :])[..., :, None] * S + jnp.einsum("...sk,...sv->...kv", k_dec, vx)
        return S_new, o_intra + o_inter

    S0 = jnp.zeros((2, b, h, kd, vd), jnp.float32)
    _, out = lax.scan(step, S0, (to_chunks(qs), to_chunks(ks), to_chunks(vs), to_chunks(lf)))
    out = jnp.transpose(out, (1, 2, 0, 4, 3, 5)).reshape(2, b, n, h, vd)
    return out[0] + flip(out[1])

def hgrn2_group(q, zf_fwd, zf_bwd, i_in, g, lb, out_g):
    b, n = q.shape[0], q.shape[1]

    def heads(a, d):
        return a.reshape(b, n, HG_HEADS, d)

    def log_forget(z, lb_dir):
        f = lb_dir + (1.0 - lb_dir) * jax.nn.sigmoid(z.astype(jnp.float32))
        return heads(jnp.log(f), HG_HEAD_K)

    qf = heads(jax.nn.silu(q.astype(jnp.float32)), HG_HEAD_K)
    o = bidirectional_gated_scan(qf, log_forget(zf_fwd, lb[0]), log_forget(zf_bwd, lb[1]),
                                 heads(i_in.astype(jnp.float32), HG_HEAD_V))
    o = rmsnorm_2(o, out_g).reshape(b, n, HG_VAL_DIM)
    return (o * jax.nn.silu(g.astype(jnp.float32))).astype(g.dtype)

def memory_cross_attention_2(h, m, wq, wkv, wo):
    b, n = h.shape[0], h.shape[1]
    nm = m.shape[1]
    q = (h @ wq).reshape(b, n, X_HEADS, X_HEAD_DIM)
    kv = (m @ wkv).reshape(b, nm, 2, X_HEADS, X_HEAD_DIM)
    k, v = kv[:, :, 0], kv[:, :, 1]
    s = jnp.einsum("bqhd,bkhd->bhqk", q, k).astype(jnp.float32) * (X_HEAD_DIM ** -0.5)
    p = jax.nn.softmax(s, axis=-1).astype(v.dtype)
    o = jnp.einsum("bhqk,bkhd->bqhd", p, v).reshape(b, n, X_HEADS * X_HEAD_DIM)
    return o @ wo

def conv_ffn(h, w_up, conv_w, conv_b, w_down):
    n = h.shape[1]
    u = h @ w_up
    half = CONV_W // 2
    up = jnp.pad(u, ((0, 0), (half, half), (0, 0)))
    acc = conv_b
    for j in range(CONV_W):
        acc = acc + up[:, j:j + n] * conv_w[j]
    gate, val = jnp.split(acc, 2, axis=-1)
    return (jax.nn.silu(gate) * val) @ w_down

def second_inputs(seed: int = 0) -> dict:
    key = jax.random.key(seed)
    ks = jax.random.split(key, 22)
    f32 = jnp.float32
    L = DEPTH

    def nrm(k, shape, scale):
        return jax.random.normal(k, shape, f32) * scale

    def gain(k, shape):
        return 1.0 + nrm(k, shape, 0.05)

    return {
        "x": nrm(ks[0], (BATCH, SEQ, D_MODEL), 1.0),
        "mem": nrm(ks[1], (BATCH, N_MEM, D_MODEL), 1.0),
        "pre_mix_g": gain(ks[2], (L, D_MODEL)),
        "w_in": nrm(ks[3], (L, D_MODEL, N_IN), D_MODEL ** -0.5),
        "q_norm_g": gain(ks[4], (L, ATT_HEAD_DIM)),
        "k_norm_g": gain(ks[5], (L, ATT_HEAD_DIM)),
        "hg_lb": nrm(ks[6], (2, L + 1, HG_KEY_DIM), 0.5),
        "hg_out_norm_g": gain(ks[7], (L, HG_HEAD_V)),
        "w_out": nrm(ks[8], (L, MIX_WIDTH, D_MODEL), MIX_WIDTH ** -0.5),
        "post_mix_g": gain(ks[9], (L, D_MODEL)),
        "pre_x_g": gain(ks[10], (L, D_MODEL)),
        "mem_norm_g": gain(ks[11], (L, D_MODEL)),
        "w_xq": nrm(ks[12], (L, D_MODEL, D_MODEL), D_MODEL ** -0.5),
        "w_xkv": nrm(ks[13], (L, D_MODEL, 2 * D_MODEL), D_MODEL ** -0.5),
        "w_xo": nrm(ks[14], (L, D_MODEL, D_MODEL), D_MODEL ** -0.5),
        "post_x_g": gain(ks[15], (L, D_MODEL)),
        "pre_ffn_g": gain(ks[16], (L, D_MODEL)),
        "w_up": nrm(ks[17], (L, D_MODEL, 2 * D_FF), D_MODEL ** -0.5),
        "conv_w": nrm(ks[18], (L, CONV_W, 2 * D_FF), CONV_W ** -0.5),
        "conv_b": nrm(ks[19], (L, 2 * D_FF), 0.02),
        "w_down": nrm(ks[20], (L, D_FF, D_MODEL), D_FF ** -0.5),
        "post_ffn_g": gain(ks[21], (L, D_MODEL)),
    }

def second_block(x, mem, pre_mix_g, w_in, q_norm_g, k_norm_g, hg_lb, hg_out_norm_g, w_out, post_mix_g,
              pre_x_g, mem_norm_g, w_xq, w_xkv, w_xo, post_x_g, pre_ffn_g, w_up, conv_w, conv_b,
              w_down, post_ffn_g):
    b, n = x.shape[0], x.shape[1]
    cos, sin = axial_rope_tables(n)
    lb_all = jnp.cumsum(jax.nn.softmax(hg_lb.astype(jnp.float32), axis=1), axis=1)
    for l in range(DEPTH):
        h = rmsnorm_2(x, pre_mix_g[l])
        aq, ak, av, hq, hf_fwd, hf_bwd, hi, hg = split_columns(h @ w_in[l], IN_SPLITS)
        aq = rmsnorm_2(aq.reshape(b, n, ATT_HEADS, ATT_HEAD_DIM), q_norm_g[l])
        ak = rmsnorm_2(ak.reshape(b, n, ATT_KV_HEADS, ATT_HEAD_DIM), k_norm_g[l])
        av = av.reshape(b, n, ATT_KV_HEADS, ATT_HEAD_DIM)
        att = axial_gqa_attention(apply_rope(aq, cos, sin), apply_rope(ak, cos, sin), av)
        rec = hgrn2_group(hq, hf_fwd, hf_bwd, hi, hg, lb_all[:, l], hg_out_norm_g[l])
        mixed = jnp.concatenate([att, rec], axis=-1) @ w_out[l]
        x = x + rmsnorm_2(mixed, post_mix_g[l])
        h = rmsnorm_2(x, pre_x_g[l])
        m = rmsnorm_2(mem, mem_norm_g[l])
        x = x + rmsnorm_2(memory_cross_attention_2(h, m, w_xq[l], w_xkv[l], w_xo[l]), post_x_g[l])
        h = rmsnorm_2(x, pre_ffn_g[l])
        x = x + rmsnorm_2(conv_ffn(h, w_up[l], conv_w[l], conv_b[l], w_down[l]), post_ffn_g[l])
    return x


def setup_inputs(seed=0):
    out = dict(first_inputs(seed))
    for name, value in second_inputs(seed + 1).items():
        if name != "x":
            out[name + "_2"] = value
    return out


def reference(
    x, mem, norm_mix_g, w_in, conv_a_w, conv_a_b, ln_a_g, ln_a_b, w_a_out, w_pool_grp,
    pool_scale, conv_c_w, w_c_out, w_o, norm_x_g, norm_mem_g, w_xq, w_xkv, w_xo, norm_ffn_g,
    w_rg, b_rg, w_re, b_re, w_e_gate, w_e_up, w_e_down, norm_f_g, mem_2, pre_mix_g_2, w_in_2,
    q_norm_g_2, k_norm_g_2, hg_lb_2, hg_out_norm_g_2, w_out_2, post_mix_g_2, pre_x_g_2,
    mem_norm_g_2, w_xq_2, w_xkv_2, w_xo_2, post_x_g_2, pre_ffn_g_2, w_up_2, conv_w_2, conv_b_2,
    w_down_2, post_ffn_g_2,
):
    x = first_block(
        x, mem, norm_mix_g, w_in, conv_a_w, conv_a_b, ln_a_g, ln_a_b, w_a_out, w_pool_grp,
        pool_scale, conv_c_w, w_c_out, w_o, norm_x_g, norm_mem_g, w_xq, w_xkv, w_xo, norm_ffn_g,
        w_rg, b_rg, w_re, b_re, w_e_gate, w_e_up, w_e_down, norm_f_g,
    )
    return second_block(
        x, mem_2, pre_mix_g_2, w_in_2, q_norm_g_2, k_norm_g_2, hg_lb_2, hg_out_norm_g_2,
        w_out_2, post_mix_g_2, pre_x_g_2, mem_norm_g_2, w_xq_2, w_xkv_2, w_xo_2, post_x_g_2,
        pre_ffn_g_2, w_up_2, conv_w_2, conv_b_2, w_down_2, post_ffn_g_2,
    )


_drawn_inputs = setup_inputs


def setup_inputs(seed=0):
    import zlib

    import numpy as np

    out = dict(_drawn_inputs(seed))
    spreads = {}
    factors = {'pool_scale': 3.448,
     'norm_x_g': 8.0,
     'norm_mem_g': 3.503,
     'b_rg': 28.109,
     'b_re': 22.265,
     'q_norm_g_2': 8.0,
     'k_norm_g_2': 6.54,
     'conv_b_2': 3.912,
     'hg_lb_2': 2.778,
     'hg_out_norm_g_2': 3.006}
    for name, (base, spread) in spreads.items():
        noise = np.random.default_rng([zlib.crc32(name.encode()), seed]).standard_normal(out[name].shape)
        drawn = base * np.exp(spread * noise) if base else spread * noise
        out[name] = jnp.asarray(drawn.astype(out[name].dtype))
    for name, factor in factors.items():
        out[name] = (out[name] * factor).astype(out[name].dtype)
    return out
```

```python
from contextlib import ExitStack

import numpy as np
import concourse.bass as bass
from concourse import mybir

ALU = mybir.AluOpType
ACT = mybir.ActivationFunctionType
F32 = mybir.dt.float32
I32 = mybir.dt.int32
AX_X = mybir.AxisListType.X

P = 128
T = 256
TT = T // P
D = 1024
DK = D // P
EPS = 1e-6
CW = 2048
SLOTS = 6
UNITS = 4
SB = 3
STAT = 7
ACC = 4
CONV_K = 31
C_K = 3
POOL_W = (2, 4, 8, 16)
PADW = 16
EXPERTS = 16
GROUPS = 4
FF = 2816
FSTEPS = FF // 256
HG = 4
QH = 8
NEG = -1.0e30

C_WIN = 0
C_POOL = C_WIN + 24
C_MERGE = C_POOL + 1
C_K1 = C_MERGE + 4
C_WO = C_K1 + 4
C_V1 = C_WO + 4
C_Q1 = C_V1 + 4
C_XO1 = C_Q1 + 4
C_MOE = C_XO1 + 4
C_K2 = C_MOE + 3 * EXPERTS
C_WIN2 = C_K2 + 4
C_V2 = C_WIN2 + 13
C_WO2 = C_V2 + 4
C_Q2 = C_WO2 + 4
C_XO2 = C_Q2 + 4
C_FFN = C_XO2 + 4
CHUNKS = C_FFN + 3 * FSTEPS
WIN2_ORDER = (3, 4, 5, 6, 7, 8, 9, 10, 11, 12, 0, 1, 2)

U_MOE_FIRST = 64
U_MOE = U_MOE_FIRST + 2 + EXPERTS // 2
U_WIN2 = U_MOE + 2 * (EXPERTS - 1) + 4
U_REC = 162
U_WO2 = U_REC + 4
U_XO2 = U_WO2 + 4 + 4 + 8

SMALL = {}
_at = 0
for _name, _n in (("mix_g", 8), ("pool_s", 8), ("x_g", 8), ("mem_g", 8), ("ffn_g", 8), ("f_g", 8),
                  ("conv_b", 4), ("ln_g", 4), ("ln_b", 4), ("c_w", 4 * C_K), ("conv_w", 4 * CONV_K),
                  ("pre_mix_g", 8), ("post_mix_g", 8), ("pre_x_g", 8), ("mem2_g", 8), ("post_x_g", 8),
                  ("pre_ffn_g", 8), ("post_ffn_g", 8), ("hg_g", 1), ("q_g", 1), ("k_g", 1),
                  ("lb", 16), ("r_b", 1), ("ffn_w", 16 * FSTEPS)):
    SMALL[_name] = _at
    _at += _n
NSMALL = _at

CONST = {}
_at = 0
for _name, _n in (("ident", 128), ("ones", 128), ("rcnt", 4 * T), ("cos", T), ("sin", T), ("rot", 128),
                  ("dup", 256), ("qk_sum", 5 * 10), ("qk_row", 5 * 128), ("hg_sum", 16), ("hg_row", 512),
                  ("prio", 8)):
    CONST[_name] = _at
    _at += _n
NCONST = _at


def build(nc, stream, xt_in, memt_in, mem2t_in, small_in, const_in, mask_in, router_in, out_t):
    ctx = ExitStack()
    with ctx:
        def sb(name, shape, dt=F32):
            return ctx.enter_context(nc.sbuf_tensor(name, shape, dt))

        def sem(name):
            return ctx.enter_context(nc.semaphore(name))

        psum = ctx.enter_context(nc.psum_tensor("psum", [P, 8, 512], F32))

        ring = sb("ring", [P, SLOTS, CW])
        xT = sb("xT", [P, DK, T])
        xg = sb("xg", [P, DK, T])
        sq = sb("sq", [P, DK, T])
        memn = sb("memn", [P, 2, DK, T])
        kT = sb("kT", [P, DK, T])
        vm = sb("vm", [P, TT, D])
        small = sb("small", [P, NSMALL])
        const = sb("const", [P, NCONST])
        mask = sb("mask", [P, 8, P], I32)
        router = sb("router", [P, DK, 20])
        rstd = sb("rstd", [P, 4, T])
        std = sb("std", [P, T])
        av2 = sb("av2", [P, TT, 128])
        cden = sb("cden", [16, 2, T])
        zeros = sb("zeros", [P, P])
        eps = sb("eps", [P, 1])
        nmax = sb("nmax", [P, 16, TT])
        negm = sb("negm", [P, 16, TT])
        ssum = sb("ssum", [P, 16, TT])
        rsum = sb("rsum", [P, 16, TT])
        cols = sb("cols", [P, 2, TT])
        lbt = sb("lbt", [P, 8, 8])
        WORK = 18432
        work = sb("work", [P, WORK])

        def sm(name, i=0, n=1):
            return small[:, SMALL[name] + i:SMALL[name] + i + n]

        def cn(name, i=0, n=128, p=P):
            return const[0:p, CONST[name] + i:CONST[name] + i + n]

        ident = cn("ident")
        ones = cn("ones")

        class Region:

            def __init__(self, start=0):
                self.at = start

            def __call__(self, *dims):
                n = int(np.prod(dims))
                v = work[:, self.at:self.at + n]
                self.at += n
                assert self.at <= WORK, self.at
                if len(dims) == 2:
                    v = v.rearrange("p (a b) -> p a b", a=dims[0])
                elif len(dims) == 3:
                    v = v.rearrange("p (a b c) -> p a b c", a=dims[0], b=dims[1])
                return v

        r = Region()
        gates = r(24, T)
        aval = r(4, T)
        agate = r(4, T)
        apad = r(4, T + CONV_K - 1)
        aacc = r(4, T)
        lnstd = r(T)
        lnrstd = r(T)
        cx = r(4, T)
        cpad = r(4, T + C_K - 1)
        pT = r(4, T)
        upad = r(4, T + PADW)
        ubuf = r(4, T + PADW)
        asq = agate
        actT = aval
        cc, ctmp = kT[:, 0:4, :], kT[:, 4:8, :]
        vm_flat = vm.rearrange("p t d -> p (t d)")
        cb = vm_flat[:, 0:4 * T].rearrange("p (a b) -> p a b", a=4)
        cy = vm_flat[:, 4 * T:8 * T].rearrange("p (a b) -> p a b", a=4)
        merged = work[:, r.at - 8 * (T + PADW):r.at - 8 * (T + PADW) + DK * T].rearrange("p (a b) -> p a b", a=DK)
        mt1, mt2 = agate, aacc

        r = Region(14336)
        probs = r(4, TT, T)
        probsT = r(4, TT, T)
        r = Region(0)
        qT = r(DK, T)
        oT = r(DK, T)
        yT = r(DK, T)

        r = Region(0)
        rg = r(EXPERTS, T)
        gs = r(2, 2, T)
        us = r(2, 2, T)
        act_e = r(2, 2, T)
        logitT = r(T)
        gateT = r(T)
        lt = r(TT, 20)
        gmx = r(TT, 1)
        gsub = r(TT, 4)
        gexp = r(TT, 4)
        gsm = r(TT, 1)
        gval = r(TT, 1)
        eqp = r(TT, 4)
        eqm = r(TT, 1)
        ohg = r(TT, 4)
        lsel = r(TT, 4)
        lprod = r(TT, 16)
        m1 = r(TT, 1)
        oh1 = r(TT, 4)
        lsel2 = r(TT, 4)
        m2 = r(TT, 1)
        oh2 = r(TT, 4)
        dm = r(TT, 1)
        ed = r(TT, 1)
        den = r(TT, 1)
        w1 = r(TT, 1)
        w2 = r(TT, 1)
        g4a = r(TT, 4)
        g4b = r(TT, 4)
        gate16 = r(TT, 16)

        r = Region(0)
        mix2 = r(DK, T)
        qh = r(HG, T)
        ff = r(HG, T)
        fb = r(HG, T)
        kf = r(HG, T)
        kb = r(HG, T)
        hgate = r(HG, T)
        v2 = r(TT, 512)
        Kc = r(HG, T)
        Qc = r(HG, T)
        Lf = r(HG, T)
        Lb = r(HG, T)
        assert r.at <= 14336, r.at
        AT = xg.rearrange("p (h s) t -> p h s t", h=HG)
        AT_flat = xg.rearrange("p k t -> p (k t)")
        aqk = memn[:, 0, 0:5, :]
        kdup = memn[:, 0, 5:7, :]
        Kc2, Qc2 = memn[:, 0, 0:4, :], memn[:, 0, 4:8, :]
        asq2 = sq[:, 0:5, :]
        aqn = sq[:, 0:5, :]
        rtmp = Kc[:, 0:2, :]

        r = Region(0)
        upad2 = r(2, 4, T + 2)
        fconv = r(2, 4, T)
        act_f = r(2, 2, T)
        yF = r(DK, T)

        s_small = sem("small_loaded")
        s_x = sem("x_loaded")
        s_mem = sem("mem_loaded")
        s_mem2 = sem("mem2_loaded")
        s_cst = sem("const_loaded")
        s_mask = sem("mask_loaded")
        s_rt = sem("router_loaded")
        landed = [sem(f"landed{i}") for i in range(SLOTS)]
        chunk_done = sem("chunk_done")
        unit_free = sem("unit_free")
        zeroed = sem("zeroed")
        xg_ready = sem("xg_ready")
        x_new = sem("x_new")
        y_ready = sem("y_ready")
        sq_ready = sem("sq_ready")
        stats_done = sem("stats_done")
        std_ready = sem("std_ready")
        rstd_ready = sem("rstd_ready")
        memn_ready = sem("memn_ready")
        agate_sig = sem("agate_sig")
        gates_sig = sem("gates_sig")
        a_glu = sem("a_glu")
        conv_a = sem("conv_a_steps")
        pads_zero = sem("pads_zero")
        pool_steps = sem("pool_steps")
        p_ready = sem("pooled_ready")
        c_ready = sem("c_ready")
        ln_mean = sem("ln_mean")
        ln_centered = sem("ln_centered")
        ln_sq = sem("ln_sq")
        ln_var = sem("ln_var")
        ln_std = sem("ln_std")
        ln_normed = sem("ln_normed")
        a_act = sem("a_act")
        pool_full = sem("pool_full")
        merged_ready = sem("merged_ready")
        scores_done = sem("scores_done")
        maxed = sem("maxed")
        neg_ready = sem("neg_ready")
        exp_done = sem("exp_done")
        rsum_ready = sem("rsum_ready")
        probs_ready = sem("probs_ready")
        turned = sem("probs_turned")
        o_done = sem("o_done")
        logits_done = sem("logits_done")
        logits_ready = sem("logits_ready")
        ltok_done = sem("ltok_done")
        route = sem("route_steps")
        route_exp = sem("route_exp")
        gate16_ready = sem("gate16_ready")
        gateT_done = sem("gateT_done")
        gateT_ready = sem("gateT_ready")
        rg_full = sem("rg_full")
        silu_done = sem("silu_done")
        act_ready = sem("act_ready")
        acc_zero = sem("acc_zero")
        lb_steps = sem("lb_steps")
        lb_exp = sem("lb_exp")
        f_raw = sem("f_raw")
        f_sig = sem("f_sig")
        hq_act = sem("hq_act")
        hg_act = sem("hg_act")
        scan_steps = sem("scan_steps")
        level_ready = sem("level_ready")
        level_done = sem("level_done")
        A_ready = sem("A_ready")
        rec_done = sem("rec_done")
        rec_sq = sem("rec_sq")
        rec_sum = sem("rec_sum")
        rec_std = sem("rec_std")
        rec_rstd = sem("rec_rstd")
        rec_row = sem("rec_row")
        rec_ready = sem("rec_ready")
        qk_sq = sem("qk_sq")
        qk_sum = sem("qk_sum")
        qk_std = sem("qk_std")
        qk_rstd = sem("qk_rstd")
        qk_row = sem("qk_row")
        qk_rot = sem("qk_rot")
        roped = sem("roped")
        dup_done = sem("dup_done")
        rcol_ready = sem("rcol_ready")
        fconv_steps = sem("fconv_steps")
        fsilu = sem("fsilu")
        fact_ready = sem("fact_ready")
        chain = sem("dve_chain")
        stored = sem("stored")

        block = ctx.enter_context(nc.Block())

        def two(ap):
            return ap.unsqueeze(1).to_broadcast([P, 2, T])

        def unit_view(u):
            return psum[:, u % UNITS, :].rearrange("p (j t) -> p j t", j=2)

        class UnitCount:

            def __init__(self):
                self.n = 0

            def take(self, n=1):
                self.n += n
                return self.n - n

        @block.sync
        def _(sp):
            def load(slot, chunk):
                sp.dma_start(ring[:, slot, :], stream[chunk]).then_inc(landed[slot], 16)

            for n in range(SLOTS):
                load(n, n)
            rounds = CHUNKS // SLOTS
            with sp.Fori(1, rounds) as i:
                for j in range(SLOTS):
                    sp.wait_ge(chunk_done, i * SLOTS + (j - SLOTS + 1))
                    load(j, i * SLOTS + j)
            for n in range(rounds * SLOTS, CHUNKS):
                sp.wait_ge(chunk_done, n - SLOTS + 1)
                load(n % SLOTS, n)
            for m in range(4):
                sp.wait_ge(x_new, 4 * 6 + m + 1)
                sp.dma_start(out_t[:, 2 * m:2 * m + 2, :], xT[:, 2 * m:2 * m + 2, :]).then_inc(stored, 16)
            sp.wait_ge(stored, 64)

        @block.tensor
        def _(pe):
            units = UnitCount()

            def matmul(out, w, x, start, stop, **kw):
                return nc.tensor.matmul(out, w, x, start=start, stop=stop, **kw)

            def wait_chunk(n):
                pe.wait_ge(landed[n % SLOTS], 16 * (n // SLOTS + 1))

            def free_bank(u):
                if u >= UNITS:
                    pe.wait_ge(unit_free, u - UNITS + 1)

            def project(n, x, kt=DK):
                u = units.take()
                wait_chunk(n)
                free_bank(u)
                w = ring[:, n % SLOTS, :]
                for j in range(2):
                    for k in range(kt):
                        last = matmul(psum[:, u % UNITS, j * T:(j + 1) * T], w[:, k * 256 + j * P:k * 256 + (j + 1) * P],
                                      x[:, k, :], k == 0, k == kt - 1)
                last.then_inc(chunk_done, 1)

            def project_rows(n, x, width=256, start=0, signal=True):
                u = units.take()
                wait_chunk(n)
                free_bank(u)
                w = ring[:, n % SLOTS, :]
                for t in range(TT):
                    for k in range(DK):
                        last = matmul(psum[:, u % UNITS, t * 256:t * 256 + width], x[:, k, t * P:(t + 1) * P],
                                      w[:, k * 256 + start:k * 256 + start + width], k == 0, k == DK - 1)
                last.then_inc(chunk_done, 1)

            def stats(k, columns=False):
                pe.wait_ge(sq_ready, 4 * (k + 1))
                if k:
                    pe.wait_ge(std_ready, k)
                for i in range(DK):
                    last = matmul(psum[:, STAT, 0:T], ones, sq[:, i, :], i == 0, i == DK - 1)
                if columns:
                    for t in range(TT):
                        for i in range(DK):
                            last = matmul(psum[:, STAT, T + t:T + t + 1], sq[:, i, t * P:(t + 1) * P],
                                          ones[:, 0:1], i == 0, i == DK - 1)
                last.then_inc(stats_done, 1)

            def attention(base, heads, group, scores, values):
                def score(h):
                    hh = base + h
                    if hh >= SB:
                        pe.wait_ge(exp_done, hh - SB + 1)
                    scores(h, 4 + hh % SB).then_inc(scores_done, 1)

                for h in range(SB):
                    score(h)
                for g in range(0, heads, group):
                    for h in range(g, g + group):
                        hh = base + h
                        u = units.take()
                        free_bank(u)
                        pe.wait_ge(probs_ready, hh + 1)
                        for m in range(TT):
                            for t in range(TT):
                                last = nc.tensor.transpose(psum[:, u % UNITS, m * T + t * P:m * T + (t + 1) * P],
                                                           probs[:, hh % 4, t, m * P:(m + 1) * P], ident)
                        last.then_inc(turned, 1)
                        if h + SB < heads:
                            score(h + SB)
                    uo = units.take()
                    free_bank(uo)
                    pe.wait_ge(unit_free, uo)
                    for h in range(g, g + group):
                        last = values(h, (base + h) % 4, uo % UNITS)
                        last.then_inc(o_done, 1)

            def cross_scores(h, bank):
                for t in range(TT):
                    for d in range(2):
                        last = matmul(psum[:, bank, t * T:(t + 1) * T], qT[:, 2 * h + d, t * P:(t + 1) * P],
                                      kT[:, 2 * h + d, :], d == 0, d == 1)
                return last

            def cross_values(h, pslot, bank):
                for d in range(2):
                    for m in range(TT):
                        last = matmul(psum[:, bank, d * T:(d + 1) * T], vm[:, m, h * 256 + d * P:h * 256 + (d + 1) * P],
                                      probsT[:, pslot, m, :], m == 0, m == 1)
                return last

            pe.wait_ge(s_cst, 16)
            stats(0)
            pe.wait_ge(xg_ready, 4)
            project(C_WIN, xg)
            stats(1)
            project(C_WIN + 1, xg)
            stats(2)
            for n in range(C_WIN + 2, C_WIN + 14):
                project(n, xg)
            pe.wait_ge(conv_a, 4 * CONV_K)
            for c in range(4):
                last = matmul(psum[:, 6, 0:T], ones, aacc[:, c, :], c == 0, c == 3)
            last.then_inc(ln_mean, 1)
            for n in range(C_WIN + 14, C_WIN + 17):
                project(n, xg)
            pe.wait_ge(ln_sq, 2)
            for c in range(4):
                last = matmul(psum[:, 5, 0:T], ones, asq[:, c, :], c == 0, c == 3)
            last.then_inc(ln_var, 1)
            for n in range(C_WIN + 17, C_WIN + 24):
                project(n, xg)

            wait_chunk(C_POOL)
            pe.wait_ge(p_ready, 1)
            for m in range(4):
                u = units.take()
                free_bank(u)
                for j in range(2):
                    last = matmul(psum[:, u % UNITS, j * T:(j + 1) * T],
                                  ring[:, C_POOL % SLOTS, m * 256 + j * P:m * 256 + (j + 1) * P], pT[:, m, :], True, True)
                if m == 3:
                    last.then_inc(chunk_done, 1)
                else:
                    last.then_inc(pool_full, 1)
            pe.wait_ge(a_act, 4)
            pe.wait_ge(c_ready, 1)
            for m in range(4):
                n = C_MERGE + m
                wait_chunk(n)
                w = ring[:, n % SLOTS, :]
                for at, x in ((0, actT), (1024, cy)):
                    u = units.take()
                    free_bank(u)
                    for j in range(2):
                        for k in range(4):
                            last = matmul(psum[:, u % UNITS, j * T:(j + 1) * T],
                                          w[:, at + k * 256 + j * P:at + k * 256 + (j + 1) * P], x[:, k, :], k == 0, k == 3)
                last.then_inc(chunk_done, 1)
            pe.wait_ge(memn_ready, 1)
            for m in range(4):
                project(C_K1 + m, memn[:, 0])
            pe.wait_ge(merged_ready, 4)
            for m in range(4):
                project(C_WO + m, merged)
            for m in range(4):
                project_rows(C_V1 + m, memn[:, 0])
            stats(3)
            pe.wait_ge(xg_ready, 8)
            for m in range(4):
                project(C_Q1 + m, xg)
            pe.wait_ge(unit_free, units.n)
            attention(0, 4, 1, cross_scores, cross_values)
            pe.wait_ge(unit_free, units.n)
            for m in range(4):
                project(C_XO1 + m, oT)
            stats(4)
            pe.wait_ge(xg_ready, 12)
            pe.wait_ge(s_rt, 16)
            for k in range(DK):
                last = matmul(psum[0:20, 6, 0:T], router[:, k, :], xg[:, k, :], k == 0, k == DK - 1)
            last.then_inc(logits_done, 1)
            project(C_MOE, xg)
            project(C_MOE + 1, xg)
            pe.wait_ge(logits_ready, 1)
            for t in range(TT):
                last = nc.tensor.transpose(psum[:, 5, t * 20:(t + 1) * 20], logitT[0:20, t * P:(t + 1) * P],
                                           ident[0:20, 0:20])
            last.then_inc(ltok_done, 1)
            pe.wait_ge(gate16_ready, 1)
            for t in range(TT):
                last = nc.tensor.transpose(psum[0:16, 6, t * P:(t + 1) * P], gate16[:, t, :], ident)
            last.then_inc(gateT_done, 1)
            pe.wait_ge(gateT_ready, 1)
            for e in range(0, EXPERTS, 2):
                u = units.take()
                free_bank(u)
                for j in range(2):
                    last = matmul(psum[:, u % UNITS, j * T:(j + 1) * T],
                                  ident[0:16, e + j:e + j + 1].to_broadcast([16, P]), gateT[0:16, :], True, True)
                last.then_inc(rg_full, 1)

            def clear_sums(k):
                pe.wait_ge(zeroed, 2)
                pe.wait_ge(std_ready, k)
                for b in range(4):
                    matmul(psum[:, ACC + b, :], zeros[:], const[:, 0:512], True, True)

            def project_at(slot, landed_value, u_bank, free_value, x, done_sem=chunk_done):
                pe.wait_ge(landed[slot], landed_value)
                pe.wait_ge(unit_free, free_value)
                w = ring[:, slot, :]
                for j in range(2):
                    for k in range(DK):
                        last = matmul(psum[:, u_bank, j * T:(j + 1) * T],
                                      w[:, k * 256 + j * P:k * 256 + (j + 1) * P], x[:, k, :], k == 0, k == DK - 1)
                last.then_inc(chunk_done, 1)

            def down_at(slot, landed_value, act, ready, ready_value):
                pe.wait_ge(landed[slot], landed_value)
                pe.wait_ge(ready, ready_value)
                w = ring[:, slot, :]
                for o in range(DK):
                    for k in range(2):
                        last = matmul(psum[:, ACC + o // 2, (o % 2) * T:(o % 2 + 1) * T],
                                      w[:, k * D + o * P:k * D + (o + 1) * P], act[:, k, :], False, k == 1,
                                      skip_group_check=True)
                last.then_inc(chunk_done, 1)

            def steps(first_chunk, count, act, ready):
                u0 = units.n
                c0 = first_chunk + 2

                def step(t, shift):
                    for j in range(2):
                        n, u = c0 + 3 * t + j, u0 + 2 * t + j
                        project_at(n % SLOTS, shift * 16 + 16 * (n // SLOTS + 1), u % UNITS,
                                   shift * UNITS + (u - UNITS + 1), xg)
                    n = c0 + 3 * t + 2
                    down_at(n % SLOTS, shift * 16 + 16 * (n // SLOTS + 1), act[:, t % 2], ready, shift * 2 + (t + 1))

                passes = (count - 1) // 2
                with pe.Fori(0, passes) as i:
                    step(0, i)
                    step(1, i)
                for t in range(2 * passes, count - 1):
                    step(t, 0)
                units.take(2 * (count - 1))
                n = first_chunk + 3 * count - 1
                down_at(n % SLOTS, 16 * (n // SLOTS + 1), act[:, (count - 1) % 2], ready, count)

            clear_sums(5)
            steps(C_MOE, EXPERTS, act_e, act_ready)

            pe.wait_ge(memn_ready, 2)
            project(C_K2, memn[:, 1])
            project(C_K2 + 1, memn[:, 1])
            pe.wait_ge(x_new, 12)
            stats(5)
            project(C_K2 + 2, memn[:, 1])
            project(C_K2 + 3, memn[:, 1])
            stats(6, columns=True)
            pe.wait_ge(xg_ready, 16)
            for i, u in enumerate(WIN2_ORDER):
                n = C_WIN2 + i
                if u in (9, 10):
                    project_rows(n, xg)
                elif u == 2:
                    uu = units.take()
                    wait_chunk(n)
                    free_bank(uu)
                    w = ring[:, n % SLOTS, :]
                    for k in range(DK):
                        matmul(psum[:, uu % UNITS, 0:T], w[:, k * 256:k * 256 + P], xg[:, k, :], k == 0, k == DK - 1)
                    for t in range(TT):
                        for k in range(DK):
                            last = matmul(psum[:, uu % UNITS, T + t * P:T + (t + 1) * P], xg[:, k, t * P:(t + 1) * P],
                                          w[:, k * 256 + P:k * 256 + 2 * P], k == 0, k == DK - 1)
                    last.then_inc(chunk_done, 1)
                else:
                    project(n, xg)

            def level(i):
                pe.wait_ge(level_ready, i + 1)
                for hp in range(2):
                    u = units.take()
                    free_bank(u)
                    for h in range(2):
                        for c in range(2):
                            hd = 2 * hp + h
                            s0 = c * P
                            t0 = (1 - c) * P if i == 8 else c * P
                            kk, qq = (Kc, qh) if i == 0 else ((Kc, Qc), (Kc2, Qc2))[i % 2]
                            last = matmul(psum[:, u % UNITS, (2 * h + c) * P:(2 * h + c + 1) * P],
                                          kk[:, hd, s0:s0 + P], qq[:, hd, t0:t0 + P], True, True)
                    last.then_inc(level_done, 1)

            pe.wait_ge(qk_sq, 5)
            pe.wait_ge(std_ready, 7)
            for j in range(5):
                last = matmul(psum[0:10, 4, 0:T], cn("qk_sum", 10 * j, 10), asq2[:, j, :], j == 0, j == 4)
            last.then_inc(qk_sum, 1)
            pe.wait_ge(qk_rstd, 1)
            for j0 in (0, 2, 4):
                u = units.take()
                free_bank(u)
                for j in range(j0, min(j0 + 2, 5)):
                    last = matmul(psum[:, u % UNITS, (j - j0) * T:(j - j0 + 1) * T],
                                  cn("qk_row", 128 * j, 128, 10), cden[0:10, 1, :], True, True)
                last.then_inc(qk_row, 1)
            for j0 in (0, 2, 4):
                u = units.take()
                free_bank(u)
                pe.wait_ge(unit_free, u - 2)
                for j in range(j0, min(j0 + 2, 5)):
                    last = matmul(psum[:, u % UNITS, (j - j0) * T:(j - j0 + 1) * T], cn("rot"), aqn[:, j, :],
                                  True, True)
                last.then_inc(qk_rot, 1)
            u = units.take()
            free_bank(u)
            pe.wait_ge(roped, 3)
            for j in range(2):
                last = matmul(psum[:, u % UNITS, j * T:(j + 1) * T], cn("dup", 128 * j), aqk[:, 4, :], True, True)
            last.then_inc(dup_done, 1)

            def gqa_scores(h, bank):
                b = 64 * (h % 2)
                for t in range(TT):
                    last = matmul(psum[:, bank, t * T:(t + 1) * T], aqk[b:b + 64, h // 2, t * P:(t + 1) * P],
                                  kdup[b:b + 64, h // 4, :], True, True)
                return last

            def gqa_values(h, pslot, bank):
                b = 64 * (h % 2)
                for m in range(TT):
                    last = matmul(psum[b:b + 64, bank, 0:T], av2[:, m, 64 * (h // 4):64 * (h // 4 + 1)],
                                  probsT[:, pslot, m, :], m == 0, m == 1)
                return last

            pe.wait_ge(unit_free, units.n)
            attention(4, QH, 2, gqa_scores, gqa_values)
            for i in range(9):
                level(i)
                if i % 2:
                    project_rows(C_V2 + i // 2, memn[:, 1])

            assert units.n == U_REC, units.n
            for hp in range(2):
                u = units.take()
                free_bank(u)
                pe.wait_ge(A_ready, 1)
                for h in range(2):
                    for m in range(TT):
                        last = matmul(psum[:, u % UNITS, h * T:(h + 1) * T],
                                      v2[:, m, (2 * hp + h) * P:(2 * hp + h + 1) * P], AT[:, 2 * hp + h, m, :],
                                      m == 0, m == 1)
                last.then_inc(rec_done, 1)
            pe.wait_ge(rec_sq, 2)
            for h in range(HG):
                last = matmul(psum[0:4, 4, 0:T], cn("hg_sum", 4 * h, 4), sq[:, h, :], h == 0, h == 3)
            last.then_inc(rec_sum, 1)
            pe.wait_ge(rec_rstd, 1)
            for hp in range(2):
                u = units.take()
                free_bank(u)
                for h in range(2):
                    last = matmul(psum[:, u % UNITS, h * T:(h + 1) * T],
                                  cn("hg_row", 128 * (2 * hp + h), 128, 4), cden[0:4, 1, :], True, True)
                last.then_inc(rec_row, 1)
            pe.wait_ge(rec_ready, 2)
            assert units.n == U_WO2, units.n
            for m in range(4):
                project(C_WO2 + m, mix2)
            stats(7)
            stats(8)
            pe.wait_ge(xg_ready, 20)
            for m in range(4):
                project(C_Q2 + m, xg)
            pe.wait_ge(unit_free, units.n)
            attention(12, 4, 1, cross_scores, cross_values)
            pe.wait_ge(unit_free, units.n)
            for m in range(4):
                project(C_XO2 + m, oT)
            stats(9)
            stats(10)
            pe.wait_ge(xg_ready, 24)
            project(C_FFN, xg)
            project(C_FFN + 1, xg)
            clear_sums(11)
            steps(C_FFN, FSTEPS, act_f, fact_ready)
            stats(11)

        @block.scalar
        def _(act):
            def fn(out, in_, f, **kw):
                return nc.scalar.activation(out, in_, f, **kw)

            act.dma_start(xT[:], xt_in).then_inc(s_x, 16)
            act.dma_start(small[:], small_in).then_inc(s_small, 16)
            act.dma_start(const[:], const_in).then_inc(s_cst, 16)
            act.dma_start(memn[:, 0], memt_in).then_inc(s_mem, 16)
            act.dma_start(memn[:, 1], mem2t_in).then_inc(s_mem2, 16)
            act.dma_start(router[:], router_in).then_inc(s_rt, 16)
            act.dma_start(mask[:], mask_in).then_inc(s_mask, 16)

            def squares(k, src, ready=None, base=0):
                if k:
                    act.wait_ge(stats_done, k)
                for m in range(4):
                    if ready is not None:
                        act.wait_ge(ready, base + m + 1)
                    fn(sq[:, 2 * m:2 * m + 2, :], src[:, 2 * m:2 * m + 2, :], ACT.Square).then_inc(sq_ready, 1)

            def root(k, columns=False):
                act.wait_ge(stats_done, k + 1)
                if k:
                    act.wait_ge(rstd_ready, k)
                if columns:
                    fn(cols[:, 0, :], psum[:, STAT, T:T + TT], ACT.Sqrt, scale=1.0 / D, bias=eps[:])
                fn(std[:], psum[:, STAT, 0:T], ACT.Sqrt, scale=1.0 / D, bias=eps[:]).then_inc(std_ready, 1)

            act.wait_ge(s_x, 16)
            act.wait_ge(zeroed, 1)
            squares(0, xT)
            root(0)
            act.wait_ge(s_mem, 16)
            squares(1, memn[:, 0])
            root(1)
            act.wait_ge(s_mem2, 16)
            squares(2, memn[:, 1])
            root(2)
            for m in range(2):
                act.wait_ge(unit_free, 2 + m + 1)
                fn(agate[:, 2 * m:2 * m + 2, :], agate[:, 2 * m:2 * m + 2, :], ACT.Sigmoid).then_inc(agate_sig, 1)

            def gate_sigmoid(m):
                act.wait_ge(unit_free, 12 + m + 1)
                fn(gates[:, 2 * m:2 * m + 2, :], gates[:, 2 * m:2 * m + 2, :], ACT.Sigmoid).then_inc(gates_sig, 1)

            gate_sigmoid(0)
            gate_sigmoid(1)
            for m in range(2):
                act.wait_ge(ln_centered, m + 1)
                fn(asq[:, 2 * m:2 * m + 2, :], aacc[:, 2 * m:2 * m + 2, :], ACT.Square).then_inc(ln_sq, 1)
            for m in range(2, 5):
                gate_sigmoid(m)
            act.wait_ge(ln_var, 1)
            fn(lnstd, psum[:, 5, 0:T], ACT.Sqrt, scale=1.0 / 512, bias=eps[:]).then_inc(ln_std, 1)
            act.wait_ge(ln_normed, 2)
            for c in range(4):
                fn(actT[:, c, :], aacc[:, c, :], ACT.Silu, scale=sm("ln_g", c), bias=sm("ln_b", c)).then_inc(a_act, 1)
            for m in range(5, 12):
                gate_sigmoid(m)

            def exps(base, heads, scale):
                for h in range(heads):
                    hh = base + h
                    act.wait_ge(neg_ready, hh + 1)
                    if hh >= 4:
                        act.wait_ge(turned, hh - 3)
                    for t in range(TT):
                        last = fn(probs[:, hh % 4, t, :], psum[:, 4 + hh % SB, t * T:(t + 1) * T], ACT.Exp,
                                  scale=scale, bias=negm[:, hh, t:t + 1], accum_out=ssum[:, hh, t:t + 1])
                    last.then_inc(exp_done, 1)

            squares(3, xT, x_new, 0)
            root(3)
            exps(0, 4, 1.0 / 16)
            squares(4, xT, x_new, 4)
            root(4)
            act.wait_ge(route, 2)
            fn(gexp[:], gsub[:], ACT.Exp).then_inc(route_exp, 1)
            act.wait_ge(route, 17)
            fn(ed[:], dm[:], ACT.Exp).then_inc(route_exp, 1)

            u0 = U_MOE

            def expert_silu(parity, value):
                act.wait_ge(unit_free, value)
                fn(gs[:, parity], gs[:, parity], ACT.Silu).then_inc(silu_done, 1)

            expert_silu(0, U_MOE_FIRST + 1)
            with act.Fori(0, 7) as i:
                for s in range(2):
                    expert_silu((1 + s) % 2, i * 4 + (u0 + 2 * s + 1))
            expert_silu(1, u0 + 2 * 14 + 1)

            squares(5, xT, x_new, 8)
            root(5)
            act.wait_ge(lb_steps, 3)
            fn(lbt[:, 3:5, :], lbt[:, 1:3, :], ACT.Exp).then_inc(lb_exp, 1)
            squares(6, xT, x_new, 12)
            root(6, columns=True)
            for m in range(2):
                act.wait_ge(unit_free, U_WIN2 + m + 1)
                fn(qh[:, 2 * m:2 * m + 2, :], qh[:, 2 * m:2 * m + 2, :], ACT.Silu).then_inc(hq_act, 1)
            for m in range(4):
                act.wait_ge(unit_free, U_WIN2 + 2 + m + 1)
                f, k = ((ff, kf), (fb, kb))[m // 2]
                h = slice(2 * (m % 2), 2 * (m % 2) + 2)
                fn(k[:, h, :], f[:, h, :], ACT.Sigmoid, scale=-1.0)
                fn(f[:, h, :], f[:, h, :], ACT.Sigmoid).then_inc(f_sig, 1)
            for m in range(2):
                act.wait_ge(unit_free, U_WIN2 + 8 + m + 1)
                fn(hgate[:, 2 * m:2 * m + 2, :], hgate[:, 2 * m:2 * m + 2, :], ACT.Silu).then_inc(hg_act, 1)
            act.wait_ge(stats_done, 7)
            for j in range(5):
                act.wait_ge(unit_free, U_WIN2 + 10 + j // 2 + 1)
                fn(asq2[:, j, :], aqk[:, j, :], ACT.Square).then_inc(qk_sq, 1)
            act.wait_ge(qk_sum, 1)
            fn(cden[0:10, 0, :], psum[0:10, 4, 0:T], ACT.Sqrt, scale=1.0 / 64, bias=eps[0:10, :]).then_inc(qk_std, 1)
            exps(4, QH, 1.0 / 8)
            for hp in range(2):
                act.wait_ge(unit_free, U_REC + hp + 1)
                fn(sq[:, 2 * hp:2 * hp + 2, :], mix2[:, 4 + 2 * hp:6 + 2 * hp, :], ACT.Square).then_inc(rec_sq, 1)
            act.wait_ge(rec_sum, 1)
            fn(cden[0:4, 0, :], psum[0:4, 4, 0:T], ACT.Sqrt, scale=1.0 / 128, bias=eps[0:4, :]).then_inc(rec_std, 1)
            squares(7, yT, unit_free, U_WO2)
            root(7)
            squares(8, xT, x_new, 16)
            root(8)
            exps(12, 4, 1.0 / 16)
            squares(9, yT, unit_free, U_XO2)
            root(9)
            squares(10, xT, x_new, 20)
            root(10)

            def ffn_silu(parity, value):
                act.wait_ge(fconv_steps, value)
                fn(fconv[:, parity, 0:2, :], fconv[:, parity, 0:2, :], ACT.Silu).then_inc(fsilu, 1)

            ffn_silu(0, 6)
            with act.Fori(0, 5) as i:
                for s in range(2):
                    ffn_silu((1 + s) % 2, i * 24 + (12 * (1 + s) + 6))
            squares(11, yF, y_ready, 0)
            root(11)

        @block.gpsimd
        def _(pool):
            nc.gpsimd.memset(apad[:, :, 0:CONV_K - 1], 0.0)
            nc.gpsimd.memset(upad[:, :, 0:PADW], 0.0)
            nc.gpsimd.memset(cpad[:, :, 0:C_K - 1], 0.0).then_inc(pads_zero, 1)
            pool.wait_ge(pads_zero, 1)
            n = [0]

            def step(ins):
                ins.then_inc(pool_steps, 1)
                n[0] += 1
                pool.wait_ge(pool_steps, n[0])

            add = lambda o, a, b: nc.gpsimd.tensor_tensor(o, a, b, ALU.add)
            pool.wait_ge(unit_free, 6)
            W = T + PADW
            step(add(ubuf[:, :, 1:W], upad[:, :, 1:W], upad[:, :, 0:W - 1]))
            pool.wait_ge(stats_done, 3)
            buf = sq.rearrange("p k t -> p (k t)")[:, 0:4 * W].rearrange("p (a b) -> p a b", a=4)
            step(add(buf[:, 1:4, 4:W], ubuf[:, 1:4, 4:W], ubuf[:, 1:4, 2:W - 2]))
            step(add(ubuf[:, 2:4, 8:W], buf[:, 2:4, 8:W], buf[:, 2:4, 4:W - 4]))
            step(add(buf[:, 3:4, 16:W], ubuf[:, 3:4, 16:W], ubuf[:, 3:4, 8:W - 8]))
            pool.wait_ge(s_cst, 16)
            for i, src in enumerate((ubuf, buf, ubuf, buf)):
                step(nc.gpsimd.tensor_tensor(pT[:, i, :], src[:, i, PADW:W], cn("rcnt", T * i, T), ALU.mult))
            nc.gpsimd.tensor_tensor(pT[:], pT[:], upad[:, :, PADW:W], ALU.subtract).then_inc(p_ready, 1)
            pool.wait_ge(unit_free, 12)
            pool.wait_ge(s_small, 16)
            step(nc.gpsimd.tensor_tensor(cpad[:, :, C_K - 1:C_K - 1 + T], cc[:], cx[:], ALU.mult))
            for j in range(C_K):
                for c in range(4):
                    dst = cy if j == 0 else ctmp
                    last = nc.gpsimd.tensor_scalar(dst[:, c, :], cpad[:, c, j:j + T], sm("c_w", 4 * j + c), None, ALU.mult)
                step(last)
                if j:
                    step(nc.gpsimd.tensor_tensor(cy[:], cy[:], ctmp[:], ALU.add))
            nc.gpsimd.tensor_tensor(cy[:], cy[:], cb[:], ALU.mult).then_inc(c_ready, 1)

        @block.vector
        def _(dve):
            units = UnitCount()
            v = nc.vector
            upd = [0]
            links = [0]

            def link(ins):
                ins.then_inc(chain, 1)
                links[0] += 1
                dve.wait_ge(chain, links[0])

            def tt(out, a, b, op):
                return v.tensor_tensor(out, a, b, op)

            def full(n):
                dve.wait_ge(chunk_done, n + 1)

            def evac_scaled(n, out, k):
                full(n)
                u = units.take()
                tt(out, unit_view(u), two(rstd[:, k % 4, :]), ALU.mult).then_inc(unit_free, 1)
                return u

            def recip(k):
                dve.wait_ge(std_ready, k + 1)
                v.reciprocal(rstd[:, k % 4, :], std[:]).then_inc(rstd_ready, 1)

            def gain(name, m, also=None):
                first, second = (v.tensor_scalar(xg[:, k, :], xT[:, k, :], sm(name, k), None, ALU.mult)
                                 for k in (2 * m, 2 * m + 1))
                if also is not None:
                    first.then_inc(also, 1)
                second.then_inc(xg_ready, 1)

            def residual(chunk, name):
                for m in range(4):
                    full(chunk + m)
                    u = units.take()
                    upd[0] += 1
                    q = xT[:, 2 * m:2 * m + 2, :]
                    tt(q, unit_view(u), q, ALU.add).then_inc(x_new, 1)
                    dve.wait_ge(x_new, upd[0])
                    gain(name, m, unit_free)

            v.memset(eps[:], EPS).then_inc(zeroed, 1)
            v.memset(zeros[:], 0.0).then_inc(zeroed, 1)
            dve.wait_ge(s_x, 16)
            dve.wait_ge(s_small, 16)
            for m in range(4):
                gain("mix_g", m)
            recip(0)
            dve.wait_ge(rstd_ready, 1)
            dve.wait_ge(pads_zero, 1)
            for m in range(2):
                evac_scaled(C_WIN + m, aval[:, 2 * m:2 * m + 2, :], 0)
            recip(1)
            recip(2)

            def normalise_memory(i, name):
                dve.wait_ge(rstd_ready, 2 + i)
                dve.wait_ge(stats_done, 2 + i)
                for k in range(DK):
                    last = v.scalar_tensor_tensor(memn[:, i, k, :], memn[:, i, k, :], sm(name, k),
                                                  rstd[:, 1 + i, :], ALU.mult, ALU.mult)
                last.then_inc(memn_ready, 1)

            for m in range(2):
                evac_scaled(C_WIN + 2 + m, agate[:, 2 * m:2 * m + 2, :], 0)
            for m in range(2):
                dve.wait_ge(agate_sig, m + 1)
                h = slice(2 * m, 2 * m + 2)
                tt(apad[:, h, CONV_K - 1:], aval[:, h, :], agate[:, h, :], ALU.mult).then_inc(a_glu, 1)
            dve.wait_ge(a_glu, 2)
            done = [0]

            def convolve(taps):
                for j in taps:
                    for c in range(4):
                        x = apad[:, c, j:j + T]
                        if j == 0:
                            ins = v.tensor_scalar(aacc[:, c, :], x, sm("conv_w", c), sm("conv_b", c), ALU.mult, ALU.add)
                        else:
                            dve.wait_ge(conv_a, done[0] - 3)
                            ins = v.scalar_tensor_tensor(aacc[:, c, :], x, sm("conv_w", 4 * j + c), aacc[:, c, :],
                                                         ALU.mult, ALU.add)
                        ins.then_inc(conv_a, 1)
                        done[0] += 1

            dst = {4: upad[:, 0:2, PADW:], 5: upad[:, 2:4, PADW:], 6: cx[:, 0:2, :], 7: cx[:, 2:4, :],
                   8: cb[:, 0:2, :], 9: cb[:, 2:4, :], 10: cc[:, 0:2, :], 11: cc[:, 2:4, :]}
            for n in range(4, 12):
                evac_scaled(C_WIN + n, dst[n], 0)
                convolve(range(5 * (n - 4), min(5 * (n - 3), CONV_K)))
            for m in range(2):
                evac_scaled(C_WIN + 12 + m, gates[:, 2 * m:2 * m + 2, :], 0)
            dve.wait_ge(ln_mean, 1)
            for m in range(2):
                h = slice(2 * m, 2 * m + 2)
                v.scalar_tensor_tensor(aacc[:, h, :], two(psum[:, 6, 0:T]), -1.0 / 512, aacc[:, h, :],
                                       ALU.mult, ALU.add).then_inc(ln_centered, 1)
            normalise_memory(0, "mem_g")
            for m in range(2, 5):
                evac_scaled(C_WIN + 12 + m, gates[:, 2 * m:2 * m + 2, :], 0)
            dve.wait_ge(ln_std, 1)
            link(v.reciprocal(lnrstd, lnstd))
            for m in range(2):
                h = slice(2 * m, 2 * m + 2)
                tt(aacc[:, h, :], aacc[:, h, :], two(lnrstd), ALU.mult).then_inc(ln_normed, 1)
            normalise_memory(1, "mem2_g")
            for m in range(5, 12):
                evac_scaled(C_WIN + 12 + m, gates[:, 2 * m:2 * m + 2, :], 0)
            dve.wait_ge(gates_sig, 12)
            for m in range(4):
                if m < 3:
                    dve.wait_ge(pool_full, m + 1)
                else:
                    full(C_POOL)
                u = units.take()
                for j in range(2):
                    last = v.scalar_tensor_tensor(merged[:, 2 * m + j, :], psum[:, u % UNITS, j * T:(j + 1) * T],
                                                  sm("pool_s", 2 * m + j), gates[:, 8 + 2 * m + j, :],
                                                  ALU.mult, ALU.mult)
                last.then_inc(unit_free, 1)
            for m in range(4):
                full(C_MERGE + m)
                ua, uc = units.take(), units.take()
                q = slice(2 * m, 2 * m + 2)
                b = slice(2 * (m % 2), 2 * (m % 2) + 2)
                tt(mt1[:, b, :], unit_view(ua), gates[:, 2 * m:2 * m + 2, :], ALU.mult).then_inc(unit_free, 1)
                tt(mt2[:, b, :], unit_view(uc), gates[:, 16 + 2 * m:18 + 2 * m, :], ALU.mult).then_inc(unit_free, 1)
                dve.wait_ge(unit_free, uc + 1)
                link(tt(mt1[:, b, :], mt1[:, b, :], mt2[:, b, :], ALU.add))
                tt(merged[:, q, :], mt1[:, b, :], merged[:, q, :], ALU.add).then_inc(merged_ready, 1)

            def copy_units(chunk, dst_of):
                for m in range(4):
                    full(chunk + m)
                    u = units.take()
                    v.tensor_copy(dst_of(m), unit_view(u)).then_inc(unit_free, 1)

            k_dst = lambda m: kT[:, 2 * m:2 * m + 2, :]
            v_dst = lambda m: vm[:, :, 256 * m:256 * (m + 1)]
            copy_units(C_K1, k_dst)
            residual(C_WO, "x_g")
            copy_units(C_V1, v_dst)
            recip(3)
            dve.wait_ge(rstd_ready, 4)
            for m in range(4):
                evac_scaled(C_Q1 + m, qT[:, 2 * m:2 * m + 2, :], 3)

            def attention(base, heads, group, scale, take_out):
                def row_max(h):
                    hh = base + h
                    dve.wait_ge(scores_done, hh + 1)
                    s = psum[:, 4 + hh % SB, :].rearrange("p (t m) -> p t m", t=TT)
                    v.tensor_reduce(nmax[:, hh, :], s, AX_X, ALU.max).then_inc(maxed, 1)
                    dve.wait_ge(maxed, hh + 1)
                    v.tensor_scalar(negm[:, hh, :], nmax[:, hh, :], -scale, None, ALU.mult).then_inc(neg_ready, 1)

                def normalise(h):
                    hh = base + h
                    dve.wait_ge(exp_done, hh + 1)
                    v.reciprocal(rsum[:, hh, :], ssum[:, hh, :]).then_inc(rsum_ready, 1)
                    dve.wait_ge(rsum_ready, hh + 1)
                    for t in range(TT):
                        last = v.tensor_scalar(probs[:, hh % 4, t, :], probs[:, hh % 4, t, :], rsum[:, hh, t:t + 1],
                                               None, ALU.mult)
                    last.then_inc(probs_ready, 1)

                for h in range(SB):
                    row_max(h)
                normalise(0)
                for g in range(0, heads, group):
                    for h in range(g, g + group):
                        hh = base + h
                        dve.wait_ge(turned, hh + 1)
                        if hh >= 4:
                            dve.wait_ge(o_done, hh - 3)
                        u = units.take()
                        v.tensor_copy(probsT[:, hh % 4], unit_view(u)).then_inc(unit_free, 1)
                        if h + SB < heads:
                            row_max(h + SB)
                        if h + 1 < heads:
                            normalise(h + 1)
                    dve.wait_ge(o_done, base + g + group)
                    u = units.take()
                    take_out(g, u).then_inc(unit_free, 1)

            def cross_out(h, u):
                return v.tensor_copy(oT[:, 2 * h:2 * h + 2, :], unit_view(u))

            attention(0, 4, 1, 1.0 / 16, cross_out)
            residual(C_XO1, "ffn_g")
            recip(4)
            dve.wait_ge(rstd_ready, 5)
            dve.wait_ge(logits_done, 1)
            tt(logitT[0:20, :], psum[0:20, 6, 0:T], rstd[0:20, 0, :], ALU.mult).then_inc(route, 1)
            dve.wait_ge(route, 1)
            v.tensor_scalar(logitT[0:20, :], logitT[0:20, :], sm("r_b")[0:20, :], None, ALU.add).then_inc(logits_ready, 1)
            full(C_MOE)
            ug = units.take()
            assert ug == U_MOE_FIRST, (ug, U_MOE_FIRST)
            tt(gs[:, 0], unit_view(ug), two(rstd[:, 0, :]), ALU.mult).then_inc(unit_free, 1)
            full(C_MOE + 1)
            uu = units.take()
            tt(us[:, 0], unit_view(uu), two(rstd[:, 0, :]), ALU.mult).then_inc(unit_free, 1)

            rn = [1]

            def step(ins):
                ins.then_inc(route, 1)
                rn[0] += 1
                dve.wait_ge(route, rn[0])

            b4 = lambda ap: ap.to_broadcast([P, TT, 4])
            prio = cn("prio", 0, 8).rearrange("p (a b) -> p a b", a=TT)
            dve.wait_ge(ltok_done, 1)
            link(v.tensor_copy(lt[:], psum[:, 5, 0:40].rearrange("p (t n) -> p t n", t=TT)))
            link(v.tensor_reduce(gmx[:], lt[:, :, 0:4], AX_X, ALU.max))
            step(tt(gsub[:], lt[:, :, 0:4], b4(gmx[:]), ALU.subtract))
            step(tt(eqp[:], lt[:, :, 0:4], b4(gmx[:]), ALU.is_equal))
            step(tt(eqp[:], eqp[:], prio, ALU.mult))
            step(v.tensor_reduce(eqm[:], eqp[:], AX_X, ALU.max))
            step(tt(ohg[:], eqp[:], b4(eqm[:]), ALU.is_equal))
            for t in range(TT):
                last = tt(lprod[:, t, :].rearrange("p (g e) -> p g e", g=4),
                          lt[:, t, 4:20].rearrange("p (g e) -> p g e", g=4),
                          ohg[:, t, :].unsqueeze(2).to_broadcast([P, 4, 4]), ALU.mult)
            step(last)
            for t in range(TT):
                last = v.tensor_reduce(lsel[:, t, :], lprod[:, t, :].rearrange("p (g e) -> p e g", g=4), AX_X, ALU.add)
            step(last)
            step(v.tensor_reduce(m1[:], lsel[:], AX_X, ALU.max))
            step(tt(eqp[:], lsel[:], b4(m1[:]), ALU.is_equal))
            step(tt(eqp[:], eqp[:], prio, ALU.mult))
            step(v.tensor_reduce(eqm[:], eqp[:], AX_X, ALU.max))
            step(tt(oh1[:], eqp[:], b4(eqm[:]), ALU.is_equal))
            step(v.tensor_scalar(lsel2[:], oh1[:], NEG, None, ALU.mult))
            step(tt(lsel2[:], lsel2[:], lsel[:], ALU.add))
            step(v.tensor_reduce(m2[:], lsel2[:], AX_X, ALU.max))
            step(tt(dm[:], m2[:], m1[:], ALU.subtract))
            step(tt(eqp[:], lsel2[:], b4(m2[:]), ALU.is_equal))
            step(tt(eqp[:], eqp[:], prio, ALU.mult))
            step(v.tensor_reduce(eqm[:], eqp[:], AX_X, ALU.max))
            step(tt(oh2[:], eqp[:], b4(eqm[:]), ALU.is_equal))
            dve.wait_ge(route_exp, 1)
            step(v.tensor_reduce(gsm[:], gexp[:], AX_X, ALU.add))
            step(v.reciprocal(gval[:], gsm[:]))
            dve.wait_ge(route_exp, 2)
            step(v.tensor_scalar(den[:], ed[:], 1.0, None, ALU.add))
            step(v.reciprocal(den[:], den[:]))
            step(tt(w1[:], gval[:], den[:], ALU.mult))
            step(tt(w2[:], w1[:], ed[:], ALU.mult))
            step(tt(g4a[:], oh1[:], b4(w1[:]), ALU.mult))
            step(tt(g4b[:], oh2[:], b4(w2[:]), ALU.mult))
            step(tt(g4a[:], g4a[:], g4b[:], ALU.add))
            for t in range(TT):
                last = tt(gate16[:, t, :].rearrange("p (g e) -> p g e", g=4),
                          ohg[:, t, :].unsqueeze(2).to_broadcast([P, 4, 4]),
                          g4a[:, t, :].unsqueeze(1).to_broadcast([P, 4, 4]), ALU.mult)
            last.then_inc(gate16_ready, 1)
            dve.wait_ge(gateT_done, 1)
            v.tensor_copy(gateT[0:16, :], psum[0:16, 6, 0:T]).then_inc(gateT_ready, 1)
            for e in range(0, EXPERTS, 2):
                dve.wait_ge(rg_full, e // 2 + 1)
                u = units.take()
                if e == 0:
                    link(tt(us[:, 0], us[:, 0], two(psum[:, u % UNITS, 0:T]), ALU.mult))
                tt(rg[:, e:e + 2, :], unit_view(u), two(rstd[:, 0, :]), ALU.mult).then_inc(unit_free, 1)
            dve.wait_ge(silu_done, 1)
            dve.wait_ge(unit_free, units.n)
            tt(act_e[:, 0], gs[:, 0], us[:, 0], ALU.mult).then_inc(act_ready, 1)

            assert units.n == U_MOE, (units.n, U_MOE)

            def expert(e, i):
                c = C_MOE + 2 + 3 * (e - 1)
                u = U_MOE + 2 * (e - 1)
                b = e % 2
                dve.wait_ge(chunk_done, i * 6 + (c + 1))
                tt(gs[:, b], unit_view(u), two(rstd[:, 0, :]), ALU.mult).then_inc(unit_free, 1)
                dve.wait_ge(chunk_done, i * 6 + (c + 2))
                weight = rg[:, e, :] if isinstance(i, int) else work[:, bass.ds(i * (2 * T) + e * T, T)]
                tt(us[:, b], unit_view(u + 1), two(weight), ALU.mult).then_inc(unit_free, 1)
                dve.wait_ge(unit_free, i * 4 + (u + 2))
                dve.wait_ge(silu_done, i * 2 + (e + 1))
                tt(act_e[:, b], gs[:, b], us[:, b], ALU.mult).then_inc(act_ready, 1)

            with dve.Fori(0, 7) as i:
                expert(1, i)
                expert(2, i)
            expert(15, 0)
            units.take(30)
            dve.wait_ge(chunk_done, C_MOE + 3 * EXPERTS)
            for m in range(4):
                q = xT[:, 2 * m:2 * m + 2, :]
                tt(q, psum[:, ACC + m, :].rearrange("p (j t) -> p j t", j=2), q, ALU.add).then_inc(x_new, 1)

            upd[0] += 4
            l0, l1 = sm("lb", 0, 8), sm("lb", 8, 8)
            tt(lbt[:, 0, :], l0, l1, ALU.max).then_inc(lb_steps, 1)
            dve.wait_ge(lb_steps, 1)
            tt(lbt[:, 1, :], l0, lbt[:, 0, :], ALU.subtract).then_inc(lb_steps, 1)
            tt(lbt[:, 2, :], l1, lbt[:, 0, :], ALU.subtract).then_inc(lb_steps, 1)

            def copy_unit(n, dst):
                full(n)
                u = units.take()
                v.tensor_copy(dst, unit_view(u)).then_inc(unit_free, 1)

            copy_unit(C_K2, k_dst(0))
            dve.wait_ge(lb_exp, 1)
            link(tt(lbt[:, 5, :], lbt[:, 3, :], lbt[:, 4, :], ALU.add))
            link(v.reciprocal(lbt[:, 5, :], lbt[:, 5, :]))
            tt(lbt[:, 6, :], lbt[:, 3, :], lbt[:, 5, :], ALU.mult)
            link(tt(lbt[:, 7, :], lbt[:, 4, :], lbt[:, 5, :], ALU.mult))
            copy_unit(C_K2 + 1, k_dst(1))

            recip(5)
            dve.wait_ge(rstd_ready, 6)
            for m in range(4):
                for k in (2 * m, 2 * m + 1):
                    last = v.scalar_tensor_tensor(xT[:, k, :], xT[:, k, :], sm("f_g", k), rstd[:, 1, :],
                                                  ALU.mult, ALU.mult)
                last.then_inc(x_new, 1)
                upd[0] += 1
                dve.wait_ge(x_new, upd[0])
                gain("pre_mix_g", m)
            copy_unit(C_K2 + 2, k_dst(2))
            copy_unit(C_K2 + 3, k_dst(3))
            recip(6)
            dve.wait_ge(std_ready, 7)
            v.reciprocal(cols[:, 1, :], cols[:, 0, :]).then_inc(rcol_ready, 1)
            dve.wait_ge(rstd_ready, 7)
            dve.wait_ge(rcol_ready, 1)

            assert units.n == U_WIN2, (units.n, U_WIN2)

            def forget(m):
                f, k = ((ff, kf), (fb, kb))[m // 2]
                dve.wait_ge(f_sig, m + 1)
                for h in (2 * (m % 2), 2 * (m % 2) + 1):
                    c = 4 * (m // 2) + h
                    v.tensor_scalar(f[:, h, :], f[:, h, :], lbt[:, 7, c:c + 1], lbt[:, 6, c:c + 1], ALU.mult, ALU.add)
                    last = v.tensor_scalar(k[:, h, :], k[:, h, :], lbt[:, 7, c:c + 1], None, ALU.mult)
                link(last)

            def take_rows(n, dst):
                full(n)
                u = units.take()
                for t in range(TT):
                    last = v.tensor_scalar(dst[:, t, :], psum[:, u % UNITS, t * 256:(t + 1) * 256],
                                           cols[:, 1, t:t + 1], None, ALU.mult)
                last.then_inc(unit_free, 1)

            for m in range(2):
                evac_scaled(C_WIN2 + m, qh[:, 2 * m:2 * m + 2, :], 6)
            for m in range(4):
                f = (ff, fb)[m // 2]
                evac_scaled(C_WIN2 + 2 + m, f[:, 2 * (m % 2):2 * (m % 2) + 2, :], 6)
            take_rows(C_WIN2 + 6, v2[:, :, 0:256])
            forget(0)
            forget(1)
            take_rows(C_WIN2 + 7, v2[:, :, 256:512])
            forget(2)
            forget(3)
            for m in range(2):
                evac_scaled(C_WIN2 + 8 + m, hgate[:, 2 * m:2 * m + 2, :], 6)
            for m in range(2):
                evac_scaled(C_WIN2 + 10 + m, aqk[:, 2 * m:2 * m + 2, :], 6)
            full(C_WIN2 + 12)
            u = units.take()
            tt(aqk[:, 4, :], psum[:, u % UNITS, 0:T], rstd[:, 2, :], ALU.mult)
            for t in range(TT):
                last = v.tensor_scalar(av2[:, t, :], psum[:, u % UNITS, T + t * P:T + (t + 1) * P],
                                       cols[:, 1, t:t + 1], None, ALU.mult)
            last.then_inc(unit_free, 1)

            def sides(x, h):
                y = x.rearrange("p g t -> p (g t)").rearrange("p (b s i) -> p b s i", s=2, i=h)
                return y[:, :, 0, :], y[:, :, 1, :]

            def prepare(i):
                if i == 0:
                    tt(Kc[:], kf[:], kb[:], ALU.add).then_inc(level_ready, 1)
                    v.memset(Lf[:], 1.0)
                    link(v.memset(Lb[:], 1.0))
                    return
                h = 2 ** (i - 1)
                kk, qq = ((Kc, Qc), (Kc2, Qc2))[i % 2]
                if i >= 2:
                    dve.wait_ge(level_done, 2 * (i - 1))
                (kl, kr), (ql, qr) = sides(kk, h), sides(qq, h)
                (fl, fr), (bl, br) = sides(ff, h), sides(fb, h)
                (lfl, lfr), (lbl, lbr) = sides(Lf, h), sides(Lb, h)
                tt(kl, sides(kf, h)[0], lfl, ALU.mult)
                tt(kr, sides(kb, h)[1], lbr, ALU.mult)
                tt(qr, sides(qh, h)[1], fr, ALU.mult)
                tt(ql, sides(qh, h)[0], bl, ALU.mult).then_inc(level_ready, 1)
                if i == 8:
                    return
                wide = [P, 4 * T // (2 * h), h]
                dve.wait_ge(level_ready, i + 1)
                tt(lfl, lfl, fr[:, :, h - 1:h].to_broadcast(wide), ALU.mult)
                link(tt(lbr, lbr, bl[:, :, 0:1].to_broadcast(wide), ALU.mult))
                tt(fr, fr, fl[:, :, h - 1:h].to_broadcast(wide), ALU.mult)
                link(tt(bl, bl, br[:, :, 0:1].to_broadcast(wide), ALU.mult))

            def collect(i):
                for hp in range(2):
                    dve.wait_ge(level_done, 2 * i + hp + 1)
                    u = units.take()
                    got = psum[:, u % UNITS, :].rearrange("p (h c t) -> p h c t", h=2, c=2)
                    at = hp * 4 * T
                    step_c, at = (P, at + P) if i == 8 else (T + P, at)
                    base = AT_flat[:, at:at + 1]
                    dst = bass.AP(base.tensor, base.offset, [base.ap[0], [2 * T, 2], [step_c, 2], [1, P]])
                    wide = [P, 2, 2, P]
                    if i == 0:
                        ins = tt(dst, got, ident.unsqueeze(1).unsqueeze(1).to_broadcast(wide), ALU.mult)
                    elif i < 8:
                        ins = v.copy_predicated(dst, mask[:, i - 1, :].unsqueeze(1).unsqueeze(1).to_broadcast(wide), got)
                    else:
                        ins = v.tensor_copy(dst, got)
                    ins.then_inc(unit_free, 1)

            dve.wait_ge(qk_std, 1)
            v.reciprocal(cden[0:10, 1, :], cden[0:10, 0, :]).then_inc(qk_rstd, 1)
            for n, j0 in enumerate((0, 2, 4)):
                w = min(2, 5 - j0)
                dve.wait_ge(qk_row, n + 1)
                u = units.take()
                row = psum[:, u % UNITS, 0:w * T].rearrange("p (a t) -> p a t", a=w)
                v.scalar_tensor_tensor(aqn[:, j0:j0 + w, :], row, sm("q_g" if j0 < 4 else "k_g"), aqk[:, j0:j0 + w, :],
                                       ALU.mult, ALU.mult).then_inc(unit_free, 1)
            for n, j0 in enumerate((0, 2, 4)):
                w = min(2, 5 - j0)
                cos, sin = (cn(x, 0, T).unsqueeze(1).to_broadcast([P, w, T]) for x in ("cos", "sin"))
                dve.wait_ge(qk_rot, n + 1)
                u = units.take()
                row = psum[:, u % UNITS, 0:w * T].rearrange("p (a t) -> p a t", a=w)
                if n:
                    dve.wait_ge(roped, n)
                tt(rtmp[:, 0:w, :], row, sin, ALU.mult).then_inc(unit_free, 1)
                link(tt(aqk[:, j0:j0 + w, :], aqn[:, j0:j0 + w, :], cos, ALU.mult))
                dve.wait_ge(unit_free, u + 1)
                tt(aqk[:, j0:j0 + w, :], aqk[:, j0:j0 + w, :], rtmp[:, 0:w, :], ALU.add).then_inc(roped, 1)
            dve.wait_ge(dup_done, 1)
            u = units.take()
            v.tensor_copy(kdup[:], unit_view(u)).then_inc(unit_free, 1)

            def gqa_out(g, u):
                return v.tensor_copy(mix2[:, g // 2, :], psum[:, u % UNITS, 0:T])

            attention(4, QH, 2, 1.0 / 8, gqa_out)

            dve.wait_ge(s_mask, 16)
            prepare(0)
            for i in range(9):
                if i + 1 < 9:
                    prepare(i + 1)
                collect(i)
                if i % 2:
                    copy_unit(C_V2 + i // 2, v_dst(i // 2))
                dve.wait_ge(unit_free, units.n)
            v.nop().then_inc(A_ready, 1)
            dve.wait_ge(hg_act, 2)
            for hp in range(2):
                dve.wait_ge(rec_done, hp + 1)
                u = units.take()
                v.tensor_copy(mix2[:, 4 + 2 * hp:6 + 2 * hp, :], unit_view(u)).then_inc(unit_free, 1)
            dve.wait_ge(rec_std, 1)
            v.reciprocal(cden[0:4, 1, :], cden[0:4, 0, :]).then_inc(rec_rstd, 1)
            for hp in range(2):
                dve.wait_ge(rec_row, hp + 1)
                u = units.take()
                q = mix2[:, 4 + 2 * hp:6 + 2 * hp, :]
                v.scalar_tensor_tensor(q, unit_view(u), sm("hg_g"), q, ALU.mult, ALU.mult).then_inc(unit_free, 1)
                dve.wait_ge(unit_free, u + 1)
                tt(q, q, hgate[:, 2 * hp:2 * hp + 2, :], ALU.mult).then_inc(rec_ready, 1)

            def post(k, y, gain_name, next_name):
                recip(k)
                dve.wait_ge(rstd_ready, k + 1)
                for m in range(4):
                    link(tt(y[:, 2 * m:2 * m + 2, :], y[:, 2 * m:2 * m + 2, :], two(rstd[:, k % 4, :]), ALU.mult))
                    for c in (2 * m, 2 * m + 1):
                        last = v.scalar_tensor_tensor(xT[:, c, :], y[:, c, :], sm(gain_name, c), xT[:, c, :],
                                                      ALU.mult, ALU.add)
                    last.then_inc(x_new, 1)
                    upd[0] += 1
                    if next_name:
                        dve.wait_ge(x_new, upd[0])
                        gain(next_name, m)

            y_dst = lambda m: yT[:, 2 * m:2 * m + 2, :]
            copy_units(C_WO2, y_dst)
            dve.wait_ge(unit_free, units.n)
            post(7, yT, "post_mix_g", "pre_x_g")
            recip(8)
            dve.wait_ge(rstd_ready, 9)
            for m in range(4):
                evac_scaled(C_Q2 + m, qT[:, 2 * m:2 * m + 2, :], 8)
            attention(12, 4, 1, 1.0 / 16, cross_out)
            copy_units(C_XO2, y_dst)
            v.memset(upad2[:, :, :, 0:1], 0.0)
            link(v.memset(upad2[:, :, :, T + 1:T + 2], 0.0))
            dve.wait_ge(unit_free, units.n)
            post(9, yT, "post_x_g", "pre_ffn_g")
            recip(10)
            dve.wait_ge(rstd_ready, 11)

            u_ffn = units.n

            def ffn_step(f, i):
                c = C_FFN if f == 0 else C_FFN + 2 + 3 * (f - 1)
                b = f % 2
                for half in range(2):
                    u = u_ffn + 2 * f + half
                    dve.wait_ge(chunk_done, i * 6 + (c + half + 1))
                    tt(upad2[:, b, 2 * half:2 * half + 2, 1:T + 1], unit_view(u), two(rstd[:, 2, :]),
                       ALU.mult).then_inc(unit_free, 1)
                    dve.wait_ge(unit_free, i * 4 + (u + 1))
                    n = 12 * f + 6 * half
                    for tap in (1, 0, 2):
                        for j in range(2):
                            jj = 2 * half + j
                            col = SMALL["ffn_w"] + 16 * f + 4 * jj
                            w = small[:, bass.ds(i * 32 + (col + tap), 1)]
                            x = upad2[:, b, jj, tap:tap + T]
                            if tap == 1:
                                bias = small[:, bass.ds(i * 32 + (col + 3), 1)]
                                ins = v.tensor_scalar(fconv[:, b, jj, :], x, w, bias, ALU.mult, ALU.add)
                            else:
                                dve.wait_ge(fconv_steps, i * 24 + (n - 1))
                                ins = v.scalar_tensor_tensor(fconv[:, b, jj, :], x, w, fconv[:, b, jj, :],
                                                             ALU.mult, ALU.add)
                            ins.then_inc(fconv_steps, 1)
                            n += 1
                dve.wait_ge(fconv_steps, i * 24 + (12 * f + 12))
                dve.wait_ge(fsilu, i * 2 + (f + 1))
                tt(act_f[:, b], fconv[:, b, 0:2, :], fconv[:, b, 2:4, :], ALU.mult).then_inc(fact_ready, 1)

            ffn_step(0, 0)
            with dve.Fori(0, (FSTEPS - 1) // 2) as i:
                ffn_step(1, i)
                ffn_step(2, i)
            dve.wait_ge(chunk_done, CHUNKS)
            for m in range(4):
                v.tensor_copy(yF[:, 2 * m:2 * m + 2, :],
                              psum[:, ACC + m, :].rearrange("p (j t) -> p j t", j=2)).then_inc(y_ready, 1)
            dve.wait_ge(y_ready, 4)
            post(11, yF, "post_ffn_g", None)


def _constants():
    c = np.zeros((P, NCONST), np.float32)
    p = np.arange(P)
    t = np.arange(T)

    def put(name, a, at=0):
        c[:a.shape[0], CONST[name] + at:CONST[name] + at + a.shape[1]] = a

    put("ident", np.eye(P))
    put("ones", np.ones((P, P)))
    for i, w in enumerate(POOL_W):
        put("rcnt", np.broadcast_to(np.float32(1) / np.minimum(t + 1, w).astype(np.float32), (P, T)), T * i)
    inv = np.power(np.float32(10000.0), -np.arange(16, dtype=np.float32) / np.float32(16)).astype(np.float32)
    ang = np.concatenate([(t // 64).astype(np.float32)[:, None] * inv, (t % 64).astype(np.float32)[:, None] * inv], 1)
    pair = ang[:, (p % 64) // 2].T
    put("cos", np.cos(pair))
    put("sin", np.sin(pair))
    rot = np.zeros((P, P))
    rot[p[1::2], p[0::2]] = -1
    rot[p[0::2], p[1::2]] = 1
    put("rot", rot)
    for j in range(2):
        put("dup", (p[:, None] == 64 * j + p[None, :] % 64).astype(float), 128 * j)
    for j in range(5):
        put("qk_sum", (2 * j + p[:, None] // 64 == np.arange(10)[None, :]).astype(float), 10 * j)
        put("qk_row", (np.arange(10)[:, None] == 2 * j + p[None, :] // 64).astype(float), 128 * j)
    for h in range(HG):
        put("hg_sum", np.broadcast_to(np.arange(4)[None, :] == h, (P, 4)).astype(float), 4 * h)
        put("hg_row", np.broadcast_to(np.arange(4)[:, None] == h, (4, P)).astype(float), 128 * h)
    put("prio", np.broadcast_to(np.tile([4.0, 3.0, 2.0, 1.0], 2), (P, 8)))
    x = p[:, None] ^ p[None, :]
    m = np.zeros((P, 8, P), np.int32)
    for i in range(7):
        m[:, i, :] = (x >> i) == 1
    m[:, 7, :] = x == 0
    return c, m


def _tiles(w, rows, c0, width):
    return w.reshape(rows, P, -1)[:, :, c0:c0 + width].transpose(1, 0, 2).reshape(P, rows * width)


def _stream(a):
    s = np.zeros((CHUNKS, P, CW), np.float32)

    def units(at, w, order, c0=0):
        for i, u in enumerate(order):
            s[at + i] = _tiles(w, DK, c0 + 256 * u, 256)

    units(C_WIN, a["w_in"][0], range(24))
    s[C_POOL, :, 0:1024] = a["w_pool_grp"][0].transpose(1, 0, 2).reshape(P, 1024)
    for m in range(4):
        s[C_MERGE + m, :, 0:1024] = _tiles(a["w_a_out"][0], 4, 256 * m, 256)
        s[C_MERGE + m, :, 1024:2048] = _tiles(a["w_c_out"][0], 4, 256 * m, 256)
    for suffix, k, v, q, o in (("", C_K1, C_V1, C_Q1, C_XO1), ("_2", C_K2, C_V2, C_Q2, C_XO2)):
        units(k, a["w_xkv" + suffix][0], range(4))
        units(v, a["w_xkv" + suffix][0], range(4), D)
        units(q, a["w_xq" + suffix][0], range(4))
        units(o, a["w_xo" + suffix][0], range(4))
    units(C_WO, a["w_o"][0], range(4))
    units(C_WIN2, a["w_in_2"][0], WIN2_ORDER)
    units(C_WO2, a["w_out_2"][0], range(4))

    def steps(at, count, gate, up, down):
        for e in range(count):
            g = at if e == 0 else at + 2 + 3 * (e - 1)
            s[g], s[g + 1] = gate(e), up(e)
            s[at + 3 * count - 1 if e == count - 1 else at + 3 * e + 4] = _tiles(down(e), 2, 0, D)

    steps(C_MOE, EXPERTS, lambda e: _tiles(a["w_e_gate"][0, e], DK, 0, 256),
          lambda e: _tiles(a["w_e_up"][0, e], DK, 0, 256), lambda e: a["w_e_down"][0, e])
    steps(C_FFN, FSTEPS, lambda f: _tiles(a["w_up_2"][0], DK, 256 * f, 256),
          lambda f: _tiles(a["w_up_2"][0], DK, FF + 256 * f, 256), lambda f: a["w_down_2"][0, 256 * f:256 * (f + 1)])
    return s


def _small(a):
    s = np.zeros((P, NSMALL), np.float32)

    def put(name, x, at=0):
        y = np.asarray(x).reshape(-1, P).T
        s[:, SMALL[name] + at:SMALL[name] + at + y.shape[1]] = y

    for name, key in (("mix_g", "norm_mix_g"), ("pool_s", "pool_scale"), ("x_g", "norm_x_g"), ("mem_g", "norm_mem_g"),
                      ("ffn_g", "norm_ffn_g"), ("f_g", "norm_f_g"), ("conv_b", "conv_a_b"), ("ln_g", "ln_a_g"),
                      ("ln_b", "ln_a_b"), ("c_w", "conv_c_w"), ("conv_w", "conv_a_w"), ("pre_mix_g", "pre_mix_g_2"),
                      ("post_mix_g", "post_mix_g_2"), ("pre_x_g", "pre_x_g_2"), ("mem2_g", "mem_norm_g_2"),
                      ("post_x_g", "post_x_g_2"), ("pre_ffn_g", "pre_ffn_g_2"), ("post_ffn_g", "post_ffn_g_2"),
                      ("hg_g", "hg_out_norm_g_2")):
        put(name, a[key])
    for name, key in (("q_g", "q_norm_g_2"), ("k_g", "k_norm_g_2")):
        put(name, np.tile(a[key].reshape(-1), 2))
    put("lb", a["hg_lb_2"].transpose(1, 0, 2))
    s[0:4, SMALL["r_b"]] = a["b_rg"][0]
    s[4:20, SMALL["r_b"]] = a["b_re"][0]
    w, b = a["conv_w_2"][0], a["conv_b_2"][0]
    for f in range(FSTEPS):
        for i in range(4):
            c0 = FF * (i // 2) + 256 * f + P * (i % 2)
            for j in range(3):
                put("ffn_w", w[j, c0:c0 + P], 16 * f + 4 * i + j)
            put("ffn_w", b[c0:c0 + P], 16 * f + 4 * i + 3)
    return s


def _turned(x):
    return np.ascontiguousarray(x[0].T.reshape(DK, P, T).transpose(1, 0, 2))


def kernel(**inputs):
    import concourse.bacc as _bacc
    from concourse.bass_utils import run_bass_kernel_spmd as _run

    a = {k: np.asarray(v) for k, v in inputs.items()}
    const, mask = _constants()
    router = np.concatenate([a["w_rg"][0], a["w_re"][0]], axis=1)
    arrays = {
        "stream": _stream(a),
        "x_t": _turned(a["x"]),
        "mem_t": _turned(a["mem"]),
        "mem2_t": _turned(a["mem_2"]),
        "small": _small(a),
        "const": const,
        "mask": mask,
        "router": np.ascontiguousarray(router.reshape(DK, P, 20).transpose(1, 0, 2)),
    }
    nc = _bacc.Bacc("TRN2", target_bir_lowering=False, num_devices=1)
    args = [nc.dram_tensor(k + "_in", x.shape, mybir.dt.from_np(x.dtype), kind="ExternalInput").ap() for k, x in arrays.items()]
    out = nc.dram_tensor("out_t", (P, DK, T), F32, kind="ExternalOutput").ap()
    build(nc, *args, out)
    r = _run(nc, [{k + "_in": x for k, x in arrays.items()}], core_ids=[0])
    got = r.results[0]["out_t"]
    return np.ascontiguousarray(got.transpose(1, 0, 2).reshape(D, T).T)[None]
```

```python
from contextlib import ExitStack

import numpy as np
import concourse.bass as bass
from concourse import mybir

ALU = mybir.AluOpType
ACT = mybir.ActivationFunctionType
F32 = mybir.dt.float32
F32R = mybir.dt.float32r
I32 = mybir.dt.int32
AX_X = mybir.AxisListType.X

P = 128
T = 256
TT = T // P
D = 1024
DK = D // P
EPS = 1e-6
HW = 1024
RAW = 6
SPLIT = 4
UNITS = 4
SB = 3
STAT = 7
ACC = 4
CONV_K = 31
C_K = 3
POOL_W = (2, 4, 8, 16)
PADW = 16
EXPERTS = 16
GROUPS = 4
FF = 2816
FSTEPS = FF // 256
HG = 4
QH = 8
NEG = -1.0e30

C_WIN = 0
C_POOL = C_WIN + 24
C_MERGE = C_POOL + 1
C_K1 = C_MERGE + 4
C_V1 = C_K1 + 4
C_WO = C_V1 + 4
C_Q1 = C_WO + 4
C_XO1 = C_Q1 + 4
C_MOE = C_XO1 + 4
C_K2 = C_MOE + 3 * EXPERTS
C_WIN2 = C_K2 + 4
C_V2 = C_WIN2 + 13
C_WO2 = C_V2 + 4
C_Q2 = C_WO2 + 4
C_XO2 = C_Q2 + 4
C_FFN = C_XO2 + 4
CHUNKS = C_FFN + 3 * FSTEPS
HALVES = 2 * CHUNKS
WHOLE0, WHOLE1 = 2 * C_POOL, 2 * (C_MERGE + 4)
WIN2_ORDER = (3, 4, 5, 6, 7, 8, 9, 10, 11, 12, 0, 1, 2)

U_MOE_FIRST = 64
U_MOE = U_MOE_FIRST + 2 + EXPERTS // 2
U_WIN2 = U_MOE + 2 * (EXPERTS - 1) + 4
U_REC = 162
U_WO2 = U_REC + 4
U_XO2 = U_WO2 + 4 + 4 + 8

SMALL = {}
_at = 0
for _name, _n in (("mix_g", 8), ("pool_s", 8), ("x_g", 8), ("mem_g", 8), ("ffn_g", 8), ("f_g", 8),
                  ("conv_b", 4), ("ln_g", 4), ("ln_b", 4), ("c_w", 4 * C_K), ("conv_w", 4 * CONV_K),
                  ("pre_mix_g", 8), ("post_mix_g", 8), ("pre_x_g", 8), ("mem2_g", 8), ("post_x_g", 8),
                  ("pre_ffn_g", 8), ("post_ffn_g", 8), ("hg_g", 1), ("q_g", 1), ("k_g", 1),
                  ("lb", 16), ("r_b", 1), ("ffn_w", 16 * FSTEPS)):
    SMALL[_name] = _at
    _at += _n
NSMALL = _at

CONST = {}
_at = 0
for _name, _n in (("ident", 128), ("ones", 128), ("rcnt", 4 * PADW), ("cos", T), ("sin", T), ("rot", 128),
                  ("dup", 256), ("qk_sum", 5 * 10), ("hg_sum", 16),
                  ("prio", 8)):
    CONST[_name] = _at
    _at += _n
NCONST = _at


def build(nc, stream, xt_in, memt_in, mem2t_in, small_in, const_in, mask_in, router_in, out_t):
    ctx = ExitStack()
    with ctx:
        def sb(name, shape, dt=F32):
            return ctx.enter_context(nc.sbuf_tensor(name, shape, dt))

        def sem(name):
            return ctx.enter_context(nc.semaphore(name))

        psum = ctx.enter_context(nc.psum_tensor("psum", [P, 8, 512], F32))

        raw = sb("raw", [P, RAW, HW])
        wh = sb("wh", [P, SPLIT, HW], F32R)
        wl = sb("wl", [P, SPLIT, HW], F32R)
        xT = sb("xT", [P, DK, T])
        sq = sb("sq", [P, DK, T])
        memn = sb("memn", [P, 2, DK, T])
        kT = sb("kT", [P, DK, T])
        vm = sb("vm", [P, TT, D])
        small = sb("small", [P, NSMALL])
        const = sb("const", [P, NCONST])
        mask = sb("mask", [P, 8, P], I32)
        router = sb("router", [P, DK, 20])
        rstd = sb("rstd", [P, 4, T])
        std = sb("std", [P, T])
        av2 = sb("av2", [P, TT, 128])
        cden = sb("cden", [16, 2, T])
        zeros = sb("zeros", [P, P])
        eps = sb("eps", [P, 1])
        nmax = sb("nmax", [P, 16, TT])
        negm = sb("negm", [P, 16, TT])
        ssum = sb("ssum", [P, 16, TT])
        rsum = sb("rsum", [P, 16, TT])
        cols = sb("cols", [P, 2, TT])
        lbt = sb("lbt", [P, 8, 8])
        WORK = 12800
        ACT_AT = 8192
        PAIR = DK * T
        area_at = -(-nc.sbuf_base // 32) * 32
        sb("area", [P, WORK + 4 * PAIR])

        def at(name, start, shape, dt):
            return nc.alloc_sbuf_tensor_at(name, shape, dt, offset=area_at + 4 * start)

        work = at("work", 0, [P, WORK], F32)
        xh, xl = (at(n, WORK + i * PAIR, [P, DK, T], F32R) for i, n in enumerate(("xh", "xl")))
        yh, yl = (at(n, WORK + (2 + i) * PAIR, [P, DK, T], F32R) for i, n in enumerate(("yh", "yl")))
        xpair = at("xpair", WORK, [P, 2 * PAIR], F32)
        ypair = at("ypair", WORK + 2 * PAIR, [P, 2 * PAIR], F32)
        act_h, act_l = (at(n, ACT_AT + i * 4 * T, [P, 2, 2, T], F32R) for i, n in enumerate(("act_h", "act_l")))

        def f32(ap):
            return ap.bitcast(F32)

        def sm(name, i=0, n=1):
            return small[:, SMALL[name] + i:SMALL[name] + i + n]

        def cn(name, i=0, n=128, p=P):
            return const[0:p, CONST[name] + i:CONST[name] + i + n]

        ident = cn("ident")
        ones = cn("ones")

        class Region:

            def __init__(self, start=0):
                self.at = start

            def __call__(self, *dims):
                n = int(np.prod(dims))
                v = work[:, self.at:self.at + n]
                self.at += n
                assert self.at <= WORK, self.at
                if len(dims) == 2:
                    v = v.rearrange("p (a b) -> p a b", a=dims[0])
                elif len(dims) == 3:
                    v = v.rearrange("p (a b c) -> p a b c", a=dims[0], b=dims[1])
                return v

        r = Region()
        gates = r(24, T)
        apad = r(4, T + CONV_K - 1)
        lnstd = r(T)
        lnrstd = r(T)
        cx = r(4, T)
        cpad = r(4, T + C_K - 1)
        upad = r(4, T + PADW)
        ubuf = r(4, T + PADW)
        merged = work[:, r.at - 8 * (T + PADW):r.at - 8 * (T + PADW) + DK * T].rearrange("p (a b) -> p a b", a=DK)
        aval, agate, aacc, pT = (ypair[:, 4 * T * i:4 * T * (i + 1)].rearrange("p (a b) -> p a b", a=4)
                                 for i in range(4))
        asq = agate
        actT = aval
        cc, ctmp = kT[:, 0:4, :], kT[:, 4:8, :]
        vm_flat = vm.rearrange("p t d -> p (t d)")
        cb = vm_flat[:, 0:4 * T].rearrange("p (a b) -> p a b", a=4)
        cy = vm_flat[:, 4 * T:8 * T].rearrange("p (a b) -> p a b", a=4)
        mt1, mt2 = agate, aacc

        r = Region(9216)
        probs = r(4, TT, T)
        probsT = r(3, TT, T)
        r = Region(0)
        qT = r(DK, T)
        yT = r(DK, T)

        r = Region(0)
        rg = r(EXPERTS, T)
        gs = r(2, 2, T)
        us = r(2, 2, T)
        logitT = r(T)
        gateT = r(T)
        lt = r(TT, 20)
        gmx = r(TT, 1)
        gsub = r(TT, 4)
        gexp = r(TT, 4)
        gsm = r(TT, 1)
        gval = r(TT, 1)
        eqp = r(TT, 4)
        eqm = r(TT, 1)
        ohg = r(TT, 4)
        lsel = r(TT, 4)
        lprod = r(TT, 16)
        m1 = r(TT, 1)
        oh1 = r(TT, 4)
        lsel2 = r(TT, 4)
        m2 = r(TT, 1)
        oh2 = r(TT, 4)
        dm = r(TT, 1)
        ed = r(TT, 1)
        den = r(TT, 1)
        w1 = r(TT, 1)
        w2 = r(TT, 1)
        g4a = r(TT, 4)
        g4b = r(TT, 4)
        gate16 = r(TT, 16)
        assert r.at <= ACT_AT

        r = Region(0)
        mix2 = r(DK, T)
        qh = r(HG, T)
        ff = r(HG, T)
        fb = r(HG, T)
        kf = r(HG, T)
        kb = r(HG, T)
        hgate = r(HG, T)
        v2 = r(TT, 512)
        assert r.at <= 9216, r.at
        r = Region(9216)
        Kc = r(HG, T)
        Qc = r(HG, T)
        AT_flat = xpair[:, 0:PAIR]
        AT = AT_flat.rearrange("p (h s t) -> p h s t", h=HG, s=TT)
        Lf, Lb = (xpair[:, PAIR + 4 * T * i:PAIR + 4 * T * (i + 1)].rearrange("p (a b) -> p a b", a=4)
                  for i in range(2))
        aqk = memn[:, 0, 0:5, :]
        kdup = memn[:, 0, 5:7, :]
        Kc2, Qc2 = memn[:, 0, 0:4, :], memn[:, 0, 4:8, :]
        asq2 = sq[:, 0:5, :]
        aqn = sq[:, 0:5, :]
        rtmp = Kc[:, 0:2, :]

        r = Region(0)
        upad2 = r(2, 4, T + 2)
        fconv = r(2, 4, T)
        yF = r(DK, T)
        assert r.at <= ACT_AT

        s_small = sem("small_loaded")
        s_x = sem("x_loaded")
        s_mem = sem("mem_loaded")
        s_mem2 = sem("mem2_loaded")
        s_cst = sem("const_loaded")
        s_mask = sem("mask_loaded")
        s_rt = sem("router_loaded")
        landed = [sem(f"landed{i}") for i in range(RAW)]
        hi_ready = sem("hi_ready")
        lo_pool = sem("lo_pool")
        lo_dve = sem("lo_dve")
        half_done = sem("half_done")
        mem_hi = sem("mem_hi")
        mem_split = sem("mem_split")
        unit_free = sem("unit_free")
        zeroed = sem("zeroed")
        xg_ready = sem("xg_ready")
        x_new = sem("x_new")
        y_ready = sem("y_ready")
        sq_ready = sem("sq_ready")
        stats_done = sem("stats_done")
        std_ready = sem("std_ready")
        rstd_ready = sem("rstd_ready")
        memn_ready = sem("memn_ready")
        agate_sig = sem("agate_sig")
        gates_sig = sem("gates_sig")
        a_glu = sem("a_glu")
        conv_a = sem("conv_a_steps")
        pads_zero = sem("pads_zero")
        pool_steps = sem("pool_steps")
        p_ready = sem("pooled_ready")
        c_ready = sem("c_ready")
        ln_mean = sem("ln_mean")
        ln_centered = sem("ln_centered")
        ln_sq = sem("ln_sq")
        ln_var = sem("ln_var")
        ln_std = sem("ln_std")
        ln_normed = sem("ln_normed")
        a_act = sem("a_act")
        pool_full = sem("pool_full")
        merged_ready = sem("merged_ready")
        scores_done = sem("scores_done")
        maxed = sem("maxed")
        neg_ready = sem("neg_ready")
        exp_done = sem("exp_done")
        rsum_ready = sem("rsum_ready")
        probs_ready = sem("probs_ready")
        turned = sem("probs_turned")
        o_done = sem("o_done")
        logits_done = sem("logits_done")
        logits_ready = sem("logits_ready")
        ltok_done = sem("ltok_done")
        route = sem("route_steps")
        route_exp = sem("route_exp")
        gate16_ready = sem("gate16_ready")
        gateT_done = sem("gateT_done")
        gateT_ready = sem("gateT_ready")
        rg_full = sem("rg_full")
        silu_done = sem("silu_done")
        act_ready = sem("act_ready")
        acc_zero = sem("acc_zero")
        lb_steps = sem("lb_steps")
        lb_exp = sem("lb_exp")
        f_raw = sem("f_raw")
        f_sig = sem("f_sig")
        hq_act = sem("hq_act")
        hg_act = sem("hg_act")
        scan_steps = sem("scan_steps")
        level_ready = sem("level_ready")
        level_done = sem("level_done")
        A_ready = sem("A_ready")
        rec_done = sem("rec_done")
        rec_sq = sem("rec_sq")
        rec_sum = sem("rec_sum")
        rec_std = sem("rec_std")
        rec_rstd = sem("rec_rstd")
        rec_row = sem("rec_row")
        rec_ready = sem("rec_ready")
        qk_sq = sem("qk_sq")
        qk_sum = sem("qk_sum")
        qk_std = sem("qk_std")
        qk_rstd = sem("qk_rstd")
        qk_row = sem("qk_row")
        qk_rot = sem("qk_rot")
        roped = sem("roped")
        dup_done = sem("dup_done")
        rcol_ready = sem("rcol_ready")
        fconv_steps = sem("fconv_steps")
        fsilu = sem("fsilu")
        fact_ready = sem("fact_ready")
        loop_chain = sem("dve_loop_chain")
        chain = sem("dve_chain")
        stored = sem("stored")

        block = ctx.enter_context(nc.Block())

        def hi_count(c):
            return c + 1 - (WHOLE1 - WHOLE0 if c >= WHOLE1 else 0)

        def lo_count(c):
            return c // 2 + 1 - ((WHOLE1 - WHOLE0) // 2 if c >= WHOLE1 else 0)

        def rest_sem(c):
            return lo_dve if c % 2 else lo_pool

        PASS = 12
        PASS_LANDED = 16 * PASS // RAW
        assert PASS % RAW == 0 and PASS % SPLIT == 0

        class Splitter:

            def __init__(self, issue, first, stride):
                self.issue, self.next, self.stride = issue, first, stride

            def upto(self, c):
                while self.next <= min(c, HALVES - 1):
                    if not WHOLE0 <= self.next < WHOLE1:
                        self.issue(self.next, 0)
                    self.next += self.stride

            def skip_to(self, c):
                while self.next < c:
                    self.next += self.stride

        def two(ap):
            return ap.unsqueeze(1).to_broadcast([P, 2, T])

        def unit_view(u):
            return psum[:, u % UNITS, :].rearrange("p (j t) -> p j t", j=2)

        class UnitCount:

            def __init__(self):
                self.n = 0

            def take(self, n=1):
                self.n += n
                return self.n - n

        @block.sync
        def _(sp):
            sp.dma_start(xT[:], xt_in).then_inc(s_x, 16)
            sp.dma_start(small[:], small_in).then_inc(s_small, 16)

            def load(slot, c):
                sp.dma_start(raw[:, slot, :], stream[c]).then_inc(landed[slot], 16)

            def reload(c, i=0):
                b = c - RAW
                if WHOLE0 <= b < WHOLE1:
                    sp.wait_ge(half_done, b + 1)
                else:
                    sp.wait_ge(rest_sem(b), i * (RAW // 2) + lo_count(b))
                load(c % RAW, i * RAW + c)

            for c in range(RAW):
                load(c, c)
            turn = WHOLE0 // RAW
            with sp.Fori(0, turn - 1) as i:
                for j in range(RAW):
                    reload(RAW + j, i)
            mid = -(-(WHOLE1 + RAW) // RAW) * RAW
            for c in range(turn * RAW, mid):
                reload(c)
            with sp.Fori(0, (HALVES - mid) // RAW) as i:
                for j in range(RAW):
                    reload(mid + j, i)
            for c in range(mid + (HALVES - mid) // RAW * RAW, HALVES):
                reload(c)
            for m in range(4):
                sp.wait_ge(x_new, 4 * 6 + m + 1)
                sp.dma_start(out_t[:, 2 * m:2 * m + 2, :], xT[:, 2 * m:2 * m + 2, :]).then_inc(stored, 16)
            sp.wait_ge(stored, 64)

        @block.tensor
        def _(pe):
            units = UnitCount()

            def matmul(out, w, x, start, stop, **kw):
                return nc.tensor.matmul(out, w, x, start=start, stop=stop, **kw)

            def wait_raw(c):
                pe.wait_ge(landed[c % RAW], 16 * (c // RAW + 1))

            def wait_split(c):
                pe.wait_ge(rest_sem(c), lo_count(c))

            def free_bank(u):
                if u >= UNITS:
                    pe.wait_ge(unit_free, u - UNITS + 1)

            def three(out, a_h, a_l, b_h, b_l, start, stop, **kw):
                matmul(out, a_h, b_h, start, False, **kw)
                matmul(out, a_h, b_l, False, False, **kw)
                return matmul(out, a_l, b_h, False, stop, **kw)

            def columns(out, slot, x):
                for k in range(DK):
                    w = slice(k * P, (k + 1) * P)
                    last = three(out, wh[:, slot, w], wl[:, slot, w], x[0][:, k, :], x[1][:, k, :], k == 0, k == DK - 1)
                return last

            def rows(out, slot, x):
                for t in range(TT):
                    for k in range(DK):
                        w = slice(k * P, (k + 1) * P)
                        q = slice(t * P, (t + 1) * P)
                        last = three(out(t), x[0][:, k, q], x[1][:, k, q], wh[:, slot, w], wl[:, slot, w],
                                     k == 0, k == DK - 1)
                return last

            def project(n, x):
                u = units.take()
                free_bank(u)
                for j in range(2):
                    c = 2 * n + j
                    wait_split(c)
                    columns(psum[:, u % UNITS, j * T:(j + 1) * T], c % SPLIT, x).then_inc(half_done, 1)

            def project_rows(n, x):
                u = units.take()
                free_bank(u)
                for j in range(2):
                    c = 2 * n + j
                    wait_split(c)
                    for t in range(TT):
                        q = slice(t * P, (t + 1) * P)
                        for kk in range(DK // 2):
                            k = j * DK // 2 + kk
                            w = slice(kk * 256, (kk + 1) * 256)
                            last = three(psum[:, u % UNITS, t * 256:(t + 1) * 256], x[0][:, k, q], x[1][:, k, q],
                                         wh[:, c % SPLIT, w], wl[:, c % SPLIT, w], k == 0 and t == 0, k == DK - 1,
                                         skip_group_check=True)
                    last.then_inc(half_done, 1)

            def project_two(n, x, ready):
                u0 = units.take(2)
                free_bank(u0 + 1)
                for m in range(4):
                    pe.wait_ge(xg_ready, ready + m + 1)
                    for i in range(4):
                        c = 2 * n + i
                        if m == 0:
                            wait_split(c)
                        for k in (2 * m, 2 * m + 1):
                            w = slice(k * P, (k + 1) * P)
                            last = three(psum[:, (u0 + i // 2) % UNITS, (i % 2) * T:(i % 2 + 1) * T],
                                         wh[:, c % SPLIT, w], wl[:, c % SPLIT, w], x[0][:, k, :], x[1][:, k, :],
                                         k == 0 and i % 2 == 0, k == DK - 1, skip_group_check=True)
                        if m == 3:
                            last.then_inc(half_done, 1)

            def stats(k, columns=False):
                if k:
                    pe.wait_ge(std_ready, k)
                for i in range(DK):
                    if i % 2 == 0:
                        pe.wait_ge(sq_ready, 4 * k + i // 2 + 1)
                    last = matmul(psum[:, STAT, 0:T], ones, sq[:, i, :], i == 0, i == DK - 1)
                if columns:
                    for t in range(TT):
                        for i in range(DK):
                            last = matmul(psum[:, STAT, T + t:T + t + 1], sq[:, i, t * P:(t + 1) * P],
                                          ones[:, 0:1], i == 0, i == DK - 1)
                last.then_inc(stats_done, 1)

            def attention(base, heads, group, scores, values):
                def score(h):
                    hh = base + h
                    if hh >= SB:
                        pe.wait_ge(exp_done, hh - SB + 1)
                    scores(h, 4 + hh % SB).then_inc(scores_done, 1)

                for h in range(SB):
                    score(h)
                for g in range(0, heads, group):
                    for h in range(g, g + group):
                        hh = base + h
                        u = units.take()
                        free_bank(u)
                        pe.wait_ge(probs_ready, hh + 1)
                        for m in range(TT):
                            for t in range(TT):
                                last = nc.tensor.transpose(psum[:, u % UNITS, m * T + t * P:m * T + (t + 1) * P],
                                                           probs[:, hh % 4, t, m * P:(m + 1) * P], ident)
                        last.then_inc(turned, 1)
                        if h + SB < heads:
                            score(h + SB)
                    uo = units.take()
                    free_bank(uo)
                    pe.wait_ge(unit_free, uo)
                    for h in range(g, g + group):
                        last = values(h, (base + h) % 3, uo % UNITS)
                        last.then_inc(o_done, 1)

            def cross_scores(h, bank):
                for t in range(TT):
                    for d in range(2):
                        last = matmul(psum[:, bank, t * T:(t + 1) * T], qT[:, 2 * h + d, t * P:(t + 1) * P],
                                      kT[:, 2 * h + d, :], d == 0, d == 1)
                return last

            def cross_values(h, pslot, bank):
                for d in range(2):
                    for m in range(TT):
                        last = matmul(psum[:, bank, d * T:(d + 1) * T], vm[:, m, h * 256 + d * P:h * 256 + (d + 1) * P],
                                      probsT[:, pslot, m, :], m == 0, m == 1)
                return last

            xg, yg = (xh, xl), (yh, yl)
            project_two(C_WIN, xg, 0)
            pe.wait_ge(s_cst, 16)
            stats(0)
            project(C_WIN + 2, xg)
            stats(1)
            project(C_WIN + 3, xg)
            stats(2)
            for n in range(C_WIN + 4, C_WIN + 18):
                project(n, xg)
            pe.wait_ge(conv_a, 4 * CONV_K)
            for c in range(4):
                last = matmul(psum[:, 6, 0:T], ones, aacc[:, c, :], c == 0, c == 3)
            last.then_inc(ln_mean, 1)
            for n in range(C_WIN + 18, C_WIN + 21):
                project(n, xg)
            pe.wait_ge(ln_sq, 2)
            for c in range(4):
                last = matmul(psum[:, 5, 0:T], ones, asq[:, c, :], c == 0, c == 3)
            last.then_inc(ln_var, 1)
            for n in range(C_WIN + 21, C_WIN + 24):
                project(n, xg)

            pe.wait_ge(p_ready, 1)
            wait_raw(2 * C_POOL)
            wait_raw(2 * C_POOL + 1)
            for m in range(4):
                u = units.take()
                free_bank(u)
                for j in range(2):
                    last = matmul(psum[:, u % UNITS, j * T:(j + 1) * T],
                                  raw[:, (2 * C_POOL + 1) % RAW, m * 256 + j * P:m * 256 + (j + 1) * P], pT[:, m, :], True, True)
                    if m == 3:
                        last.then_inc(half_done, 1)
                if m < 3:
                    last.then_inc(pool_full, 1)
            pe.wait_ge(a_act, 4)
            pe.wait_ge(c_ready, 1)
            for m in range(4):
                for i, x in enumerate((actT, cy)):
                    c = 2 * (C_MERGE + m) + i
                    wait_raw(c)
                    u = units.take()
                    free_bank(u)
                    for j in range(2):
                        for k in range(4):
                            last = matmul(psum[:, u % UNITS, j * T:(j + 1) * T],
                                          raw[:, c % RAW, k * 256 + j * P:k * 256 + (j + 1) * P], x[:, k, :],
                                          k == 0, k == 3)
                    last.then_inc(half_done, 1)
            pe.wait_ge(mem_split, 1)
            for m in range(4):
                project(C_K1 + m, xg)
            for m in range(4):
                project_rows(C_V1 + m, xg)
            pe.wait_ge(merged_ready, 4)
            for m in range(4):
                project(C_WO + m, yg)
            project_two(C_Q1, xg, 4)
            stats(3)
            for m in range(2, 4):
                project(C_Q1 + m, xg)
            pe.wait_ge(unit_free, units.n)
            attention(0, 4, 1, cross_scores, cross_values)
            pe.wait_ge(unit_free, units.n)
            for m in range(4):
                project(C_XO1 + m, yg)
            project_two(C_MOE, xg, 8)
            stats(4)
            pe.wait_ge(s_rt, 16)
            for part in range(2):
                for k in range(DK):
                    last = matmul(psum[0:20, 6, 0:T], router[:, k, :], f32(xg[part][:, k, :]),
                                  part == 0 and k == 0, part == 1 and k == DK - 1)
            last.then_inc(logits_done, 1)
            pe.wait_ge(logits_ready, 1)
            for t in range(TT):
                last = nc.tensor.transpose(psum[:, 5, t * 20:(t + 1) * 20], logitT[0:20, t * P:(t + 1) * P],
                                           ident[0:20, 0:20])
            last.then_inc(ltok_done, 1)
            pe.wait_ge(gate16_ready, 1)
            for t in range(TT):
                last = nc.tensor.transpose(psum[0:16, 6, t * P:(t + 1) * P], gate16[:, t, :], ident)
            last.then_inc(gateT_done, 1)
            pe.wait_ge(gateT_ready, 1)
            for e in range(0, EXPERTS, 2):
                u = units.take()
                free_bank(u)
                for j in range(2):
                    last = matmul(psum[:, u % UNITS, j * T:(j + 1) * T],
                                  ident[0:16, e + j:e + j + 1].to_broadcast([16, P]), gateT[0:16, :], True, True)
                last.then_inc(rg_full, 1)

            def clear_sums(k):
                pe.wait_ge(zeroed, 2)
                pe.wait_ge(std_ready, k)
                for b in range(4):
                    matmul(psum[:, ACC + b, :], zeros[:], const[:, 0:512], True, True)

            def steps(first_chunk, count, ready):
                u0 = units.n

                def down(c0, t, i):
                    pe.wait_ge(ready, i * 2 + (t + 1))
                    for k in range(2):
                        c = c0 + k
                        pe.wait_ge(rest_sem(c), i * (PASS // 2) + lo_count(c))
                        for o in range(DK):
                            w = slice(o * P, (o + 1) * P)
                            last = three(psum[:, ACC + o // 2, (o % 2) * T:(o % 2 + 1) * T],
                                         wh[:, c % SPLIT, w], wl[:, c % SPLIT, w],
                                         act_h[:, t % 2, k, :], act_l[:, t % 2, k, :], False, k == 1,
                                         skip_group_check=True)
                        last.then_inc(half_done, 1)

                def step(t, i):
                    c0 = 2 * (first_chunk + 2 + 3 * t)
                    for q in range(2):
                        u = u0 + 2 * t + q
                        pe.wait_ge(unit_free, i * UNITS + (u - UNITS + 1))
                        for j in range(2):
                            c = c0 + 2 * q + j
                            pe.wait_ge(rest_sem(c), i * (PASS // 2) + lo_count(c))
                            columns(psum[:, u % UNITS, j * T:(j + 1) * T], c % SPLIT, xg).then_inc(half_done, 1)
                    down(c0 + 4, t, i)

                passes = (count - 1) // 2
                with pe.Fori(0, passes) as i:
                    step(0, i)
                    step(1, i)
                for t in range(2 * passes, count - 1):
                    step(t, 0)
                units.take(2 * (count - 1))
                down(2 * (first_chunk + 3 * count - 1), count - 1, 0)

            clear_sums(5)
            steps(C_MOE, EXPERTS, act_ready)

            pe.wait_ge(mem_split, 2)
            project(C_K2, yg)
            project(C_K2 + 1, yg)
            pe.wait_ge(x_new, 12)
            stats(5)
            project(C_K2 + 2, yg)
            project(C_K2 + 3, yg)
            project_two(C_WIN2, xg, 12)
            stats(6, columns=True)
            for i, u in enumerate(WIN2_ORDER[2:]):
                n = C_WIN2 + 2 + i
                if u in (9, 10):
                    project_rows(n, xg)
                elif u == 2:
                    uu = units.take()
                    free_bank(uu)
                    c = 2 * n
                    wait_split(c)
                    columns(psum[:, uu % UNITS, 0:T], c % SPLIT, xg).then_inc(half_done, 1)
                    wait_split(c + 1)
                    rows(lambda t: psum[:, uu % UNITS, T + t * P:T + (t + 1) * P],
                         (c + 1) % SPLIT, xg).then_inc(half_done, 1)
                else:
                    project(n, xg)

            def level(i):
                pe.wait_ge(level_ready, i + 1)
                for hp in range(2):
                    u = units.take()
                    free_bank(u)
                    for h in range(2):
                        for c in range(2):
                            hd = 2 * hp + h
                            s0 = c * P
                            t0 = (1 - c) * P if i == 8 else c * P
                            kk, qq = (Kc, qh) if i == 0 else ((Kc, Qc), (Kc2, Qc2))[i % 2]
                            last = matmul(psum[:, u % UNITS, (2 * h + c) * P:(2 * h + c + 1) * P],
                                          kk[:, hd, s0:s0 + P], qq[:, hd, t0:t0 + P], True, True)
                    last.then_inc(level_done, 1)

            def head_row(heads, h, width):
                return ident[0:heads, h:h + 1].to_broadcast([heads, width])

            pe.wait_ge(qk_sq, 5)
            pe.wait_ge(std_ready, 7)
            for j in range(5):
                last = matmul(psum[0:10, 4, 0:T], cn("qk_sum", 10 * j, 10), asq2[:, j, :], j == 0, j == 4)
            last.then_inc(qk_sum, 1)
            pe.wait_ge(qk_rstd, 1)
            for j0 in (0, 2, 4):
                u = units.take()
                free_bank(u)
                for j in range(j0, min(j0 + 2, 5)):
                    for half in range(2):
                        last = matmul(psum[64 * half:64 * (half + 1), u % UNITS, (j - j0) * T:(j - j0 + 1) * T],
                                      head_row(10, 2 * j + half, 64), cden[0:10, 1, :], True, True)
                last.then_inc(qk_row, 1)
            for j0 in (0, 2, 4):
                u = units.take()
                free_bank(u)
                pe.wait_ge(unit_free, u - 2)
                for j in range(j0, min(j0 + 2, 5)):
                    last = matmul(psum[:, u % UNITS, (j - j0) * T:(j - j0 + 1) * T], cn("rot"), aqn[:, j, :],
                                  True, True)
                last.then_inc(qk_rot, 1)
            u = units.take()
            free_bank(u)
            pe.wait_ge(roped, 3)
            for j in range(2):
                last = matmul(psum[:, u % UNITS, j * T:(j + 1) * T], cn("dup", 128 * j), aqk[:, 4, :], True, True)
            last.then_inc(dup_done, 1)

            def gqa_scores(h, bank):
                b = 64 * (h % 2)
                for t in range(TT):
                    last = matmul(psum[:, bank, t * T:(t + 1) * T], aqk[b:b + 64, h // 2, t * P:(t + 1) * P],
                                  kdup[b:b + 64, h // 4, :], True, True)
                return last

            def gqa_values(h, pslot, bank):
                b = 64 * (h % 2)
                for m in range(TT):
                    last = matmul(psum[b:b + 64, bank, 0:T], av2[:, m, 64 * (h // 4):64 * (h // 4 + 1)],
                                  probsT[:, pslot, m, :], m == 0, m == 1)
                return last

            pe.wait_ge(unit_free, units.n)
            attention(4, QH, 2, gqa_scores, gqa_values)
            for i in range(9):
                level(i)
                if i % 2:
                    project_rows(C_V2 + i // 2, yg)

            assert units.n == U_REC, units.n
            for hp in range(2):
                u = units.take()
                free_bank(u)
                pe.wait_ge(A_ready, 1)
                for h in range(2):
                    for m in range(TT):
                        last = matmul(psum[:, u % UNITS, h * T:(h + 1) * T],
                                      v2[:, m, (2 * hp + h) * P:(2 * hp + h + 1) * P], AT[:, 2 * hp + h, m, :],
                                      m == 0, m == 1)
                last.then_inc(rec_done, 1)
            pe.wait_ge(rec_sq, 2)
            for h in range(HG):
                last = matmul(psum[0:4, 4, 0:T], cn("hg_sum", 4 * h, 4), sq[:, h, :], h == 0, h == 3)
            last.then_inc(rec_sum, 1)
            pe.wait_ge(rec_rstd, 1)
            for hp in range(2):
                u = units.take()
                free_bank(u)
                for h in range(2):
                    last = matmul(psum[:, u % UNITS, h * T:(h + 1) * T],
                                  head_row(4, 2 * hp + h, P), cden[0:4, 1, :], True, True)
                last.then_inc(rec_row, 1)
            pe.wait_ge(rec_ready, 2)
            assert units.n == U_WO2, units.n
            for m in range(4):
                project(C_WO2 + m, yg)
            stats(7)
            project_two(C_Q2, xg, 16)
            stats(8)
            for m in range(2, 4):
                project(C_Q2 + m, xg)
            pe.wait_ge(unit_free, units.n)
            attention(12, 4, 1, cross_scores, cross_values)
            pe.wait_ge(unit_free, units.n)
            for m in range(4):
                project(C_XO2 + m, yg)
            stats(9)
            project_two(C_FFN, xg, 20)
            stats(10)
            clear_sums(11)
            steps(C_FFN, FSTEPS, fact_ready)
            pe.wait_ge(y_ready, 4)
            stats(11)

        @block.scalar
        def _(act):
            def fn(out, in_, f, **kw):
                return nc.scalar.activation(out, in_, f, **kw)

            act.dma_start(const[:], const_in).then_inc(s_cst, 16)
            act.dma_start(memn[:, 0], memt_in).then_inc(s_mem, 16)
            act.dma_start(memn[:, 1], mem2t_in).then_inc(s_mem2, 16)
            act.dma_start(router[:], router_in).then_inc(s_rt, 16)
            act.dma_start(mask[:], mask_in).then_inc(s_mask, 16)

            def squares(k, src, ready=None, base=0):
                for m in range(4):
                    square_part(k, m, src, ready, base)

            def square_part(k, m, src, ready=None, base=0):
                if k and m == 0:
                    act.wait_ge(stats_done, k)
                if ready is not None:
                    act.wait_ge(ready, base + m + 1)
                fn(sq[:, 2 * m:2 * m + 2, :], src[:, 2 * m:2 * m + 2, :], ACT.Square).then_inc(sq_ready, 1)

            def root(k, columns=False):
                act.wait_ge(stats_done, k + 1)
                if k:
                    act.wait_ge(rstd_ready, k)
                if columns:
                    fn(cols[:, 0, :], psum[:, STAT, T:T + TT], ACT.Sqrt, scale=1.0 / D, bias=eps[:])
                fn(std[:], psum[:, STAT, 0:T], ACT.Sqrt, scale=1.0 / D, bias=eps[:]).then_inc(std_ready, 1)

            def round_high(c, i):
                act.wait_ge(landed[c % RAW], i * PASS_LANDED + 16 * (c // RAW + 1))
                if c >= SPLIT:
                    act.wait_ge(half_done, i * PASS + (c - SPLIT + 1))
                nc.scalar.copy(wh[:, c % SPLIT, :], raw[:, c % RAW, :]).then_inc(hi_ready, 1)

            high = Splitter(round_high, 0, 1)

            def after(n):
                high.upto(2 * n + 1 + SPLIT)

            high.upto(0)
            act.wait_ge(s_x, 16)
            act.wait_ge(zeroed, 1)
            high.upto(SPLIT - 1)
            squares(0, xT)
            after(0)
            root(0)
            after(1)
            act.wait_ge(s_mem, 16)
            squares(1, memn[:, 0])
            root(1)
            after(2)
            act.wait_ge(s_mem2, 16)
            squares(2, memn[:, 1])
            root(2)
            for m in range(2):
                after(C_WIN + 2 + m)
                act.wait_ge(unit_free, 2 + m + 1)
                fn(agate[:, 2 * m:2 * m + 2, :], agate[:, 2 * m:2 * m + 2, :], ACT.Sigmoid).then_inc(agate_sig, 1)

            def gate_sigmoid(m):
                after(C_WIN + 12 + m)
                act.wait_ge(unit_free, 12 + m + 1)
                fn(gates[:, 2 * m:2 * m + 2, :], gates[:, 2 * m:2 * m + 2, :], ACT.Sigmoid).then_inc(gates_sig, 1)

            for n in range(4, 12):
                after(C_WIN + n)
            for m in range(6):
                gate_sigmoid(m)
            for m in range(2):
                act.wait_ge(ln_centered, m + 1)
                fn(asq[:, 2 * m:2 * m + 2, :], aacc[:, 2 * m:2 * m + 2, :], ACT.Square).then_inc(ln_sq, 1)
            for m in range(6, 9):
                gate_sigmoid(m)
            after(C_WIN + 21)
            act.wait_ge(ln_var, 1)
            fn(lnstd, psum[:, 5, 0:T], ACT.Sqrt, scale=1.0 / 512, bias=eps[:]).then_inc(ln_std, 1)
            act.wait_ge(ln_normed, 2)
            for c in range(4):
                fn(actT[:, c, :], aacc[:, c, :], ACT.Silu, scale=sm("ln_g", c), bias=sm("ln_b", c)).then_inc(a_act, 1)
            for m in range(9, 12):
                gate_sigmoid(m)

            def exps(base, heads, scale):
                for h in range(heads):
                    hh = base + h
                    act.wait_ge(neg_ready, hh + 1)
                    if hh >= 4:
                        act.wait_ge(turned, hh - 3)
                    for t in range(TT):
                        last = fn(probs[:, hh % 4, t, :], psum[:, 4 + hh % SB, t * T:(t + 1) * T], ACT.Exp,
                                  scale=scale, bias=negm[:, hh, t:t + 1], accum_out=ssum[:, hh, t:t + 1])
                    last.then_inc(exp_done, 1)

            def split_memory(i, pair):
                act.wait_ge(memn_ready, i + 1)
                for m in range(4):
                    q = slice(2 * m, 2 * m + 2)
                    nc.scalar.copy(pair[:, q, :], memn[:, i, q, :]).then_inc(mem_hi, 1)

            act.wait_ge(half_done, 2 * C_POOL)
            split_memory(0, xh)
            for n in range(C_MERGE, C_Q1):
                after(n)
                if n >= C_WO:
                    square_part(3, n - C_WO, xT, x_new, 0)
            after(C_Q1)
            root(3)
            for n in range(C_Q1 + 1, C_XO1):
                after(n)
            exps(0, 4, 1.0 / 16)
            for n in range(C_XO1, C_MOE):
                after(n)
                square_part(4, n - C_XO1, xT, x_new, 4)
            after(C_MOE)
            root(4)
            split_memory(1, yh)

            def expert_silu(parity, value):
                act.wait_ge(unit_free, value)
                fn(gs[:, parity], gs[:, parity], ACT.Silu).then_inc(silu_done, 1)

            expert_silu(0, U_MOE_FIRST + 1)
            after(C_MOE + 1)
            act.wait_ge(route, 2)
            fn(gexp[:], gsub[:], ACT.Exp).then_inc(route_exp, 1)
            act.wait_ge(route, 17)
            fn(ed[:], dm[:], ACT.Exp).then_inc(route_exp, 1)

            def loop_steps(first_chunk, count, silu):
                def step(t, i):
                    c0 = 2 * (first_chunk + 2 + 3 * t)
                    assert i is not None
                    for c in (c0 + 4, c0 + 5):
                        round_high(c, i)
                    silu(t, i)
                    for c in range(c0 + 6, c0 + 10):
                        round_high(c, i)

                passes = (count - 1) // 2
                last = 2 * (first_chunk + 2 + 3 * (count - 1)) + 3
                assert high.next == 2 * (first_chunk + 2) + 4, (high.next, first_chunk)
                whole = passes if last < HALVES else passes - 1
                with act.Fori(0, whole) as i:
                    step(0, i)
                    step(1, i)
                high.skip_to(2 * (first_chunk + 2) + 4 + PASS * whole)
                for t in range(2 * whole, count - 1):
                    c0 = 2 * (first_chunk + 2 + 3 * t)
                    high.upto(c0 + 5)
                    silu(t, 0)
                    high.upto(c0 + 9)

            loop_steps(C_MOE, EXPERTS, lambda t, i: expert_silu((t + 1) % 2, i * 4 + (U_MOE + 2 * t + 1)))

            squares(5, xT, x_new, 8)
            after(C_K2)
            after(C_K2 + 1)
            root(5)
            act.wait_ge(lb_steps, 3)
            fn(lbt[:, 3:5, :], lbt[:, 1:3, :], ACT.Exp).then_inc(lb_exp, 1)
            squares(6, xT, x_new, 12)
            after(C_K2 + 2)
            after(C_K2 + 3)
            after(C_WIN2)
            root(6, columns=True)
            for m in range(2):
                after(C_WIN2 + m)
                act.wait_ge(unit_free, U_WIN2 + m + 1)
                fn(qh[:, 2 * m:2 * m + 2, :], qh[:, 2 * m:2 * m + 2, :], ACT.Silu).then_inc(hq_act, 1)
            for m in range(4):
                after(C_WIN2 + 2 + m)
                act.wait_ge(unit_free, U_WIN2 + 2 + m + 1)
                f, k = ((ff, kf), (fb, kb))[m // 2]
                h = slice(2 * (m % 2), 2 * (m % 2) + 2)
                fn(k[:, h, :], f[:, h, :], ACT.Sigmoid, scale=-1.0)
                fn(f[:, h, :], f[:, h, :], ACT.Sigmoid).then_inc(f_sig, 1)
            for m in range(2):
                after(C_WIN2 + 6 + m)
                after(C_WIN2 + 8 + m)
                act.wait_ge(unit_free, U_WIN2 + 8 + m + 1)
                fn(hgate[:, 2 * m:2 * m + 2, :], hgate[:, 2 * m:2 * m + 2, :], ACT.Silu).then_inc(hg_act, 1)
            act.wait_ge(stats_done, 7)
            for j in range(5):
                after(C_WIN2 + 10 + j // 2)
                act.wait_ge(unit_free, U_WIN2 + 10 + j // 2 + 1)
                fn(asq2[:, j, :], aqk[:, j, :], ACT.Square).then_inc(qk_sq, 1)
            act.wait_ge(qk_sum, 1)
            fn(cden[0:10, 0, :], psum[0:10, 4, 0:T], ACT.Sqrt, scale=1.0 / 64, bias=eps[0:10, :]).then_inc(qk_std, 1)
            exps(4, QH, 1.0 / 8)
            for n in range(C_V2, C_WO2):
                after(n)
            for hp in range(2):
                act.wait_ge(unit_free, U_REC + hp + 1)
                fn(sq[:, 2 * hp:2 * hp + 2, :], mix2[:, 4 + 2 * hp:6 + 2 * hp, :], ACT.Square).then_inc(rec_sq, 1)
            act.wait_ge(rec_sum, 1)
            fn(cden[0:4, 0, :], psum[0:4, 4, 0:T], ACT.Sqrt, scale=1.0 / 128, bias=eps[0:4, :]).then_inc(rec_std, 1)
            for m in range(4):
                after(C_WO2 + m)
                square_part(7, m, yT, unit_free, U_WO2)
            root(7)
            squares(8, xT, x_new, 16)
            after(C_Q2)
            root(8)
            for m in range(1, 4):
                after(C_Q2 + m)
            exps(12, 4, 1.0 / 16)
            for m in range(4):
                after(C_XO2 + m)
                square_part(9, m, yT, unit_free, U_XO2)
            root(9)
            squares(10, xT, x_new, 20)
            after(C_FFN)
            root(10)

            def ffn_silu(parity, value):
                act.wait_ge(fconv_steps, value)
                fn(fconv[:, parity, 0:2, :], fconv[:, parity, 0:2, :], ACT.Silu).then_inc(fsilu, 1)

            ffn_silu(0, 6)
            after(C_FFN + 1)
            loop_steps(C_FFN, FSTEPS, lambda t, i: ffn_silu((t + 1) % 2, i * 24 + (12 * (t + 1) + 6)))
            squares(11, yF, y_ready, 0)
            root(11)

        @block.gpsimd
        def _(pool):
            nc.gpsimd.memset(apad[:, :, 0:CONV_K - 1], 0.0)
            nc.gpsimd.memset(upad[:, :, 0:PADW], 0.0)
            nc.gpsimd.memset(cpad[:, :, 0:C_K - 1], 0.0).then_inc(pads_zero, 1)
            pool.wait_ge(pads_zero, 1)
            n = [0]

            def subtract(c, i):
                pool.wait_ge(hi_ready, i * PASS + hi_count(c))
                nc.gpsimd.tensor_tensor(wl[:, c % SPLIT, :], raw[:, c % RAW, :], f32(wh[:, c % SPLIT, :]),
                                        ALU.subtract).then_inc(lo_pool, 1)

            rest = Splitter(subtract, 0, 2)

            def step(ins):
                ins.then_inc(pool_steps, 1)
                n[0] += 1
                rest.upto(rest.next)
                pool.wait_ge(pool_steps, n[0])

            add = lambda o, a, b: nc.gpsimd.tensor_tensor(o, a, b, ALU.add)
            rest.upto(14)
            pool.wait_ge(unit_free, 6)
            W = T + PADW
            step(add(ubuf[:, :, 1:W], upad[:, :, 1:W], upad[:, :, 0:W - 1]))
            pool.wait_ge(stats_done, 3)
            buf = sq.rearrange("p k t -> p (k t)")[:, 0:4 * W].rearrange("p (a b) -> p a b", a=4)
            step(add(buf[:, 1:4, 4:W], ubuf[:, 1:4, 4:W], ubuf[:, 1:4, 2:W - 2]))
            step(add(ubuf[:, 2:4, 8:W], buf[:, 2:4, 8:W], buf[:, 2:4, 4:W - 4]))
            step(add(buf[:, 3:4, 16:W], ubuf[:, 3:4, 16:W], ubuf[:, 3:4, 8:W - 8]))
            pool.wait_ge(s_cst, 16)
            for i, src in enumerate((ubuf, buf, ubuf, buf)):
                w = POOL_W[i]
                nc.gpsimd.tensor_tensor(pT[:, i, 0:PADW], src[:, i, PADW:2 * PADW], cn("rcnt", PADW * i, PADW), ALU.mult)
                step(nc.gpsimd.tensor_scalar(pT[:, i, PADW:T], src[:, i, 2 * PADW:W], 1.0 / w, None, ALU.mult))
            nc.gpsimd.tensor_tensor(pT[:], pT[:], upad[:, :, PADW:W], ALU.subtract).then_inc(p_ready, 1)
            rest.upto(26)
            pool.wait_ge(unit_free, 12)
            pool.wait_ge(s_small, 16)
            step(nc.gpsimd.tensor_tensor(cpad[:, :, C_K - 1:C_K - 1 + T], cc[:], cx[:], ALU.mult))
            for j in range(C_K):
                for c in range(4):
                    dst = cy if j == 0 else ctmp
                    last = nc.gpsimd.tensor_scalar(dst[:, c, :], cpad[:, c, j:j + T], sm("c_w", 4 * j + c), None, ALU.mult)
                step(last)
                if j:
                    step(nc.gpsimd.tensor_tensor(cy[:], cy[:], ctmp[:], ALU.add))
            nc.gpsimd.tensor_tensor(cy[:], cy[:], cb[:], ALU.mult).then_inc(c_ready, 1)
            rest.upto(WHOLE1 - 1)
            first = rest.next
            passes = (HALVES - first) // PASS
            with pool.Fori(0, passes) as i:
                for c in range(first, first + PASS, 2):
                    subtract(c, i)
            for c in range(first + passes * PASS, HALVES, 2):
                subtract(c, 0)

        @block.vector
        def _(dve):
            units = UnitCount()
            v = nc.vector
            upd = [0]
            links = [0]

            def link(ins):
                ins.then_inc(chain, 1)
                links[0] += 1
                dve.wait_ge(chain, links[0])

            def tt(out, a, b, op):
                return v.tensor_tensor(out, a, b, op)

            def subtract(c, i):
                dve.wait_ge(hi_ready, i * PASS + hi_count(c))
                tt(wl[:, c % SPLIT, :], raw[:, c % RAW, :], f32(wh[:, c % SPLIT, :]), ALU.subtract).then_inc(lo_dve, 1)

            rest = Splitter(subtract, 1, 2)

            def full(n):
                rest.upto(2 * n + 3)
                dve.wait_ge(half_done, 2 * n + 2)

            def after(n):
                rest.upto(2 * n + 1 + SPLIT)

            def evac_scaled(n, out, k):
                full(n)
                u = units.take()
                tt(out, unit_view(u), two(rstd[:, k % 4, :]), ALU.mult).then_inc(unit_free, 1)
                after(n)

            def recip(k):
                dve.wait_ge(std_ready, k + 1)
                v.reciprocal(rstd[:, k % 4, :], std[:]).then_inc(rstd_ready, 1)

            def gain(name, m, also=None):
                for k in (2 * m, 2 * m + 1):
                    last = v.tensor_scalar(xh[:, k, :], xT[:, k, :], sm(name, k), None, ALU.mult)
                    if k == 2 * m and also is not None:
                        last.then_inc(also, 1)
                link(last)
                for k in (2 * m, 2 * m + 1):
                    last = v.scalar_tensor_tensor(xl[:, k, :], xT[:, k, :], sm(name, k), f32(xh[:, k, :]),
                                                  ALU.mult, ALU.subtract)
                last.then_inc(xg_ready, 1)

            def split(m, src, h, l, done, n):
                q = slice(2 * m, 2 * m + 2)
                v.tensor_copy(h[:, q, :], src).then_inc(done, 1)
                dve.wait_ge(done, n)
                return tt(l[:, q, :], src, f32(h[:, q, :]), ALU.subtract)

            def residual(chunk, name):
                for m in range(4):
                    full(chunk + m)
                    u = units.take()
                    upd[0] += 1
                    q = xT[:, 2 * m:2 * m + 2, :]
                    tt(q, unit_view(u), q, ALU.add).then_inc(x_new, 1)
                    dve.wait_ge(x_new, upd[0])
                    gain(name, m, unit_free)
                    after(chunk + m)

            v.memset(eps[:], EPS).then_inc(zeroed, 1)
            v.memset(zeros[:], 0.0).then_inc(zeroed, 1)
            dve.wait_ge(s_x, 16)
            dve.wait_ge(s_small, 16)
            for m in range(4):
                gain("mix_g", m)
                if m < 2:
                    rest.upto(2 * m + 1)
            after(0)
            recip(0)
            dve.wait_ge(rstd_ready, 1)
            dve.wait_ge(pads_zero, 1)
            for m in range(2):
                evac_scaled(C_WIN + m, aval[:, 2 * m:2 * m + 2, :], 0)

            def normalise_memory(i, name):
                dve.wait_ge(rstd_ready, 2 + i)
                dve.wait_ge(stats_done, 2 + i)
                for k in range(DK):
                    last = v.scalar_tensor_tensor(memn[:, i, k, :], memn[:, i, k, :], sm(name, k),
                                                  rstd[:, 1 + i, :], ALU.mult, ALU.mult)
                last.then_inc(memn_ready, 1)

            for m in range(2):
                evac_scaled(C_WIN + 2 + m, agate[:, 2 * m:2 * m + 2, :], 0)
                recip(1 + m)
            for m in range(2):
                dve.wait_ge(agate_sig, m + 1)
                h = slice(2 * m, 2 * m + 2)
                tt(apad[:, h, CONV_K - 1:], aval[:, h, :], agate[:, h, :], ALU.mult).then_inc(a_glu, 1)
            dve.wait_ge(a_glu, 2)
            done = [0]

            def convolve(taps):
                for j in taps:
                    for c in range(4):
                        x = apad[:, c, j:j + T]
                        if j == 0:
                            ins = v.tensor_scalar(aacc[:, c, :], x, sm("conv_w", c), sm("conv_b", c), ALU.mult, ALU.add)
                        else:
                            dve.wait_ge(conv_a, done[0] - 3)
                            ins = v.scalar_tensor_tensor(aacc[:, c, :], x, sm("conv_w", 4 * j + c), aacc[:, c, :],
                                                         ALU.mult, ALU.add)
                        ins.then_inc(conv_a, 1)
                        done[0] += 1

            dst = {4: upad[:, 0:2, PADW:], 5: upad[:, 2:4, PADW:], 6: cx[:, 0:2, :], 7: cx[:, 2:4, :],
                   8: cb[:, 0:2, :], 9: cb[:, 2:4, :], 10: cc[:, 0:2, :], 11: cc[:, 2:4, :]}
            dst.update((12 + m, gates[:, 2 * m:2 * m + 2, :]) for m in range(12))
            for n in range(4, 17):
                evac_scaled(C_WIN + n, dst[n], 0)
                convolve(range((n - 4) * CONV_K // 13, (n - 3) * CONV_K // 13))
            evac_scaled(C_WIN + 17, dst[17], 0)
            dve.wait_ge(ln_mean, 1)
            for m in range(2):
                h = slice(2 * m, 2 * m + 2)
                v.scalar_tensor_tensor(aacc[:, h, :], two(psum[:, 6, 0:T]), -1.0 / 512, aacc[:, h, :],
                                       ALU.mult, ALU.add).then_inc(ln_centered, 1)
            normalise_memory(0, "mem_g")
            for n in range(18, 21):
                evac_scaled(C_WIN + n, dst[n], 0)
            dve.wait_ge(ln_std, 1)
            link(v.reciprocal(lnrstd, lnstd))
            for m in range(2):
                h = slice(2 * m, 2 * m + 2)
                tt(aacc[:, h, :], aacc[:, h, :], two(lnrstd), ALU.mult).then_inc(ln_normed, 1)
            for n in range(21, 24):
                evac_scaled(C_WIN + n, dst[n], 0)
            def split_memory(i, h, l):
                for m in range(4):
                    q = slice(2 * m, 2 * m + 2)
                    dve.wait_ge(mem_hi, 4 * i + m + 1)
                    last = tt(l[:, q, :], memn[:, i, q, :], f32(h[:, q, :]), ALU.subtract)
                last.then_inc(mem_split, 1)

            split_memory(0, xh, xl)
            dve.wait_ge(gates_sig, 12)
            for m in range(4):
                if m < 3:
                    dve.wait_ge(pool_full, m + 1)
                else:
                    full(C_POOL)
                u = units.take()
                for j in range(2):
                    last = v.scalar_tensor_tensor(merged[:, 2 * m + j, :], psum[:, u % UNITS, j * T:(j + 1) * T],
                                                  sm("pool_s", 2 * m + j), gates[:, 8 + 2 * m + j, :],
                                                  ALU.mult, ALU.mult)
                last.then_inc(unit_free, 1)
            for m in range(4):
                full(C_MERGE + m)
                ua, uc = units.take(), units.take()
                q = slice(2 * m, 2 * m + 2)
                b = slice(2 * (m % 2), 2 * (m % 2) + 2)
                tt(mt1[:, b, :], unit_view(ua), gates[:, 2 * m:2 * m + 2, :], ALU.mult).then_inc(unit_free, 1)
                tt(mt2[:, b, :], unit_view(uc), gates[:, 16 + 2 * m:18 + 2 * m, :], ALU.mult).then_inc(unit_free, 1)
                dve.wait_ge(unit_free, uc + 1)
                link(tt(mt1[:, b, :], mt1[:, b, :], mt2[:, b, :], ALU.add))
                link(tt(merged[:, q, :], mt1[:, b, :], merged[:, q, :], ALU.add))
                after(C_MERGE + m)
            for m in range(4):
                q = slice(2 * m, 2 * m + 2)
                v.tensor_copy(yh[:, q, :], merged[:, q, :]).then_inc(chain, 1)
                links[0] += 1
                dve.wait_ge(chain, links[0])
                tt(yl[:, q, :], merged[:, q, :], f32(yh[:, q, :]), ALU.subtract).then_inc(merged_ready, 1)
            normalise_memory(1, "mem2_g")

            def copy_units(chunk, dst_of):
                for m in range(4):
                    full(chunk + m)
                    u = units.take()
                    v.tensor_copy(dst_of(m), unit_view(u)).then_inc(unit_free, 1)
                    after(chunk + m)

            k_dst = lambda m: kT[:, 2 * m:2 * m + 2, :]
            v_dst = lambda m: vm[:, :, 256 * m:256 * (m + 1)]
            copy_units(C_K1, k_dst)
            copy_units(C_V1, v_dst)
            residual(C_WO, "x_g")
            after(C_Q1)
            recip(3)
            dve.wait_ge(rstd_ready, 4)
            for m in range(4):
                evac_scaled(C_Q1 + m, qT[:, 2 * m:2 * m + 2, :], 3)

            def attention(base, heads, group, scale, take_out):
                def row_max(h):
                    hh = base + h
                    dve.wait_ge(scores_done, hh + 1)
                    s = psum[:, 4 + hh % SB, :].rearrange("p (t m) -> p t m", t=TT)
                    v.tensor_reduce(nmax[:, hh, :], s, AX_X, ALU.max).then_inc(maxed, 1)
                    dve.wait_ge(maxed, hh + 1)
                    v.tensor_scalar(negm[:, hh, :], nmax[:, hh, :], -scale, None, ALU.mult).then_inc(neg_ready, 1)

                def normalise(h):
                    hh = base + h
                    dve.wait_ge(exp_done, hh + 1)
                    v.reciprocal(rsum[:, hh, :], ssum[:, hh, :]).then_inc(rsum_ready, 1)
                    dve.wait_ge(rsum_ready, hh + 1)
                    for t in range(TT):
                        last = v.tensor_scalar(probs[:, hh % 4, t, :], probs[:, hh % 4, t, :], rsum[:, hh, t:t + 1],
                                               None, ALU.mult)
                    last.then_inc(probs_ready, 1)

                for h in range(SB):
                    row_max(h)
                normalise(0)
                for g in range(0, heads, group):
                    for h in range(g, g + group):
                        hh = base + h
                        dve.wait_ge(turned, hh + 1)
                        if hh >= 3:
                            dve.wait_ge(o_done, hh - 2)
                        u = units.take()
                        v.tensor_copy(probsT[:, hh % 3], unit_view(u)).then_inc(unit_free, 1)
                        if h + SB < heads:
                            row_max(h + SB)
                        if h + 1 < heads:
                            normalise(h + 1)
                    dve.wait_ge(o_done, base + g + group)
                    u = units.take()
                    take_out(g, u).then_inc(unit_free, 1)

            def cross_out(h, u):
                q = slice(2 * h, 2 * h + 2)
                link(v.tensor_copy(yh[:, q, :], unit_view(u)))
                return tt(yl[:, q, :], unit_view(u), f32(yh[:, q, :]), ALU.subtract)

            attention(0, 4, 1, 1.0 / 16, cross_out)
            residual(C_XO1, "ffn_g")
            after(C_MOE)
            recip(4)
            split_memory(1, yh, yl)
            dve.wait_ge(rstd_ready, 5)
            dve.wait_ge(logits_done, 1)
            tt(logitT[0:20, :], psum[0:20, 6, 0:T], rstd[0:20, 0, :], ALU.mult).then_inc(route, 1)
            dve.wait_ge(route, 1)
            v.tensor_scalar(logitT[0:20, :], logitT[0:20, :], sm("r_b")[0:20, :], None, ALU.add).then_inc(logits_ready, 1)
            full(C_MOE)
            ug = units.take()
            assert ug == U_MOE_FIRST, (ug, U_MOE_FIRST)
            tt(gs[:, 0], unit_view(ug), two(rstd[:, 0, :]), ALU.mult).then_inc(unit_free, 1)
            full(C_MOE + 1)
            uu = units.take()
            tt(us[:, 0], unit_view(uu), two(rstd[:, 0, :]), ALU.mult).then_inc(unit_free, 1)
            after(C_MOE + 1)

            rn = [1]

            def step(ins):
                ins.then_inc(route, 1)
                rn[0] += 1
                dve.wait_ge(route, rn[0])

            b4 = lambda ap: ap.to_broadcast([P, TT, 4])
            prio = cn("prio", 0, 8).rearrange("p (a b) -> p a b", a=TT)
            dve.wait_ge(ltok_done, 1)
            link(v.tensor_copy(lt[:], psum[:, 5, 0:40].rearrange("p (t n) -> p t n", t=TT)))
            link(v.tensor_reduce(gmx[:], lt[:, :, 0:4], AX_X, ALU.max))
            step(tt(gsub[:], lt[:, :, 0:4], b4(gmx[:]), ALU.subtract))
            step(tt(eqp[:], lt[:, :, 0:4], b4(gmx[:]), ALU.is_equal))
            step(tt(eqp[:], eqp[:], prio, ALU.mult))
            step(v.tensor_reduce(eqm[:], eqp[:], AX_X, ALU.max))
            step(tt(ohg[:], eqp[:], b4(eqm[:]), ALU.is_equal))
            for t in range(TT):
                last = tt(lprod[:, t, :].rearrange("p (g e) -> p g e", g=4),
                          lt[:, t, 4:20].rearrange("p (g e) -> p g e", g=4),
                          ohg[:, t, :].unsqueeze(2).to_broadcast([P, 4, 4]), ALU.mult)
            step(last)
            for t in range(TT):
                last = v.tensor_reduce(lsel[:, t, :], lprod[:, t, :].rearrange("p (g e) -> p e g", g=4), AX_X, ALU.add)
            step(last)
            step(v.tensor_reduce(m1[:], lsel[:], AX_X, ALU.max))
            step(tt(eqp[:], lsel[:], b4(m1[:]), ALU.is_equal))
            step(tt(eqp[:], eqp[:], prio, ALU.mult))
            step(v.tensor_reduce(eqm[:], eqp[:], AX_X, ALU.max))
            step(tt(oh1[:], eqp[:], b4(eqm[:]), ALU.is_equal))
            step(v.tensor_scalar(lsel2[:], oh1[:], NEG, None, ALU.mult))
            step(tt(lsel2[:], lsel2[:], lsel[:], ALU.add))
            step(v.tensor_reduce(m2[:], lsel2[:], AX_X, ALU.max))
            step(tt(dm[:], m2[:], m1[:], ALU.subtract))
            step(tt(eqp[:], lsel2[:], b4(m2[:]), ALU.is_equal))
            step(tt(eqp[:], eqp[:], prio, ALU.mult))
            step(v.tensor_reduce(eqm[:], eqp[:], AX_X, ALU.max))
            step(tt(oh2[:], eqp[:], b4(eqm[:]), ALU.is_equal))
            dve.wait_ge(route_exp, 1)
            step(v.tensor_reduce(gsm[:], gexp[:], AX_X, ALU.add))
            step(v.reciprocal(gval[:], gsm[:]))
            dve.wait_ge(route_exp, 2)
            step(v.tensor_scalar(den[:], ed[:], 1.0, None, ALU.add))
            step(v.reciprocal(den[:], den[:]))
            step(tt(w1[:], gval[:], den[:], ALU.mult))
            step(tt(w2[:], w1[:], ed[:], ALU.mult))
            step(tt(g4a[:], oh1[:], b4(w1[:]), ALU.mult))
            step(tt(g4b[:], oh2[:], b4(w2[:]), ALU.mult))
            step(tt(g4a[:], g4a[:], g4b[:], ALU.add))
            for t in range(TT):
                last = tt(gate16[:, t, :].rearrange("p (g e) -> p g e", g=4),
                          ohg[:, t, :].unsqueeze(2).to_broadcast([P, 4, 4]),
                          g4a[:, t, :].unsqueeze(1).to_broadcast([P, 4, 4]), ALU.mult)
            last.then_inc(gate16_ready, 1)
            dve.wait_ge(gateT_done, 1)
            v.tensor_copy(gateT[0:16, :], psum[0:16, 6, 0:T]).then_inc(gateT_ready, 1)
            for e in range(0, EXPERTS, 2):
                dve.wait_ge(rg_full, e // 2 + 1)
                u = units.take()
                if e == 0:
                    link(tt(us[:, 0], us[:, 0], two(psum[:, u % UNITS, 0:T]), ALU.mult))
                tt(rg[:, e:e + 2, :], unit_view(u), two(rstd[:, 0, :]), ALU.mult).then_inc(unit_free, 1)
            dve.wait_ge(silu_done, 1)
            dve.wait_ge(unit_free, units.n)
            def hidden(b, gate, up, ready):
                link_free(tt(up, gate, up, ALU.mult))
                link_free(v.tensor_copy(act_h[:, b], up))
                tt(act_l[:, b], up, f32(act_h[:, b]), ALU.subtract).then_inc(ready, 1)

            in_loop = [0, 0, 0]

            def link_free(ins):
                ins.then_inc(loop_chain, 1)
                in_loop[0] += 1
                dve.wait_ge(loop_chain, in_loop[1] + in_loop[0])

            hidden(0, gs[:, 0], us[:, 0], act_ready)

            assert units.n == U_MOE, (units.n, U_MOE)

            def expert(t, i):
                c0 = 2 * (C_MOE + 2 + 3 * t)
                u = U_MOE + 2 * t
                b = (t + 1) % 2
                dve.wait_ge(half_done, i * PASS + (c0 + 2))
                tt(gs[:, b], unit_view(u), two(rstd[:, 0, :]), ALU.mult).then_inc(unit_free, 1)
                subtract(c0 + 5, i)
                dve.wait_ge(half_done, i * PASS + (c0 + 4))
                weight = rg[:, t + 1, :] if isinstance(i, int) else work[:, bass.ds(i * (2 * T) + (t + 1) * T, T)]
                tt(us[:, b], unit_view(u + 1), two(weight), ALU.mult).then_inc(unit_free, 1)
                subtract(c0 + 7, i)
                dve.wait_ge(unit_free, i * 4 + (u + 2))
                dve.wait_ge(silu_done, i * 2 + (t + 2))
                hidden(b, gs[:, b], us[:, b], act_ready)
                subtract(c0 + 9, i)

            def loop_steps(first_chunk, count, one):
                passes = (count - 1) // 2
                assert rest.next == 2 * (first_chunk + 2) + 5, (rest.next, first_chunk)
                last = 2 * (first_chunk + 2 + 3 * (count - 1)) + 3
                whole = passes if last < HALVES else passes - 1
                before = in_loop[0]
                with dve.Fori(0, whole) as i:
                    in_loop[1] = i * 4
                    one(0, i)
                    one(1, i)
                in_loop[0], in_loop[1] = before + 4 * whole, 0
                rest.skip_to(2 * (first_chunk + 2) + 5 + PASS * whole)
                return whole

            whole = loop_steps(C_MOE, EXPERTS, expert)
            for t in range(2 * whole, EXPERTS - 1):
                expert(t, 0)
            rest.skip_to(2 * (C_MOE + 3 * EXPERTS) + 3)
            units.take(30)
            dve.wait_ge(half_done, 2 * (C_MOE + 3 * EXPERTS))
            for m in range(4):
                q = xT[:, 2 * m:2 * m + 2, :]
                tt(q, psum[:, ACC + m, :].rearrange("p (j t) -> p j t", j=2), q, ALU.add).then_inc(x_new, 1)

            upd[0] += 4
            l0, l1 = sm("lb", 0, 8), sm("lb", 8, 8)
            tt(lbt[:, 0, :], l0, l1, ALU.max).then_inc(lb_steps, 1)
            dve.wait_ge(lb_steps, 1)
            tt(lbt[:, 1, :], l0, lbt[:, 0, :], ALU.subtract).then_inc(lb_steps, 1)
            tt(lbt[:, 2, :], l1, lbt[:, 0, :], ALU.subtract).then_inc(lb_steps, 1)

            def copy_unit(n, dst):
                full(n)
                u = units.take()
                v.tensor_copy(dst, unit_view(u)).then_inc(unit_free, 1)
                after(n)

            copy_unit(C_K2, k_dst(0))
            dve.wait_ge(lb_exp, 1)
            link(tt(lbt[:, 5, :], lbt[:, 3, :], lbt[:, 4, :], ALU.add))
            link(v.reciprocal(lbt[:, 5, :], lbt[:, 5, :]))
            tt(lbt[:, 6, :], lbt[:, 3, :], lbt[:, 5, :], ALU.mult)
            link(tt(lbt[:, 7, :], lbt[:, 4, :], lbt[:, 5, :], ALU.mult))
            copy_unit(C_K2 + 1, k_dst(1))

            recip(5)
            dve.wait_ge(rstd_ready, 6)
            for m in range(4):
                for k in (2 * m, 2 * m + 1):
                    last = v.scalar_tensor_tensor(xT[:, k, :], xT[:, k, :], sm("f_g", k), rstd[:, 1, :],
                                                  ALU.mult, ALU.mult)
                last.then_inc(x_new, 1)
                upd[0] += 1
                dve.wait_ge(x_new, upd[0])
                gain("pre_mix_g", m)
            copy_unit(C_K2 + 2, k_dst(2))
            copy_unit(C_K2 + 3, k_dst(3))
            after(C_WIN2)
            recip(6)
            dve.wait_ge(std_ready, 7)
            v.reciprocal(cols[:, 1, :], cols[:, 0, :]).then_inc(rcol_ready, 1)
            dve.wait_ge(rstd_ready, 7)
            dve.wait_ge(rcol_ready, 1)

            assert units.n == U_WIN2, (units.n, U_WIN2)

            def forget(m):
                f, k = ((ff, kf), (fb, kb))[m // 2]
                dve.wait_ge(f_sig, m + 1)
                for h in (2 * (m % 2), 2 * (m % 2) + 1):
                    c = 4 * (m // 2) + h
                    v.tensor_scalar(f[:, h, :], f[:, h, :], lbt[:, 7, c:c + 1], lbt[:, 6, c:c + 1], ALU.mult, ALU.add)
                    last = v.tensor_scalar(k[:, h, :], k[:, h, :], lbt[:, 7, c:c + 1], None, ALU.mult)
                link(last)

            def take_rows(n, dst):
                full(n)
                u = units.take()
                for t in range(TT):
                    last = v.tensor_scalar(dst[:, t, :], psum[:, u % UNITS, t * 256:(t + 1) * 256],
                                           cols[:, 1, t:t + 1], None, ALU.mult)
                last.then_inc(unit_free, 1)
                after(n)

            for m in range(2):
                evac_scaled(C_WIN2 + m, qh[:, 2 * m:2 * m + 2, :], 6)
            for m in range(4):
                f = (ff, fb)[m // 2]
                evac_scaled(C_WIN2 + 2 + m, f[:, 2 * (m % 2):2 * (m % 2) + 2, :], 6)
            take_rows(C_WIN2 + 6, v2[:, :, 0:256])
            forget(0)
            forget(1)
            take_rows(C_WIN2 + 7, v2[:, :, 256:512])
            forget(2)
            forget(3)
            for m in range(2):
                evac_scaled(C_WIN2 + 8 + m, hgate[:, 2 * m:2 * m + 2, :], 6)
            for m in range(2):
                evac_scaled(C_WIN2 + 10 + m, aqk[:, 2 * m:2 * m + 2, :], 6)
            full(C_WIN2 + 12)
            u = units.take()
            tt(aqk[:, 4, :], psum[:, u % UNITS, 0:T], rstd[:, 2, :], ALU.mult)
            for t in range(TT):
                last = v.tensor_scalar(av2[:, t, :], psum[:, u % UNITS, T + t * P:T + (t + 1) * P],
                                       cols[:, 1, t:t + 1], None, ALU.mult)
            last.then_inc(unit_free, 1)
            after(C_WIN2 + 12)

            def sides(x, h):
                y = x.rearrange("p g t -> p (g t)").rearrange("p (b s i) -> p b s i", s=2, i=h)
                return y[:, :, 0, :], y[:, :, 1, :]

            def prepare(i):
                if i == 0:
                    tt(Kc[:], kf[:], kb[:], ALU.add).then_inc(level_ready, 1)
                    v.memset(Lf[:], 1.0)
                    link(v.memset(Lb[:], 1.0))
                    return
                h = 2 ** (i - 1)
                kk, qq = ((Kc, Qc), (Kc2, Qc2))[i % 2]
                if i >= 2:
                    dve.wait_ge(level_done, 2 * (i - 1))
                (kl, kr), (ql, qr) = sides(kk, h), sides(qq, h)
                (fl, fr), (bl, br) = sides(ff, h), sides(fb, h)
                (lfl, lfr), (lbl, lbr) = sides(Lf, h), sides(Lb, h)
                tt(kl, sides(kf, h)[0], lfl, ALU.mult)
                tt(kr, sides(kb, h)[1], lbr, ALU.mult)
                tt(qr, sides(qh, h)[1], fr, ALU.mult)
                tt(ql, sides(qh, h)[0], bl, ALU.mult).then_inc(level_ready, 1)
                if i == 8:
                    return
                wide = [P, 4 * T // (2 * h), h]
                dve.wait_ge(level_ready, i + 1)
                tt(lfl, lfl, fr[:, :, h - 1:h].to_broadcast(wide), ALU.mult)
                link(tt(lbr, lbr, bl[:, :, 0:1].to_broadcast(wide), ALU.mult))
                tt(fr, fr, fl[:, :, h - 1:h].to_broadcast(wide), ALU.mult)
                link(tt(bl, bl, br[:, :, 0:1].to_broadcast(wide), ALU.mult))

            def collect(i):
                for hp in range(2):
                    dve.wait_ge(level_done, 2 * i + hp + 1)
                    u = units.take()
                    got = psum[:, u % UNITS, :].rearrange("p (h c t) -> p h c t", h=2, c=2)
                    at = hp * 4 * T
                    step_c, at = (P, at + P) if i == 8 else (T + P, at)
                    base = AT_flat[:, at:at + 1]
                    dst = bass.AP(base.tensor, base.offset, [base.ap[0], [2 * T, 2], [step_c, 2], [1, P]])
                    wide = [P, 2, 2, P]
                    if i == 0:
                        ins = tt(dst, got, ident.unsqueeze(1).unsqueeze(1).to_broadcast(wide), ALU.mult)
                    elif i < 8:
                        ins = v.copy_predicated(dst, mask[:, i - 1, :].unsqueeze(1).unsqueeze(1).to_broadcast(wide), got)
                    else:
                        ins = v.tensor_copy(dst, got)
                    ins.then_inc(unit_free, 1)

            dve.wait_ge(qk_std, 1)
            v.reciprocal(cden[0:10, 1, :], cden[0:10, 0, :]).then_inc(qk_rstd, 1)
            for n, j0 in enumerate((0, 2, 4)):
                w = min(2, 5 - j0)
                dve.wait_ge(qk_row, n + 1)
                u = units.take()
                row = psum[:, u % UNITS, 0:w * T].rearrange("p (a t) -> p a t", a=w)
                v.scalar_tensor_tensor(aqn[:, j0:j0 + w, :], row, sm("q_g" if j0 < 4 else "k_g"), aqk[:, j0:j0 + w, :],
                                       ALU.mult, ALU.mult).then_inc(unit_free, 1)
            for n, j0 in enumerate((0, 2, 4)):
                w = min(2, 5 - j0)
                cos, sin = (cn(x, 0, T).unsqueeze(1).to_broadcast([P, w, T]) for x in ("cos", "sin"))
                dve.wait_ge(qk_rot, n + 1)
                u = units.take()
                row = psum[:, u % UNITS, 0:w * T].rearrange("p (a t) -> p a t", a=w)
                if n:
                    dve.wait_ge(roped, n)
                tt(rtmp[:, 0:w, :], row, sin, ALU.mult).then_inc(unit_free, 1)
                link(tt(aqk[:, j0:j0 + w, :], aqn[:, j0:j0 + w, :], cos, ALU.mult))
                dve.wait_ge(unit_free, u + 1)
                tt(aqk[:, j0:j0 + w, :], aqk[:, j0:j0 + w, :], rtmp[:, 0:w, :], ALU.add).then_inc(roped, 1)
            dve.wait_ge(dup_done, 1)
            u = units.take()
            v.tensor_copy(kdup[:], unit_view(u)).then_inc(unit_free, 1)

            def gqa_out(g, u):
                return v.tensor_copy(mix2[:, g // 2, :], psum[:, u % UNITS, 0:T])

            attention(4, QH, 2, 1.0 / 8, gqa_out)

            dve.wait_ge(s_mask, 16)
            prepare(0)
            for i in range(9):
                if i + 1 < 9:
                    prepare(i + 1)
                collect(i)
                if i % 2:
                    copy_unit(C_V2 + i // 2, v_dst(i // 2))
                dve.wait_ge(unit_free, units.n)
            v.nop().then_inc(A_ready, 1)
            for m in range(2):
                q = slice(2 * m, 2 * m + 2)
                link(v.tensor_copy(yh[:, q, :], mix2[:, q, :]))
                tt(yl[:, q, :], mix2[:, q, :], f32(yh[:, q, :]), ALU.subtract)
            dve.wait_ge(hg_act, 2)
            for hp in range(2):
                dve.wait_ge(rec_done, hp + 1)
                u = units.take()
                v.tensor_copy(mix2[:, 4 + 2 * hp:6 + 2 * hp, :], unit_view(u)).then_inc(unit_free, 1)
            dve.wait_ge(rec_std, 1)
            v.reciprocal(cden[0:4, 1, :], cden[0:4, 0, :]).then_inc(rec_rstd, 1)
            for hp in range(2):
                dve.wait_ge(rec_row, hp + 1)
                u = units.take()
                q = mix2[:, 4 + 2 * hp:6 + 2 * hp, :]
                v.scalar_tensor_tensor(q, unit_view(u), sm("hg_g"), q, ALU.mult, ALU.mult).then_inc(unit_free, 1)
                dve.wait_ge(unit_free, u + 1)
                link(tt(q, q, hgate[:, 2 * hp:2 * hp + 2, :], ALU.mult))
                p = slice(4 + 2 * hp, 6 + 2 * hp)
                link(v.tensor_copy(yh[:, p, :], q))
                tt(yl[:, p, :], q, f32(yh[:, p, :]), ALU.subtract).then_inc(rec_ready, 1)

            def post(k, y, gain_name, next_name):
                recip(k)
                dve.wait_ge(rstd_ready, k + 1)
                for m in range(4):
                    link(tt(y[:, 2 * m:2 * m + 2, :], y[:, 2 * m:2 * m + 2, :], two(rstd[:, k % 4, :]), ALU.mult))
                    for c in (2 * m, 2 * m + 1):
                        last = v.scalar_tensor_tensor(xT[:, c, :], y[:, c, :], sm(gain_name, c), xT[:, c, :],
                                                      ALU.mult, ALU.add)
                    last.then_inc(x_new, 1)
                    upd[0] += 1
                    if next_name:
                        dve.wait_ge(x_new, upd[0])
                        gain(next_name, m)

            y_dst = lambda m: yT[:, 2 * m:2 * m + 2, :]
            copy_units(C_WO2, y_dst)
            dve.wait_ge(unit_free, units.n)
            post(7, yT, "post_mix_g", "pre_x_g")
            after(C_Q2)
            recip(8)
            dve.wait_ge(rstd_ready, 9)
            for m in range(4):
                evac_scaled(C_Q2 + m, qT[:, 2 * m:2 * m + 2, :], 8)
            attention(12, 4, 1, 1.0 / 16, cross_out)
            copy_units(C_XO2, y_dst)
            dve.wait_ge(unit_free, units.n)
            post(9, yT, "post_x_g", "pre_ffn_g")
            v.memset(upad2[:, :, :, 0:1], 0.0)
            link(v.memset(upad2[:, :, :, T + 1:T + 2], 0.0))
            after(C_FFN)
            recip(10)
            dve.wait_ge(rstd_ready, 11)

            u_ffn = units.n

            def ffn_step(f, i, at=0):
                c0 = 2 * (C_FFN if f == 0 else C_FFN + 2 + 3 * (f - 1))
                b = f % 2
                for half in range(2):
                    u = u_ffn + 2 * f + half
                    if f == 0:
                        rest.upto(c0 + 2 * half + 3)
                    dve.wait_ge(half_done, i * PASS + (c0 + 2 * half + 2))
                    tt(upad2[:, b, 2 * half:2 * half + 2, 1:T + 1], unit_view(u), two(rstd[:, 2, :]),
                       ALU.mult).then_inc(unit_free, 1)
                    if f == 0:
                        rest.upto(c0 + 2 * half + 5)
                    elif c0 + 2 * half + 5 + at < HALVES:
                        subtract(c0 + 2 * half + 5, i)
                    dve.wait_ge(unit_free, i * 4 + (u + 1))
                    n = 12 * f + 6 * half
                    for tap in (1, 0, 2):
                        for j in range(2):
                            jj = 2 * half + j
                            col = SMALL["ffn_w"] + 16 * f + 4 * jj
                            w = small[:, bass.ds(i * 32 + (col + tap), 1)]
                            x = upad2[:, b, jj, tap:tap + T]
                            if tap == 1:
                                bias = small[:, bass.ds(i * 32 + (col + 3), 1)]
                                ins = v.tensor_scalar(fconv[:, b, jj, :], x, w, bias, ALU.mult, ALU.add)
                            else:
                                dve.wait_ge(fconv_steps, i * 24 + (n - 1))
                                ins = v.scalar_tensor_tensor(fconv[:, b, jj, :], x, w, fconv[:, b, jj, :],
                                                             ALU.mult, ALU.add)
                            ins.then_inc(fconv_steps, 1)
                            n += 1
                dve.wait_ge(fconv_steps, i * 24 + (12 * f + 12))
                dve.wait_ge(fsilu, i * 2 + (f + 1))
                hidden(b, fconv[:, b, 0:2, :], fconv[:, b, 2:4, :], fact_ready)
                if f and c0 + 9 < HALVES:
                    subtract(c0 + 9, i)

            ffn_step(0, 0)
            whole = loop_steps(C_FFN, FSTEPS, lambda t, i: ffn_step(t + 1, i))
            for t in range(2 * whole, FSTEPS - 1):
                ffn_step(t + 1, 0)
            dve.wait_ge(half_done, HALVES)
            for m in range(4):
                v.tensor_copy(yF[:, 2 * m:2 * m + 2, :],
                              psum[:, ACC + m, :].rearrange("p (j t) -> p j t", j=2)).then_inc(y_ready, 1)
            dve.wait_ge(y_ready, 4)
            post(11, yF, "post_ffn_g", None)


def _constants():
    c = np.zeros((P, NCONST), np.float32)
    p = np.arange(P)
    t = np.arange(T)

    def put(name, a, at=0):
        c[:a.shape[0], CONST[name] + at:CONST[name] + at + a.shape[1]] = a

    put("ident", np.eye(P))
    put("ones", np.ones((P, P)))
    for i, w in enumerate(POOL_W):
        put("rcnt", np.broadcast_to(np.float32(1) / np.minimum(t[:PADW] + 1, w).astype(np.float32), (P, PADW)), PADW * i)
    inv = np.power(np.float32(10000.0), -np.arange(16, dtype=np.float32) / np.float32(16)).astype(np.float32)
    ang = np.concatenate([(t // 64).astype(np.float32)[:, None] * inv, (t % 64).astype(np.float32)[:, None] * inv], 1)
    pair = ang[:, (p % 64) // 2].T
    put("cos", np.cos(pair))
    put("sin", np.sin(pair))
    rot = np.zeros((P, P))
    rot[p[1::2], p[0::2]] = -1
    rot[p[0::2], p[1::2]] = 1
    put("rot", rot)
    for j in range(2):
        put("dup", (p[:, None] == 64 * j + p[None, :] % 64).astype(float), 128 * j)
    for j in range(5):
        put("qk_sum", (2 * j + p[:, None] // 64 == np.arange(10)[None, :]).astype(float), 10 * j)
    for h in range(HG):
        put("hg_sum", np.broadcast_to(np.arange(4)[None, :] == h, (P, 4)).astype(float), 4 * h)
    put("prio", np.broadcast_to(np.tile([4.0, 3.0, 2.0, 1.0], 2), (P, 8)))
    x = p[:, None] ^ p[None, :]
    m = np.zeros((P, 8, P), np.int32)
    for i in range(7):
        m[:, i, :] = (x >> i) == 1
    m[:, 7, :] = x == 0
    return c, m


def _tiles(w, rows, c0, width):
    return w.reshape(rows, P, -1)[:, :, c0:c0 + width].transpose(1, 0, 2).reshape(P, rows * width)


def _stream(a):
    s = np.zeros((CHUNKS, 2, P, HW), np.float32)

    def halves(w, c0):
        return [_tiles(w, DK, c0 + P * j, P) for j in range(2)]

    def row_halves(w, c0):
        return [_tiles(w[512 * j:512 * (j + 1)], 4, c0, 256) for j in range(2)]

    def units(at, w, order, c0=0, cut=halves):
        for i, u in enumerate(order):
            s[at + i] = cut(w, c0 + 256 * u)

    units(C_WIN, a["w_in"][0], range(24))
    s[C_POOL, 1] = a["w_pool_grp"][0].transpose(1, 0, 2).reshape(P, 1024)
    for m in range(4):
        s[C_MERGE + m, 0] = _tiles(a["w_a_out"][0], 4, 256 * m, 256)
        s[C_MERGE + m, 1] = _tiles(a["w_c_out"][0], 4, 256 * m, 256)
    for suffix, k, v, q, o in (("", C_K1, C_V1, C_Q1, C_XO1), ("_2", C_K2, C_V2, C_Q2, C_XO2)):
        units(k, a["w_xkv" + suffix][0], range(4))
        units(v, a["w_xkv" + suffix][0], range(4), D, row_halves)
        units(q, a["w_xq" + suffix][0], range(4))
        units(o, a["w_xo" + suffix][0], range(4))
    units(C_WO, a["w_o"][0], range(4))
    units(C_WIN2, a["w_in_2"][0], WIN2_ORDER)
    units(C_WIN2 + WIN2_ORDER.index(9), a["w_in_2"][0], (9, 10), 0, row_halves)
    units(C_WO2, a["w_out_2"][0], range(4))

    def steps(at, count, gate, up, down):
        for e in range(count):
            g = at if e == 0 else at + 2 + 3 * (e - 1)
            s[g], s[g + 1] = gate(e), up(e)
            s[at + 3 * count - 1 if e == count - 1 else at + 3 * e + 4] = down(e).reshape(2, P, D)

    steps(C_MOE, EXPERTS, lambda e: halves(a["w_e_gate"][0, e], 0), lambda e: halves(a["w_e_up"][0, e], 0),
          lambda e: a["w_e_down"][0, e])
    steps(C_FFN, FSTEPS, lambda f: halves(a["w_up_2"][0], 256 * f), lambda f: halves(a["w_up_2"][0], FF + 256 * f),
          lambda f: a["w_down_2"][0, 256 * f:256 * (f + 1)])
    return s.reshape(HALVES, P, HW)


def _small(a):
    s = np.zeros((P, NSMALL), np.float32)

    def put(name, x, at=0):
        y = np.asarray(x).reshape(-1, P).T
        s[:, SMALL[name] + at:SMALL[name] + at + y.shape[1]] = y

    for name, key in (("mix_g", "norm_mix_g"), ("pool_s", "pool_scale"), ("x_g", "norm_x_g"), ("mem_g", "norm_mem_g"),
                      ("ffn_g", "norm_ffn_g"), ("f_g", "norm_f_g"), ("conv_b", "conv_a_b"), ("ln_g", "ln_a_g"),
                      ("ln_b", "ln_a_b"), ("c_w", "conv_c_w"), ("conv_w", "conv_a_w"), ("pre_mix_g", "pre_mix_g_2"),
                      ("post_mix_g", "post_mix_g_2"), ("pre_x_g", "pre_x_g_2"), ("mem2_g", "mem_norm_g_2"),
                      ("post_x_g", "post_x_g_2"), ("pre_ffn_g", "pre_ffn_g_2"), ("post_ffn_g", "post_ffn_g_2"),
                      ("hg_g", "hg_out_norm_g_2")):
        put(name, a[key])
    for name, key in (("q_g", "q_norm_g_2"), ("k_g", "k_norm_g_2")):
        put(name, np.tile(a[key].reshape(-1), 2))
    put("lb", a["hg_lb_2"].transpose(1, 0, 2))
    s[0:4, SMALL["r_b"]] = a["b_rg"][0]
    s[4:20, SMALL["r_b"]] = a["b_re"][0]
    w, b = a["conv_w_2"][0], a["conv_b_2"][0]
    for f in range(FSTEPS):
        for i in range(4):
            c0 = FF * (i // 2) + 256 * f + P * (i % 2)
            for j in range(3):
                put("ffn_w", w[j, c0:c0 + P], 16 * f + 4 * i + j)
            put("ffn_w", b[c0:c0 + P], 16 * f + 4 * i + 3)
    return s


def _turned(x):
    return np.ascontiguousarray(x[0].T.reshape(DK, P, T).transpose(1, 0, 2))


def kernel(**inputs):
    import concourse.bacc as _bacc
    from concourse.bass_utils import run_bass_kernel_spmd as _run

    a = {k: np.asarray(v) for k, v in inputs.items()}
    const, mask = _constants()
    router = np.concatenate([a["w_rg"][0], a["w_re"][0]], axis=1)
    arrays = {
        "stream": _stream(a),
        "x_t": _turned(a["x"]),
        "mem_t": _turned(a["mem"]),
        "mem2_t": _turned(a["mem_2"]),
        "small": _small(a),
        "const": const,
        "mask": mask,
        "router": np.ascontiguousarray(router.reshape(DK, P, 20).transpose(1, 0, 2)),
    }
    nc = _bacc.Bacc("TRN2", target_bir_lowering=False, num_devices=1)
    args = [nc.dram_tensor(k + "_in", x.shape, mybir.dt.from_np(x.dtype), kind="ExternalInput").ap() for k, x in arrays.items()]
    out = nc.dram_tensor("out_t", (P, DK, T), F32, kind="ExternalOutput").ap()
    build(nc, *args, out)
    r = _run(nc, [{k + "_in": x for k, x in arrays.items()}], core_ids=[0])
    got = r.results[0]["out_t"]
    return np.ascontiguousarray(got.transpose(1, 0, 2).reshape(D, T).T)[None]
```

```python
from contextlib import ExitStack

import numpy as np
import concourse.bass as bass
from concourse import mybir

ALU = mybir.AluOpType
ACT = mybir.ActivationFunctionType
F32 = mybir.dt.float32
F32R = mybir.dt.float32r
BF16 = mybir.dt.bfloat16
I32 = mybir.dt.int32
AX_X = mybir.AxisListType.X

P = 128
T = 256
TT = T // P
D = 1024
DK = D // P
EPS = 1e-6
HW = 1024
RAW = 6
SPLIT = 4
UNITS = 4
EARLY = 2
SB = 3
STAT = 7
ACC = 4
CONV_K = 31
C_K = 3
POOL_W = (2, 4, 8, 16)
PADW = 16
EXPERTS = 16
FF = 2816
FSTEPS = FF // 256
HG = 4
QH = 8
NEG = -1.0e30

C_WIN = 0
C_POOL = C_WIN + 24
C_MERGE = C_POOL + 1
C_K1 = C_MERGE + 4
C_V1 = C_K1 + 4
C_WO = C_V1 + 4
C_Q1 = C_WO + 4
C_XO1 = C_Q1 + 4
C_E0 = C_XO1 + 4
C_V2 = C_E0 + 2
C_MOE = C_V2 + 2
C_K2 = C_MOE + 3 * EXPERTS
C_WIN2 = C_K2 + 4
C_WO2 = C_WIN2 + 13
C_Q2 = C_WO2 + 4
C_XO2 = C_Q2 + 4
C_FFN = C_XO2 + 4
CHUNKS = C_FFN + 3 * FSTEPS
HALVES = 2 * CHUNKS
WHOLE0, WHOLE1 = 2 * C_POOL, 2 * (C_MERGE + 4)
WIN2_ORDER = (0, 1, 2, 5, 6, 7, 8, 3, 4, 9, 10, 11, 12)

U_MOE_FIRST = 24 + 4 + 8 + 8 + 4 + 4 + 8 + 4
U_MOE = U_MOE_FIRST + 2 + 4 + EXPERTS // 2
U_WIN2 = U_MOE + 2 * (EXPERTS - 1) + 4
U_ATT1 = U_MOE_FIRST - 4 - 8
U_GQA = U_WIN2 + 13 + 7 + 2
U_REC = U_WIN2 + 13 + 7 + 12 + 18
U_WO2 = U_REC + 4
U_ATT2 = U_WO2 + 4 + 4
U_XO2 = U_ATT2 + 8

SMALL = {}
_at = 0
for _name, _n in (("mix_g", 8), ("pool_s", 8), ("x_g", 8), ("mem_g", 8), ("ffn_g", 8), ("f_g", 8),
                  ("conv_b", 4), ("ln_g", 4), ("ln_b", 4), ("c_w", 4 * C_K), ("conv_w", 4 * CONV_K),
                  ("pre_mix_g", 8), ("post_mix_g", 8), ("pre_x_g", 8), ("mem2_g", 8), ("post_x_g", 8),
                  ("pre_ffn_g", 8), ("post_ffn_g", 8), ("hg_g", 1), ("q_g", 1), ("k_g", 1),
                  ("lb", 16), ("r_b", 1), ("ffn_w", 16 * FSTEPS)):
    SMALL[_name] = _at
    _at += _n
NSMALL = _at

CONST = {}
_at = 0
for _name, _n in (("ident", 128), ("ones", 128), ("rcnt", 4 * PADW), ("cos", T), ("sin", T), ("rot", 128),
                  ("dup", 256), ("qk_sum", 5 * 10), ("hg_sum", 16),
                  ("prio", 8)):
    CONST[_name] = _at
    _at += _n
NCONST = _at


def build(nc, stream, xt_in, memt_in, mem2t_in, small_in, const_in, mask_in, router_in, out_t):
    ctx = ExitStack()
    with ctx:
        def sb(name, shape, dt=F32):
            return ctx.enter_context(nc.sbuf_tensor(name, shape, dt))

        def sem(name):
            return ctx.enter_context(nc.semaphore(name))

        psum = ctx.enter_context(nc.psum_tensor("psum", [P, 8, 512], F32))

        raw = sb("raw", [P, RAW, HW])
        wh = sb("wh", [P, SPLIT, HW], F32R)
        wl = sb("wl", [P, SPLIT, HW], F32R)
        xT = sb("xT", [P, DK, T])
        sq = sb("sq", [P, DK, T])
        memn = sb("memn", [P, 2, DK, T])
        kT = sb("kT", [P, DK, T])
        vm = sb("vm", [P, TT, D])
        small = sb("small", [P, NSMALL])
        const = sb("const", [P, NCONST])
        mask = sb("mask", [P, 8, P], I32)
        router = sb("router", [P, DK, 20])
        rstd = sb("rstd", [P, 4, T])
        std = sb("std", [P, T])
        av2 = sb("av2", [P, TT, 128])
        cden = sb("cden", [16, 2, T])
        zeros = sb("zeros", [P, P], BF16)
        pick = sb("pick", [16, 16], F32R)
        eps = sb("eps", [P, 1])
        nmax = sb("nmax", [P, 16, TT])
        negm = sb("negm", [P, 16, TT])
        ssum = sb("ssum", [P, 16, TT])
        rsum = sb("rsum", [P, 16, TT])
        cols = sb("cols", [P, 2, TT])
        lbt = sb("lbt", [P, 8, 8])
        WORK = 12800
        ACT_AT = 8192
        PAIR = DK * T
        area_at = -(-nc.sbuf_base // 32) * 32
        sb("area", [P, WORK + 4 * PAIR])

        def at(name, start, shape, dt):
            return nc.alloc_sbuf_tensor_at(name, shape, dt, offset=area_at + 4 * start)

        work = at("work", 0, [P, WORK], F32)
        xh, xl = (at(n, WORK + i * PAIR, [P, DK, T], F32R) for i, n in enumerate(("xh", "xl")))
        yh, yl = (at(n, WORK + (2 + i) * PAIR, [P, DK, T], F32R) for i, n in enumerate(("yh", "yl")))
        xpair = at("xpair", WORK, [P, 2 * PAIR], F32)
        ypair = at("ypair", WORK + 2 * PAIR, [P, 2 * PAIR], F32)
        act_h, act_l = (at(n, ACT_AT + i * 4 * T, [P, 2, 2, T], F32R) for i, n in enumerate(("act_h", "act_l")))

        router_h, router_l = (at(n, 10240 + i * DK * 20, [P, DK, 20], F32R) for i, n in enumerate(("router_h", "router_l")))

        def f32(ap):
            return ap.bitcast(F32)

        def sm(name, i=0, n=1):
            return small[:, SMALL[name] + i:SMALL[name] + i + n]

        def cn(name, i=0, n=128, p=P):
            return const[0:p, CONST[name] + i:CONST[name] + i + n]

        ident = cn("ident")
        ones = cn("ones")

        class Region:

            def __init__(self, start=0):
                self.at = start

            def __call__(self, *dims):
                n = int(np.prod(dims))
                v = work[:, self.at:self.at + n]
                self.at += n
                assert self.at <= WORK, self.at
                if len(dims) == 2:
                    v = v.rearrange("p (a b) -> p a b", a=dims[0])
                elif len(dims) == 3:
                    v = v.rearrange("p (a b c) -> p a b c", a=dims[0], b=dims[1])
                return v

        r = Region()
        gates = r(24, T)
        apad = r(4, T + CONV_K - 1)
        lnstd = r(T)
        lnrstd = r(T)
        cx = r(4, T)
        cpad = r(4, T + C_K - 1)
        upad = r(4, T + PADW)
        ubuf = r(4, T + PADW)
        merged = work[:, r.at - 8 * (T + PADW):r.at - 8 * (T + PADW) + DK * T].rearrange("p (a b) -> p a b", a=DK)
        aval, agate, aacc, pT = (ypair[:, 4 * T * i:4 * T * (i + 1)].rearrange("p (a b) -> p a b", a=4)
                                 for i in range(4))
        asq = agate
        actT = aval
        cc, ctmp = kT[:, 0:4, :], kT[:, 4:8, :]
        vm_flat = vm.rearrange("p t d -> p (t d)")
        cb = vm_flat[:, 0:4 * T].rearrange("p (a b) -> p a b", a=4)
        cy = vm_flat[:, 4 * T:8 * T].rearrange("p (a b) -> p a b", a=4)
        mt1, mt2 = agate, aacc

        r = Region(9216)
        probs = r(4, TT, T)
        probsT = r(3, TT, T)
        r = Region(0)
        qT = r(DK, T)
        yT = r(DK, T)

        r = Region(0)
        rg = r(EXPERTS, T)
        gs = r(2, 2, T)
        us = r(2, 2, T)
        logitT = r(T)
        lt = r(TT, 20)
        gmx = r(TT, 1)
        gsub = r(TT, 4)
        gexp = r(TT, 4)
        gsm = r(TT, 1)
        gval = r(TT, 1)
        eqp = r(TT, 4)
        eqm = r(TT, 1)
        ohg = r(TT, 4)
        lsel = r(TT, 4)
        lprod = r(TT, 16)
        m1 = r(TT, 1)
        oh1 = r(TT, 4)
        lsel2 = r(TT, 4)
        m2 = r(TT, 1)
        oh2 = r(TT, 4)
        dm = r(TT, 1)
        ed = r(TT, 1)
        den = r(TT, 1)
        w1 = r(TT, 1)
        w2 = r(TT, 1)
        g4a = r(TT, 4)
        g4b = r(TT, 4)
        gate16 = r(TT, 16)
        gateT = act_h[0:16, 1, 0, :], act_l[0:16, 1, 0, :]
        assert r.at <= ACT_AT

        r = Region(0)
        mix2 = r(DK, T)
        qh = r(HG, T)
        ff = r(HG, T)
        fb = r(HG, T)
        kf = r(HG, T)
        kb = r(HG, T)
        hgate = r(HG, T)
        v2 = r(TT, 512)
        assert r.at <= 9216, r.at
        Kc, Qc, Kc2, Qc2 = (ypair[:, 4 * T * i:4 * T * (i + 1)].rearrange("p (a b) -> p a b", a=4)
                            for i in range(4))
        AT_flat = xpair[:, 0:PAIR]
        AT = AT_flat.rearrange("p (h s t) -> p h s t", h=HG, s=TT)
        Lf, Lb = (xpair[:, PAIR + 4 * T * i:PAIR + 4 * T * (i + 1)].rearrange("p (a b) -> p a b", a=4)
                  for i in range(2))
        aqk = memn[:, 0, 0:5, :]
        kdup = memn[:, 0, 5:7, :]
        asq2 = sq[:, 0:5, :]
        aqn = sq[:, 0:5, :]
        rtmp = Kc[:, 0:2, :]

        r = Region(0)
        upad2 = r(2, 4, T + 2)
        fconv = r(2, 4, T)
        yF = r(DK, T)
        assert r.at <= ACT_AT

        s_small = sem("small_loaded")
        s_x = [sem(f"x_loaded{m}") for m in range(4)]
        s_mem = sem("mem_loaded")
        s_mem2 = sem("mem2_loaded")
        s_cst = sem("const_loaded")
        s_mask = sem("mask_loaded")
        s_rt = sem("router_loaded")
        landed = [sem(f"landed{i}") for i in range(RAW)]
        hi_ready = sem("hi_ready")
        lo_pool = sem("lo_pool")
        lo_dve = sem("lo_dve")
        half_done = sem("half_done")
        router_split = sem("router_split")
        mem_hi = sem("mem_hi")
        mem_split = sem("mem_split")
        unit_free = sem("unit_free")
        zeroed = sem("zeroed")
        xg_ready = sem("xg_ready")
        x_new = sem("x_new")
        y_ready = sem("y_ready")
        sq_ready = sem("sq_ready")
        sq_folded = sem("sq_folded")
        stats_done = sem("stats_done")
        std_ready = sem("std_ready")
        rstd_ready = sem("rstd_ready")
        memn_ready = sem("memn_ready")
        agate_sig = sem("agate_sig")
        gates_sig = sem("gates_sig")
        a_glu = sem("a_glu")
        conv_a = sem("conv_a_steps")
        pads_zero = sem("pads_zero")
        pool_steps = sem("pool_steps")
        p_ready = sem("pooled_ready")
        c_ready = sem("c_ready")
        ln_mean = sem("ln_mean")
        ln_centered = sem("ln_centered")
        ln_sq = sem("ln_sq")
        ln_var = sem("ln_var")
        ln_std = sem("ln_std")
        ln_normed = sem("ln_normed")
        a_act = sem("a_act")
        pool_full = sem("pool_full")
        merged_ready = sem("merged_ready")
        scores_done = sem("scores_done")
        maxed = sem("maxed")
        neg_ready = sem("neg_ready")
        exp_done = sem("exp_done")
        rsum_ready = sem("rsum_ready")
        probs_ready = sem("probs_ready")
        turned = sem("probs_turned")
        copied = sem("probs_copied")
        o_done = sem("o_done")
        logits_done = sem("logits_done")
        logits_ready = sem("logits_ready")
        ltok_done = sem("ltok_done")
        route = sem("route_steps")
        route_exp = sem("route_exp")
        gate16_ready = sem("gate16_ready")
        gateT_done = sem("gateT_done")
        gateT_ready = sem("gateT_ready")
        rg_full = sem("rg_full")
        silu_done = sem("silu_done")
        act_ready = sem("act_ready")
        sum_done = sem("sum_done")
        lb_steps = sem("lb_steps")
        lb_exp = sem("lb_exp")
        f_sig = sem("f_sig")
        hq_act = sem("hq_act")
        hg_act = sem("hg_act")
        forget_ready = sem("forget_ready")
        forward_ready = sem("forward_ready")
        forward_next = sem("forward_next")
        back_ready = sem("back_ready")
        back_step = sem("back_step")
        back_next = sem("back_next")
        level_done = sem("level_done")
        A_ready = sem("A_ready")
        mix_split = sem("mix_split")
        rec_done = sem("rec_done")
        rec_sq = sem("rec_sq")
        rec_sum = sem("rec_sum")
        rec_std = sem("rec_std")
        rec_rstd = sem("rec_rstd")
        rec_row = sem("rec_row")
        rec_ready = sem("rec_ready")
        qk_sq = sem("qk_sq")
        qk_sum = sem("qk_sum")
        qk_std = sem("qk_std")
        qk_rstd = sem("qk_rstd")
        qk_row = sem("qk_row")
        qk_rot = sem("qk_rot")
        roped = sem("roped")
        dup_done = sem("dup_done")
        rcol_ready = sem("rcol_ready")
        fconv_steps = sem("fconv_steps")
        fsilu = sem("fsilu")
        fact_ready = sem("fact_ready")
        loop_chain = sem("dve_loop_chain")
        chain = sem("dve_chain")
        stored = sem("stored")

        block = ctx.enter_context(nc.Block())

        def hi_count(c):
            return c + 1 - (WHOLE1 - WHOLE0 if c >= WHOLE1 else 0)

        def lo_count(c):
            return c // 2 + 1 - ((WHOLE1 - WHOLE0) // 2 if c >= WHOLE1 else 0)

        def rest_sem(c):
            return lo_dve if c % 2 else lo_pool

        PASS = 12
        PASS_LANDED = 16 * PASS // RAW
        assert PASS % RAW == 0 and PASS % SPLIT == 0

        class Splitter:

            def __init__(self, issue, first, stride):
                self.issue, self.next, self.stride = issue, first, stride

            def upto(self, c):
                while self.next <= min(c, HALVES - 1):
                    if not WHOLE0 <= self.next < WHOLE1:
                        self.issue(self.next, 0)
                    self.next += self.stride

            def skip_to(self, c):
                while self.next < c:
                    self.next += self.stride

        def sides(x, h):
            y = x.rearrange("p g t -> p (g t)").rearrange("p (b s i) -> p b s i", s=2, i=h)
            return y[:, :, 0, :], y[:, :, 1, :]

        def two(ap):
            return ap.unsqueeze(1).to_broadcast([P, 2, T])

        def unit_view(u):
            return psum[:, u % UNITS, :].rearrange("p (j t) -> p j t", j=2)

        def in_attention_order(heads, group, turn, out):
            for h in range(group):
                turn(h)
            for g in range(0, heads, group):
                if g + group < heads:
                    turn(g + group)
                out(g)
                for h in range(g + group + 1, min(g + 2 * group, heads)):
                    turn(h)

        def turn_units(u, heads, group, between):
            seq = []
            in_attention_order(heads, group, lambda h: seq.extend(["turn"] + ["between"] * between),
                               lambda g: seq.append("out"))
            return [u + i for i, what in enumerate(seq) if what == "turn"]

        class UnitCount:

            def __init__(self):
                self.n = 0

            def take(self, n=1):
                self.n += n
                return self.n - n

        @block.sync
        def _(sp):
            def load(slot, c):
                sp.dma_start(raw[:, slot, :], stream[c]).then_inc(landed[slot], 16)

            def reload(c, i=0):
                b = c - RAW
                if WHOLE0 <= b < WHOLE1:
                    sp.wait_ge(half_done, b + 1)
                else:
                    sp.wait_ge(rest_sem(b), i * (RAW // 2) + lo_count(b))
                load(c % RAW, i * RAW + c)

            def load_x(m):
                q = slice(2 * m, 2 * m + 2)
                sp.dma_start(xT[:, q, :], xt_in[:, q, :]).then_inc(s_x[m], 16)

            load(0, 0)
            sp.dma_start(small[:], small_in).then_inc(s_small, 16)
            load_x(0)
            for m in range(1, 4):
                load(m, m)
                load_x(m)
            for c in range(4, RAW):
                load(c, c)
            turn = WHOLE0 // RAW
            with sp.Fori(0, turn - 1) as i:
                for j in range(RAW):
                    reload(RAW + j, i)
            mid = -(-(WHOLE1 + RAW) // RAW) * RAW
            for c in range(turn * RAW, mid):
                reload(c)
            with sp.Fori(0, (HALVES - mid) // RAW) as i:
                for j in range(RAW):
                    reload(mid + j, i)
            for c in range(mid + (HALVES - mid) // RAW * RAW, HALVES):
                reload(c)
            for m in range(4):
                sp.wait_ge(x_new, 4 * 6 + m + 1)
                sp.dma_start(out_t[:, 2 * m:2 * m + 2, :], xT[:, 2 * m:2 * m + 2, :]).then_inc(stored, 16)
            sp.wait_ge(stored, 64)

        @block.tensor
        def _(pe):
            units = UnitCount()

            def matmul(out, w, x, start, stop, **kw):
                return nc.tensor.matmul(out, w, x, start=start, stop=stop, **kw)

            def wait_raw(c):
                pe.wait_ge(landed[c % RAW], 16 * (c // RAW + 1))

            def wait_split(c):
                pe.wait_ge(rest_sem(c), lo_count(c))

            def free_bank(u):
                if u >= UNITS:
                    pe.wait_ge(unit_free, u - UNITS + 1)

            def three(out, a_h, a_l, b_h, b_l, start, stop, **kw):
                matmul(out, a_h, b_h, start, False, **kw)
                matmul(out, a_h, b_l, False, False, **kw)
                return matmul(out, a_l, b_h, False, stop, **kw)

            def columns(out, slot, x):
                for k in range(DK):
                    w = slice(k * P, (k + 1) * P)
                    last = three(out, wh[:, slot, w], wl[:, slot, w], x[0][:, k, :], x[1][:, k, :], k == 0, k == DK - 1)
                return last

            def rows(out, slot, x):
                for t in range(TT):
                    for k in range(DK):
                        w = slice(k * P, (k + 1) * P)
                        q = slice(t * P, (t + 1) * P)
                        last = three(out(t), x[0][:, k, q], x[1][:, k, q], wh[:, slot, w], wl[:, slot, w],
                                     k == 0, k == DK - 1)
                return last

            def project(n, x):
                u = units.take()
                free_bank(u)
                for j in range(2):
                    c = 2 * n + j
                    wait_split(c)
                    columns(psum[:, u % UNITS, j * T:(j + 1) * T], c % SPLIT, x).then_inc(half_done, 1)

            def project_rows(n, x):
                u = units.take()
                free_bank(u)
                for j in range(2):
                    c = 2 * n + j
                    wait_split(c)
                    for t in range(TT):
                        q = slice(t * P, (t + 1) * P)
                        for kk in range(DK // 2):
                            k = j * DK // 2 + kk
                            w = slice(kk * 256, (kk + 1) * 256)
                            last = three(psum[:, u % UNITS, t * 256:(t + 1) * 256], x[0][:, k, q], x[1][:, k, q],
                                         wh[:, c % SPLIT, w], wl[:, c % SPLIT, w], k == 0 and t == 0, k == DK - 1,
                                         skip_group_check=True)
                    last.then_inc(half_done, 1)

            def project_two(n, x, ready):
                part = two_units(n, x, units.take(2), lambda k: pe.wait_ge(xg_ready, DK * ready + k + 1))
                for m in range(4):
                    part(m)

            def project_heads(n):
                heads_out = units.n
                part = two_units(n, yg, units.take(2))
                pe.wait_ge(unit_free, heads_out - 1)
                part(0)
                part(1)
                pe.wait_ge(unit_free, heads_out)
                part(2, 4)
                for m in range(2, 4):
                    project(n + m, yg)

            def two_units(n, x, u0, wait_tile=None):
                def part(m, end=None):
                    end = end or m + 1
                    if m == 0:
                        free_bank(u0 + 1)
                    for i in range(4):
                        c = 2 * n + i
                        if m == 0:
                            wait_split(c)
                        for k in range(2 * m, 2 * end):
                            if wait_tile and i == 0:
                                wait_tile(k)
                            w = slice(k * P, (k + 1) * P)
                            last = three(psum[:, (u0 + i // 2) % UNITS, (i % 2) * T:(i % 2 + 1) * T],
                                         wh[:, c % SPLIT, w], wl[:, c % SPLIT, w], x[0][:, k, :], x[1][:, k, :],
                                         k == 0 and i % 2 == 0, k == DK - 1, skip_group_check=True)
                        if end == 4:
                            last.then_inc(half_done, 1)

                return part

            def stats(k, columns=False):
                if k:
                    pe.wait_ge(std_ready, k)
                for m in range(4):
                    pe.wait_ge(sq_folded, 4 * k + m + 1)
                    last = matmul(psum[:, STAT, 0:T], ones, sq[:, 2 * m, :], m == 0, m == 3)
                if columns:
                    for t in range(TT):
                        for m in range(4):
                            last = matmul(psum[:, STAT, T + t:T + t + 1], sq[:, 2 * m, t * P:(t + 1) * P],
                                          ones[:, 0:1], m == 0, m == 3)
                last.then_inc(stats_done, 1)

            def attention(base, heads, group, scores, values, between=None):
                def score(h):
                    hh = base + h
                    if hh >= SB:
                        pe.wait_ge(exp_done, hh - SB + 1)
                    scores(h, 4 + hh % SB).then_inc(scores_done, 1)

                def turn(h):
                    u = units.take()
                    free_bank(u)
                    pe.wait_ge(probs_ready, base + h + 1)
                    for m in range(TT):
                        for t in range(TT):
                            last = nc.tensor.transpose(psum[:, u % UNITS, m * T + t * P:m * T + (t + 1) * P],
                                                       probs[:, (base + h) % 4, t, m * P:(m + 1) * P], ident)
                    last.then_inc(turned, 1)
                    if h + SB < heads:
                        score(h + SB)
                    if between:
                        between(h)

                def out(g):
                    u = units.take()
                    free_bank(u)
                    pe.wait_ge(copied, base + g + group)
                    for h in range(g, g + group):
                        values(h, (base + h) % 3, u % UNITS).then_inc(o_done, 1)

                def early():
                    for h in range(EARLY):
                        score(h)

                def rest():
                    for h in range(EARLY, SB):
                        score(h)
                    in_attention_order(heads, group, turn, out)

                return early, rest

            def cross_scores(h, bank):
                pe.wait_ge(unit_free, query_unit[0] + h + 1)
                for t in range(TT):
                    for d in range(2):
                        last = matmul(psum[:, bank, t * T:(t + 1) * T], qT[:, 2 * h + d, t * P:(t + 1) * P],
                                      kT[:, 2 * h + d, :], d == 0, d == 1)
                return last

            def cross_values(h, pslot, bank):
                for d in range(2):
                    for m in range(TT):
                        last = matmul(psum[:, bank, d * T:(d + 1) * T], vm[:, m, h * 256 + d * P:h * 256 + (d + 1) * P],
                                      probsT[:, pslot, m, :], m == 0, m == 1)
                return last

            query_unit = [0]

            xg, yg = (xh, xl), (yh, yl)
            project_two(C_WIN, xg, 0)
            pe.wait_ge(s_cst, 16)
            stats(0)
            project(C_WIN + 2, xg)
            stats(1)
            project(C_WIN + 3, xg)
            stats(2)
            for n in range(C_WIN + 4, C_WIN + 19):
                project(n, xg)
            pe.wait_ge(conv_a, 4 * CONV_K)
            for c in range(4):
                last = matmul(psum[:, 6, 0:T], ones, aacc[:, c, :], c == 0, c == 3)
            last.then_inc(ln_mean, 1)
            for n in range(C_WIN + 19, C_WIN + 21):
                project(n, xg)
            pe.wait_ge(ln_sq, 2)
            for c in range(4):
                last = matmul(psum[:, 5, 0:T], ones, asq[:, c, :], c == 0, c == 3)
            last.then_inc(ln_var, 1)
            for n in range(C_WIN + 21, C_WIN + 24):
                project(n, xg)

            pe.wait_ge(p_ready, 1)
            wait_raw(2 * C_POOL)
            wait_raw(2 * C_POOL + 1)
            for m in range(4):
                u = units.take()
                free_bank(u)
                for j in range(2):
                    last = matmul(psum[:, u % UNITS, j * T:(j + 1) * T],
                                  raw[:, (2 * C_POOL + 1) % RAW, m * 256 + j * P:m * 256 + (j + 1) * P], pT[:, m, :], True, True)
                    if m == 3:
                        last.then_inc(half_done, 1)
                if m < 3:
                    last.then_inc(pool_full, 1)
            pe.wait_ge(a_act, 4)
            pe.wait_ge(c_ready, 1)
            for m in range(4):
                for i, x in enumerate((actT, cy)):
                    c = 2 * (C_MERGE + m) + i
                    wait_raw(c)
                    u = units.take()
                    free_bank(u)
                    for j in range(2):
                        for k in range(4):
                            last = matmul(psum[:, u % UNITS, j * T:(j + 1) * T],
                                          raw[:, c % RAW, k * 256 + j * P:k * 256 + (j + 1) * P], x[:, k, :],
                                          k == 0, k == 3)
                    last.then_inc(half_done, 1)
            pe.wait_ge(mem_split, 1)
            for m in range(4):
                project(C_K1 + m, xg)
            for m in range(4):
                project_rows(C_V1 + m, xg)
            pe.wait_ge(merged_ready, 4)
            for m in range(4):
                project(C_WO + m, yg)
            query_unit[0] = units.n
            project_two(C_Q1, xg, 1)
            stats(3)
            project(C_Q1 + 2, xg)
            early, rest = attention(0, 4, 1, cross_scores, cross_values)
            early()
            project(C_Q1 + 3, xg)
            assert units.n == U_ATT1, units.n
            rest()
            project_heads(C_XO1)
            project_two(C_E0, xg, 2)
            stats(4)
            pe.wait_ge(router_split, 1)
            for k in range(DK):
                last = three(psum[0:20, 6, 0:T], router_h[:, k, :], router_l[:, k, :], xg[0][:, k, :], xg[1][:, k, :],
                             k == 0, k == DK - 1)
            last.then_inc(logits_done, 1)
            pe.wait_ge(mem_split, 2)
            project_rows(C_V2, yg)
            pe.wait_ge(logits_ready, 1)
            for t in range(TT):
                last = nc.tensor.transpose(psum[:, 5, t * 20:(t + 1) * 20], logitT[0:20, t * P:(t + 1) * P],
                                           ident[0:20, 0:20])
            last.then_inc(ltok_done, 1)
            for m in range(1, 4):
                project_rows(C_V2 + m, yg)
            pe.wait_ge(gate16_ready, 1)
            for t in range(TT):
                last = nc.tensor.transpose(psum[0:16, 6, t * P:(t + 1) * P], gate16[:, t, :], ident)
            last.then_inc(gateT_done, 1)
            pe.wait_ge(gateT_ready, 1)
            for e in range(0, EXPERTS, 2):
                u = units.take()
                free_bank(u)
                for j in range(2):
                    for part in range(2):
                        last = matmul(psum[:, u % UNITS, j * T:(j + 1) * T],
                                      pick[0:16, e + j:e + j + 1].to_broadcast([16, P]), gateT[part], part == 0, part == 1)
                last.then_inc(rg_full, 1)

            def clear_sums(k):
                pe.wait_ge(zeroed, 2)
                pe.wait_ge(std_ready, k)
                for b in range(4):
                    matmul(psum[:, ACC + b, :], zeros[:], zeros[:, 0:1].to_broadcast([P, 512]), True, True)

            def steps(first_chunk, count, ready):
                u0 = units.n

                def down(c0, t, i, final=False):
                    pe.wait_ge(ready, i * 2 + (t + 1))
                    for k in range(2):
                        c = c0 + k
                        pe.wait_ge(rest_sem(c), i * (PASS // 2) + lo_count(c))
                        for o in range(DK):
                            w = slice(o * P, (o + 1) * P)
                            last = three(psum[:, ACC + o // 2, (o % 2) * T:(o % 2 + 1) * T],
                                         wh[:, c % SPLIT, w], wl[:, c % SPLIT, w],
                                         act_h[:, t % 2, k, :], act_l[:, t % 2, k, :], False, k == 1,
                                         skip_group_check=True)
                            if final and k == 1 and o % 2 and o < DK - 1:
                                last.then_inc(sum_done, 1)
                        last.then_inc(half_done, 1)

                def step(t, i):
                    c0 = 2 * (first_chunk + 2 + 3 * t)
                    for q in range(2):
                        u = u0 + 2 * t + q
                        pe.wait_ge(unit_free, i * UNITS + (u - UNITS + 1))
                        for j in range(2):
                            c = c0 + 2 * q + j
                            pe.wait_ge(rest_sem(c), i * (PASS // 2) + lo_count(c))
                            columns(psum[:, u % UNITS, j * T:(j + 1) * T], c % SPLIT, xg).then_inc(half_done, 1)
                    down(c0 + 4, t, i)

                passes = (count - 1) // 2
                with pe.Fori(0, passes) as i:
                    step(0, i)
                    step(1, i)
                for t in range(2 * passes, count - 1):
                    step(t, 0)
                units.take(2 * (count - 1))
                down(2 * (first_chunk + 3 * count - 1), count - 1, 0, final=True)

            clear_sums(5)
            steps(C_MOE, EXPERTS, act_ready)

            project(C_K2, yg)
            pe.wait_ge(x_new, 12)
            stats(5)
            for m in range(1, 4):
                project(C_K2 + m, yg)
            project_two(C_WIN2, xg, 3)
            stats(6, columns=True)
            def level(i):
                pe.wait_ge(forward_ready, i + 1)
                if i:
                    pe.wait_ge(back_ready, i)
                for hp in range(2):
                    u = units.take()
                    free_bank(u)
                    for h in range(2):
                        for c in range(2):
                            hd = 2 * hp + h
                            s0 = c * P
                            t0 = (1 - c) * P if i == 8 else c * P
                            kk, qq = (Kc, qh) if i == 0 else ((Kc, Qc), (Kc2, Qc2))[i % 2]
                            last = matmul(psum[:, u % UNITS, (2 * h + c) * P:(2 * h + c + 1) * P],
                                          kk[:, hd, s0:s0 + P], qq[:, hd, t0:t0 + P], True, True)
                    last.then_inc(level_done, 1)

            def head_row(heads, h, width):
                return ident[0:heads, h:h + 1].to_broadcast([heads, width])

            uu = units.take()
            free_bank(uu)
            c = 2 * (C_WIN2 + 2)
            wait_split(c)
            columns(psum[:, uu % UNITS, 0:T], c % SPLIT, xg).then_inc(half_done, 1)
            wait_split(c + 1)
            rows(lambda t: psum[:, uu % UNITS, T + t * P:T + (t + 1) * P],
                 (c + 1) % SPLIT, xg).then_inc(half_done, 1)
            project(C_WIN2 + 3, xg)
            pe.wait_ge(qk_sq, 5)
            for j in range(5):
                last = matmul(psum[0:10, 4, 0:T], cn("qk_sum", 10 * j, 10), asq2[:, j, :], j == 0, j == 4)
            last.then_inc(qk_sum, 1)
            project(C_WIN2 + 4, xg)
            pe.wait_ge(qk_rstd, 1)
            for j0 in (0, 2, 4):
                u = units.take()
                free_bank(u)
                for j in range(j0, min(j0 + 2, 5)):
                    for half in range(2):
                        last = matmul(psum[64 * half:64 * (half + 1), u % UNITS, (j - j0) * T:(j - j0 + 1) * T],
                                      head_row(10, 2 * j + half, 64), cden[0:10, 1, :], True, True)
                last.then_inc(qk_row, 1)
            project(C_WIN2 + 5, xg)
            for j0 in (0, 2, 4):
                u = units.take()
                free_bank(u)
                for j in range(j0, min(j0 + 2, 5)):
                    last = matmul(psum[:, u % UNITS, (j - j0) * T:(j - j0 + 1) * T], cn("rot"), aqn[:, j, :],
                                  True, True)
                last.then_inc(qk_rot, 1)
            project(C_WIN2 + 6, xg)
            u = units.take()
            free_bank(u)
            pe.wait_ge(roped, 3)
            for j in range(2):
                last = matmul(psum[:, u % UNITS, j * T:(j + 1) * T], cn("dup", 128 * j), aqk[:, 4, :], True, True)
            last.then_inc(dup_done, 1)
            for i in (7, 8):
                project(C_WIN2 + i, xg)
            def gqa_scores(h, bank):
                b = 64 * (h % 2)
                for t in range(TT):
                    last = matmul(psum[:, bank, t * T:(t + 1) * T], aqk[b:b + 64, h // 2, t * P:(t + 1) * P],
                                  kdup[b:b + 64, h // 4, :], True, True)
                return last

            def gqa_values(h, pslot, bank):
                b = 64 * (h % 2)
                for m in range(TT):
                    last = matmul(psum[b:b + 64, bank, 0:T], av2[:, m, 64 * (h // 4):64 * (h // 4 + 1)],
                                  probsT[:, pslot, m, :], m == 0, m == 1)
                return last

            early, rest = attention(4, QH, 2, gqa_scores, gqa_values, lambda h: level(h + 1))
            project_rows(C_WIN2 + 9, xg)
            pe.wait_ge(unit_free, U_WIN2 + 14)
            early()
            project_rows(C_WIN2 + 10, xg)
            for i in (11, 12):
                project(C_WIN2 + i, xg)
            level(0)
            assert units.n == U_GQA, units.n
            rest()

            assert units.n == U_REC, units.n
            for hp in range(2):
                u = units.take()
                free_bank(u)
                pe.wait_ge(A_ready, 1)
                for h in range(2):
                    for m in range(TT):
                        last = matmul(psum[:, u % UNITS, h * T:(h + 1) * T],
                                      v2[:, m, (2 * hp + h) * P:(2 * hp + h + 1) * P], AT[:, 2 * hp + h, m, :],
                                      m == 0, m == 1)
                last.then_inc(rec_done, 1)
            out_part = two_units(C_WO2, yg, U_WO2)
            pe.wait_ge(mix_split, 1)
            out_part(0)
            pe.wait_ge(rec_sq, 2)
            for h in range(HG):
                last = matmul(psum[0:4, 4, 0:T], cn("hg_sum", 4 * h, 4), sq[:, h, :], h == 0, h == 3)
            last.then_inc(rec_sum, 1)
            out_part(1)
            pe.wait_ge(rec_rstd, 1)
            for hp in range(2):
                u = units.take()
                free_bank(u)
                for h in range(2):
                    last = matmul(psum[:, u % UNITS, h * T:(h + 1) * T],
                                  head_row(4, 2 * hp + h, P), cden[0:4, 1, :], True, True)
                last.then_inc(rec_row, 1)
            assert units.n == U_WO2, units.n
            units.take(2)
            for m in range(2):
                pe.wait_ge(rec_ready, m + 1)
                out_part(2 + m)
            for m in range(2, 4):
                project(C_WO2 + m, yg)
            stats(7)
            query_unit[0] = units.n
            project_two(C_Q2, xg, 4)
            stats(8)
            project(C_Q2 + 2, xg)
            early, rest = attention(12, 4, 1, cross_scores, cross_values)
            early()
            project(C_Q2 + 3, xg)
            assert units.n == U_ATT2, units.n
            rest()
            project_heads(C_XO2)
            stats(9)
            project_two(C_FFN, xg, 5)
            stats(10)
            clear_sums(11)
            steps(C_FFN, FSTEPS, fact_ready)
            pe.wait_ge(y_ready, 4)
            stats(11)

        @block.scalar
        def _(act):
            def fn(out, in_, f, **kw):
                return nc.scalar.activation(out, in_, f, **kw)

            act.dma_start(const[:], const_in).then_inc(s_cst, 16)

            def squares(k, src, ready=None, base=0):
                for m in range(4):
                    square_part(k, m, src, ready, base)

            def square_part(k, m, src, ready=None, base=0):
                if k and m == 0:
                    act.wait_ge(stats_done, k)
                if ready is not None:
                    act.wait_ge(ready, base + m + 1)
                fn(sq[:, 2 * m:2 * m + 2, :], src[:, 2 * m:2 * m + 2, :], ACT.Square).then_inc(sq_ready, 1)

            def root(k, columns=False):
                act.wait_ge(stats_done, k + 1)
                if k:
                    act.wait_ge(rstd_ready, k)
                if columns:
                    fn(cols[:, 0, :], psum[:, STAT, T:T + TT], ACT.Sqrt, scale=1.0 / D, bias=eps[:])
                fn(std[:], psum[:, STAT, 0:T], ACT.Sqrt, scale=1.0 / D, bias=eps[:]).then_inc(std_ready, 1)

            def round_high(c, i):
                act.wait_ge(landed[c % RAW], i * PASS_LANDED + 16 * (c // RAW + 1))
                if c >= SPLIT:
                    act.wait_ge(half_done, i * PASS + (c - SPLIT + 1))
                nc.scalar.copy(wh[:, c % SPLIT, :], raw[:, c % RAW, :]).then_inc(hi_ready, 1)

            high = Splitter(round_high, 0, 1)

            def after(n):
                high.upto(2 * n + 1 + SPLIT)

            high.upto(0)
            act.wait_ge(zeroed, 1)
            for m in range(4):
                high.upto(m)
                act.wait_ge(s_x[m], 16)
                square_part(0, m, xT)
            act.dma_start(memn[:, 0], memt_in).then_inc(s_mem, 16)
            act.dma_start(memn[:, 1], mem2t_in).then_inc(s_mem2, 16)
            act.dma_start(router[:], router_in).then_inc(s_rt, 16)
            act.dma_start(mask[:], mask_in).then_inc(s_mask, 16)
            after(0)
            root(0)
            after(1)
            act.wait_ge(s_mem, 16)
            squares(1, memn[:, 0])
            root(1)
            after(2)
            act.wait_ge(s_mem2, 16)
            squares(2, memn[:, 1])
            root(2)
            for m in range(2):
                after(C_WIN + 2 + m)
                act.wait_ge(unit_free, 2 + m + 1)
                fn(agate[:, 2 * m:2 * m + 2, :], agate[:, 2 * m:2 * m + 2, :], ACT.Sigmoid).then_inc(agate_sig, 1)

            def gate_sigmoid(m):
                after(C_WIN + 12 + m)
                act.wait_ge(unit_free, 12 + m + 1)
                fn(gates[:, 2 * m:2 * m + 2, :], gates[:, 2 * m:2 * m + 2, :], ACT.Sigmoid).then_inc(gates_sig, 1)

            for n in range(4, 12):
                after(C_WIN + n)
            for m in range(6):
                gate_sigmoid(m)
            for m in range(2):
                act.wait_ge(ln_centered, m + 1)
                fn(asq[:, 2 * m:2 * m + 2, :], aacc[:, 2 * m:2 * m + 2, :], ACT.Square).then_inc(ln_sq, 1)
            for m in range(6, 9):
                gate_sigmoid(m)
            after(C_WIN + 21)
            act.wait_ge(ln_var, 1)
            fn(lnstd, psum[:, 5, 0:T], ACT.Sqrt, scale=1.0 / 512, bias=eps[:]).then_inc(ln_std, 1)
            act.wait_ge(ln_normed, 2)
            for c in range(4):
                fn(actT[:, c, :], aacc[:, c, :], ACT.Silu, scale=sm("ln_g", c), bias=sm("ln_b", c)).then_inc(a_act, 1)
            for m in range(9, 12):
                gate_sigmoid(m)

            def divide(hh):
                act.wait_ge(rsum_ready, hh + 1)
                for t in range(TT):
                    last = fn(probs[:, hh % 4, t, :], probs[:, hh % 4, t, :], ACT.Copy, scale=rsum[:, hh, t:t + 1])
                last.then_inc(probs_ready, 1)

            def copy_turned(hh, u):
                act.wait_ge(turned, hh + 1)
                if hh >= 3:
                    act.wait_ge(o_done, hh - 2)
                nc.scalar.copy(probsT[:, hh % 3], unit_view(u)).then_inc(copied, 1)

            def exps(base, heads, scale, turn_units, start, end):
                for h in range(start, end):
                    hh = base + h
                    act.wait_ge(neg_ready, hh + 1)
                    if hh >= 4:
                        act.wait_ge(turned, hh - 3)
                    for t in range(TT):
                        last = fn(probs[:, hh % 4, t, :], psum[:, 4 + hh % SB, t * T:(t + 1) * T], ACT.Exp,
                                  scale=scale, bias=negm[:, hh, t:t + 1], accum_out=ssum[:, hh, t:t + 1])
                    last.then_inc(exp_done, 1)
                    if h:
                        divide(hh - 1)
                    if h > 1:
                        copy_turned(hh - 2, turn_units[h - 2])
                if end < heads:
                    return
                divide(base + heads - 1)
                for h in (heads - 2, heads - 1):
                    copy_turned(base + h, turn_units[h])

            def split_memory(i, pair):
                act.wait_ge(memn_ready, i + 1)
                for m in range(4):
                    q = slice(2 * m, 2 * m + 2)
                    nc.scalar.copy(pair[:, q, :], memn[:, i, q, :]).then_inc(mem_hi, 1)

            act.wait_ge(half_done, 2 * C_POOL)
            split_memory(0, xh)
            for n in range(C_MERGE, C_Q1):
                after(n)
                if n >= C_WO:
                    square_part(3, n - C_WO, xT, x_new, 0)
            after(C_Q1)
            root(3)
            after(C_Q1 + 1)
            after(C_Q1 + 2)
            act.wait_ge(lb_steps, 3)
            fn(lbt[:, 3:5, :], lbt[:, 1:3, :], ACT.Exp).then_inc(lb_exp, 1)
            heads = 0, 4, 1.0 / 16, turn_units(U_ATT1, 4, 1, 0)
            exps(*heads, 0, EARLY)
            after(C_Q1 + 3)
            exps(*heads, EARLY, 4)
            for n in range(C_XO1, C_E0):
                after(n)
                square_part(4, n - C_XO1, xT, x_new, 4)
            after(C_E0)
            split_memory(1, yh)
            root(4)

            def expert_silu(parity, value):
                act.wait_ge(unit_free, value)
                fn(gs[:, parity], gs[:, parity], ACT.Silu).then_inc(silu_done, 1)

            after(C_E0 + 1)
            expert_silu(0, U_MOE_FIRST + 1)
            after(C_V2)
            act.wait_ge(route, 2)
            fn(gexp[:], gsub[:], ACT.Exp).then_inc(route_exp, 1)
            act.wait_ge(route, 17)
            fn(ed[:], dm[:], ACT.Exp).then_inc(route_exp, 1)
            for m in range(1, 4):
                after(C_V2 + m)

            def loop_steps(first_chunk, count, silu):
                def step(t, i):
                    c0 = 2 * (first_chunk + 2 + 3 * t)
                    assert i is not None
                    for c in (c0 + 4, c0 + 5):
                        round_high(c, i)
                    silu(t, i)
                    for c in range(c0 + 6, c0 + 10):
                        round_high(c, i)

                passes = (count - 1) // 2
                last = 2 * (first_chunk + 2 + 3 * (count - 1)) + 3
                assert high.next == 2 * (first_chunk + 2) + 4, (high.next, first_chunk)
                whole = passes if last < HALVES else passes - 1
                with act.Fori(0, whole) as i:
                    step(0, i)
                    step(1, i)
                high.skip_to(2 * (first_chunk + 2) + 4 + PASS * whole)
                for t in range(2 * whole, count - 1):
                    c0 = 2 * (first_chunk + 2 + 3 * t)
                    high.upto(c0 + 5)
                    silu(t, 0)
                    high.upto(c0 + 9)

            loop_steps(C_MOE, EXPERTS, lambda t, i: expert_silu((t + 1) % 2, i * 4 + (U_MOE + 2 * t + 1)))

            squares(5, xT, x_new, 8)
            after(C_K2)
            root(5)
            after(C_K2 + 1)
            for m in range(4):
                if m == 3:
                    after(C_K2 + 2)
                    after(C_K2 + 3)
                square_part(6, m, xT, x_new, 12)
            after(C_WIN2)
            root(6, columns=True)
            after(C_WIN2 + 1)
            act.wait_ge(stats_done, 7)
            for j in range(5):
                if j == 4:
                    after(C_WIN2 + 2)
                act.wait_ge(unit_free, U_WIN2 + j // 2 + 1)
                fn(asq2[:, j, :], aqk[:, j, :], ACT.Square).then_inc(qk_sq, 1)
            after(C_WIN2 + 3)

            def forget_sigmoid(m, unit):
                act.wait_ge(unit_free, unit + 1)
                f, k = ((ff, kf), (fb, kb))[m // 2]
                h = slice(2 * (m % 2), 2 * (m % 2) + 2)
                fn(k[:, h, :], f[:, h, :], ACT.Sigmoid, scale=-1.0)
                fn(f[:, h, :], f[:, h, :], ACT.Sigmoid).then_inc(f_sig, 1)

            act.wait_ge(qk_sum, 1)
            fn(cden[0:10, 0, :], psum[0:10, 4, 0:T], ACT.Sqrt, scale=1.0 / 64, bias=eps[0:10, :]).then_inc(qk_std, 1)
            forget_sigmoid(0, U_WIN2 + 3)
            after(C_WIN2 + 4)
            forget_sigmoid(1, U_WIN2 + 4)
            after(C_WIN2 + 5)
            forget_sigmoid(2, U_WIN2 + 8)
            after(C_WIN2 + 6)
            forget_sigmoid(3, U_WIN2 + 12)
            for m in range(2):
                after(C_WIN2 + 7 + m)
                act.wait_ge(unit_free, U_WIN2 + 14 + m + 1)
                fn(qh[:, 2 * m:2 * m + 2, :], qh[:, 2 * m:2 * m + 2, :], ACT.Silu).then_inc(hq_act, 1)
            after(C_WIN2 + 9)
            after(C_WIN2 + 10)
            heads = 4, QH, 1.0 / 8, turn_units(U_GQA, QH, 2, 2)
            exps(*heads, 0, EARLY)
            for m in range(2):
                after(C_WIN2 + 11 + m)
                act.wait_ge(unit_free, U_WIN2 + 18 + m + 1)
                fn(hgate[:, 2 * m:2 * m + 2, :], hgate[:, 2 * m:2 * m + 2, :], ACT.Silu).then_inc(hg_act, 1)
            exps(*heads, EARLY, QH)
            for hp in range(2):
                act.wait_ge(unit_free, U_REC + hp + 1)
                fn(sq[:, 2 * hp:2 * hp + 2, :], mix2[:, 4 + 2 * hp:6 + 2 * hp, :], ACT.Square).then_inc(rec_sq, 1)
            act.wait_ge(rec_sum, 1)
            fn(cden[0:4, 0, :], psum[0:4, 4, 0:T], ACT.Sqrt, scale=1.0 / 128, bias=eps[0:4, :]).then_inc(rec_std, 1)
            for m in range(4):
                after(C_WO2 + m)
                square_part(7, m, yT, unit_free, U_WO2)
            root(7)
            squares(8, xT, x_new, 16)
            after(C_Q2)
            root(8)
            after(C_Q2 + 1)
            after(C_Q2 + 2)
            heads = 12, 4, 1.0 / 16, turn_units(U_ATT2, 4, 1, 0)
            exps(*heads, 0, EARLY)
            after(C_Q2 + 3)
            exps(*heads, EARLY, 4)
            for m in range(4):
                after(C_XO2 + m)
                square_part(9, m, yT, unit_free, U_XO2)
            root(9)
            squares(10, xT, x_new, 20)
            after(C_FFN)
            root(10)

            def ffn_silu(parity, value):
                act.wait_ge(fconv_steps, value)
                fn(fconv[:, parity, 0:2, :], fconv[:, parity, 0:2, :], ACT.Silu).then_inc(fsilu, 1)

            after(C_FFN + 1)
            ffn_silu(0, 6)
            loop_steps(C_FFN, FSTEPS, lambda t, i: ffn_silu((t + 1) % 2, i * 24 + (12 * (t + 1) + 6)))
            squares(11, yF, y_ready, 0)
            root(11)

        @block.gpsimd
        def _(pool):
            nc.gpsimd.memset(apad[:, :, 0:CONV_K - 1], 0.0)
            nc.gpsimd.memset(upad[:, :, 0:PADW], 0.0)
            nc.gpsimd.memset(cpad[:, :, 0:C_K - 1], 0.0).then_inc(pads_zero, 1)
            pool.wait_ge(pads_zero, 1)
            n = [0]

            def subtract(c, i):
                pool.wait_ge(hi_ready, i * PASS + hi_count(c))
                nc.gpsimd.tensor_tensor(wl[:, c % SPLIT, :], raw[:, c % RAW, :], f32(wh[:, c % SPLIT, :]),
                                        ALU.subtract).then_inc(lo_pool, 1)

            rest = Splitter(subtract, 0, 2)

            def after(n):
                rest.upto(2 * n + 1 + SPLIT)

            def fold(k, m):
                pool.wait_ge(sq_ready, 4 * k + m + 1)
                nc.gpsimd.tensor_tensor(sq[:, 2 * m, :], sq[:, 2 * m, :], sq[:, 2 * m + 1, :], ALU.add).then_inc(sq_folded, 1)

            for m in range(4):
                rest.upto(m)
                fold(0, m)
            for k in range(1, 3):
                after(k)
                for m in range(4):
                    fold(k, m)

            def step(ins):
                ins.then_inc(pool_steps, 1)
                n[0] += 1
                rest.upto(rest.next)
                pool.wait_ge(pool_steps, n[0])

            add = lambda o, a, b: nc.gpsimd.tensor_tensor(o, a, b, ALU.add)
            rest.upto(14)
            pool.wait_ge(unit_free, 6)
            W = T + PADW
            step(add(ubuf[:, :, 1:W], upad[:, :, 1:W], upad[:, :, 0:W - 1]))
            pool.wait_ge(stats_done, 3)
            buf = sq.rearrange("p k t -> p (k t)")[:, 0:4 * W].rearrange("p (a b) -> p a b", a=4)
            step(add(buf[:, 1:4, 4:W], ubuf[:, 1:4, 4:W], ubuf[:, 1:4, 2:W - 2]))
            step(add(ubuf[:, 2:4, 8:W], buf[:, 2:4, 8:W], buf[:, 2:4, 4:W - 4]))
            step(add(buf[:, 3:4, 16:W], ubuf[:, 3:4, 16:W], ubuf[:, 3:4, 8:W - 8]))
            pool.wait_ge(s_cst, 16)
            for i, src in enumerate((ubuf, buf, ubuf, buf)):
                w = POOL_W[i]
                nc.gpsimd.tensor_tensor(pT[:, i, 0:PADW], src[:, i, PADW:2 * PADW], cn("rcnt", PADW * i, PADW), ALU.mult)
                step(nc.gpsimd.tensor_scalar(pT[:, i, PADW:T], src[:, i, 2 * PADW:W], 1.0 / w, None, ALU.mult))
            nc.gpsimd.tensor_tensor(pT[:], pT[:], upad[:, :, PADW:W], ALU.subtract).then_inc(p_ready, 1)
            rest.upto(26)
            pool.wait_ge(unit_free, 12)
            pool.wait_ge(s_small, 16)
            step(nc.gpsimd.tensor_tensor(cpad[:, :, C_K - 1:C_K - 1 + T], cc[:], cx[:], ALU.mult))
            for j in range(C_K):
                for c in range(4):
                    dst = cy if j == 0 else ctmp
                    last = nc.gpsimd.tensor_scalar(dst[:, c, :], cpad[:, c, j:j + T], sm("c_w", 4 * j + c), None, ALU.mult)
                step(last)
                if j:
                    step(nc.gpsimd.tensor_tensor(cy[:], cy[:], ctmp[:], ALU.add))
            nc.gpsimd.tensor_tensor(cy[:], cy[:], cb[:], ALU.mult).then_inc(c_ready, 1)
            rest.upto(WHOLE1 - 1)
            def stretch(end):
                first = rest.next
                passes = (end - first) // PASS
                with pool.Fori(0, passes) as i:
                    for c in range(first, first + PASS, 2):
                        subtract(c, i)
                rest.skip_to(first + passes * PASS)
                rest.upto(end - 1)

            for k, first in ((3, C_WO), (4, C_XO1)):
                for m in range(4):
                    after(first + m)
                    fold(k, m)
            stretch(2 * C_K2 + 2)
            for m in range(4):
                fold(5, m)
            after(C_K2)
            after(C_K2 + 1)
            for m in range(4):
                if m == 3:
                    after(C_K2 + 2)
                    after(C_K2 + 3)
                fold(6, m)
            stretch(2 * C_WO2 + 4)
            pool.wait_ge(half_done, 2 * C_WO2)
            pool.wait_ge(hq_act, 2)
            pool.wait_ge(forget_ready, 1)
            nc.gpsimd.memset(Lb[:], 1.0).then_inc(back_next, 1)
            for i in range(1, 9):
                h = 2 ** (i - 1)
                kk, qq = ((Kc, Qc), (Kc2, Qc2))[i % 2]
                pool.wait_ge(back_next, i)
                if i >= 2:
                    pool.wait_ge(level_done, 2 * (i - 1))
                (bl, br), (lbl, lbr) = sides(fb, h), sides(Lb, h)
                ptt = nc.gpsimd.tensor_tensor
                ptt(sides(kk, h)[1], sides(kb, h)[1], lbr, ALU.mult)
                ptt(sides(qq, h)[0], sides(qh, h)[0], bl, ALU.mult).then_inc(back_ready, 1)
                if i == 8:
                    break
                wide = [P, 4 * T // (2 * h), h]
                pool.wait_ge(back_ready, i)
                ptt(lbr, lbr, bl[:, :, 0:1].to_broadcast(wide), ALU.mult).then_inc(back_step, 1)
                pool.wait_ge(back_step, i)
                ptt(bl, bl, br[:, :, 0:1].to_broadcast(wide), ALU.mult).then_inc(back_next, 1)
            for m in range(4):
                after(C_WO2 + m)
                fold(7, m)
            for m in range(4):
                fold(8, m)
            for m in range(4):
                after(C_XO2 + m)
                fold(9, m)
            for m in range(4):
                fold(10, m)
            stretch(HALVES)
            for m in range(4):
                fold(11, m)

        @block.vector
        def _(dve):
            units = UnitCount()
            v = nc.vector
            upd = [0]
            links = [0]

            def link(ins):
                ins.then_inc(chain, 1)
                links[0] += 1
                dve.wait_ge(chain, links[0])

            def tt(out, a, b, op):
                return v.tensor_tensor(out, a, b, op)

            def subtract(c, i):
                dve.wait_ge(hi_ready, i * PASS + hi_count(c))
                tt(wl[:, c % SPLIT, :], raw[:, c % RAW, :], f32(wh[:, c % SPLIT, :]), ALU.subtract).then_inc(lo_dve, 1)

            rest = Splitter(subtract, 1, 2)

            def full(n):
                rest.upto(2 * n + 3)
                dve.wait_ge(half_done, 2 * n + 2)

            def after(n):
                rest.upto(2 * n + 1 + SPLIT)

            def evac_scaled(n, out, k):
                full(n)
                u = units.take()
                tt(out, unit_view(u), two(rstd[:, k % 4, :]), ALU.mult).then_inc(unit_free, 1)
                after(n)

            def recip(k):
                dve.wait_ge(std_ready, k + 1)
                v.reciprocal(rstd[:, k % 4, :], std[:]).then_inc(rstd_ready, 1)

            def gain(name, m, also=None):
                for k in (2 * m, 2 * m + 1):
                    last = v.tensor_scalar(xh[:, k, :], xT[:, k, :], sm(name, k), None, ALU.mult)
                    if k == 2 * m and also is not None:
                        last.then_inc(also, 1)
                link(last)
                for k in (2 * m, 2 * m + 1):
                    last = v.scalar_tensor_tensor(xl[:, k, :], xT[:, k, :], sm(name, k), f32(xh[:, k, :]),
                                                  ALU.mult, ALU.subtract)
                    last.then_inc(xg_ready, 1)

            def split(m, src, h, l, done, n):
                q = slice(2 * m, 2 * m + 2)
                v.tensor_copy(h[:, q, :], src).then_inc(done, 1)
                dve.wait_ge(done, n)
                return tt(l[:, q, :], src, f32(h[:, q, :]), ALU.subtract)

            def residual(chunk, name):
                for m in range(4):
                    full(chunk + m)
                    u = units.take()
                    upd[0] += 1
                    q = xT[:, 2 * m:2 * m + 2, :]
                    tt(q, unit_view(u), q, ALU.add).then_inc(x_new, 1)
                    if m == 3:
                        after(chunk + m)
                    dve.wait_ge(x_new, upd[0])
                    gain(name, m, unit_free)
                    if m < 3:
                        after(chunk + m)

            v.memset(eps[:], EPS).then_inc(zeroed, 1)
            v.memset(zeros[:], 0.0).then_inc(zeroed, 1)
            dve.wait_ge(s_small, 16)
            for m in range(4):
                dve.wait_ge(s_x[m], 16)
                gain("mix_g", m)
                if m % 2:
                    rest.upto(m)
            after(0)
            recip(0)
            dve.wait_ge(rstd_ready, 1)
            dve.wait_ge(pads_zero, 1)
            for m in range(2):
                evac_scaled(C_WIN + m, aval[:, 2 * m:2 * m + 2, :], 0)

            def normalise_memory(i, name):
                dve.wait_ge(rstd_ready, 2 + i)
                dve.wait_ge(stats_done, 2 + i)
                for k in range(DK):
                    last = v.scalar_tensor_tensor(memn[:, i, k, :], memn[:, i, k, :], sm(name, k),
                                                  rstd[:, 1 + i, :], ALU.mult, ALU.mult)
                last.then_inc(memn_ready, 1)

            for m in range(2):
                evac_scaled(C_WIN + 2 + m, agate[:, 2 * m:2 * m + 2, :], 0)
                recip(1 + m)
            for m in range(2):
                dve.wait_ge(agate_sig, m + 1)
                h = slice(2 * m, 2 * m + 2)
                tt(apad[:, h, CONV_K - 1:], aval[:, h, :], agate[:, h, :], ALU.mult).then_inc(a_glu, 1)
            dve.wait_ge(a_glu, 2)
            done = [0]

            def convolve(taps):
                for j in taps:
                    for c in range(4):
                        x = apad[:, c, j:j + T]
                        if j == 0:
                            ins = v.tensor_scalar(aacc[:, c, :], x, sm("conv_w", c), sm("conv_b", c), ALU.mult, ALU.add)
                        else:
                            dve.wait_ge(conv_a, done[0] - 3)
                            ins = v.scalar_tensor_tensor(aacc[:, c, :], x, sm("conv_w", 4 * j + c), aacc[:, c, :],
                                                         ALU.mult, ALU.add)
                        ins.then_inc(conv_a, 1)
                        done[0] += 1

            dst = {4: upad[:, 0:2, PADW:], 5: upad[:, 2:4, PADW:], 6: cx[:, 0:2, :], 7: cx[:, 2:4, :],
                   8: cb[:, 0:2, :], 9: cb[:, 2:4, :], 10: cc[:, 0:2, :], 11: cc[:, 2:4, :]}
            dst.update((12 + m, gates[:, 2 * m:2 * m + 2, :]) for m in range(12))
            for n in range(4, 17):
                evac_scaled(C_WIN + n, dst[n], 0)
                convolve(range((n - 4) * CONV_K // 13, (n - 3) * CONV_K // 13))
            evac_scaled(C_WIN + 17, dst[17], 0)
            dve.wait_ge(ln_mean, 1)
            for m in range(2):
                h = slice(2 * m, 2 * m + 2)
                v.scalar_tensor_tensor(aacc[:, h, :], two(psum[:, 6, 0:T]), -1.0 / 512, aacc[:, h, :],
                                       ALU.mult, ALU.add).then_inc(ln_centered, 1)
            normalise_memory(0, "mem_g")
            for n in range(18, 21):
                evac_scaled(C_WIN + n, dst[n], 0)
            dve.wait_ge(ln_std, 1)
            link(v.reciprocal(lnrstd, lnstd))
            for m in range(2):
                h = slice(2 * m, 2 * m + 2)
                tt(aacc[:, h, :], aacc[:, h, :], two(lnrstd), ALU.mult).then_inc(ln_normed, 1)
            for n in range(21, 24):
                evac_scaled(C_WIN + n, dst[n], 0)
            def split_memory(i, h, l):
                for m in range(4):
                    q = slice(2 * m, 2 * m + 2)
                    dve.wait_ge(mem_hi, 4 * i + m + 1)
                    last = tt(l[:, q, :], memn[:, i, q, :], f32(h[:, q, :]), ALU.subtract)
                last.then_inc(mem_split, 1)

            split_memory(0, xh, xl)
            dve.wait_ge(gates_sig, 12)
            for m in range(4):
                if m < 3:
                    dve.wait_ge(pool_full, m + 1)
                else:
                    full(C_POOL)
                u = units.take()
                for j in range(2):
                    last = v.scalar_tensor_tensor(merged[:, 2 * m + j, :], psum[:, u % UNITS, j * T:(j + 1) * T],
                                                  sm("pool_s", 2 * m + j), gates[:, 8 + 2 * m + j, :],
                                                  ALU.mult, ALU.mult)
                last.then_inc(unit_free, 1)
            for m in range(4):
                full(C_MERGE + m)
                ua, uc = units.take(), units.take()
                q = slice(2 * m, 2 * m + 2)
                b = slice(2 * (m % 2), 2 * (m % 2) + 2)
                tt(mt1[:, b, :], unit_view(ua), gates[:, 2 * m:2 * m + 2, :], ALU.mult).then_inc(unit_free, 1)
                tt(mt2[:, b, :], unit_view(uc), gates[:, 16 + 2 * m:18 + 2 * m, :], ALU.mult).then_inc(unit_free, 1)
                dve.wait_ge(unit_free, uc + 1)
                link(tt(mt1[:, b, :], mt1[:, b, :], mt2[:, b, :], ALU.add))
                link(tt(merged[:, q, :], mt1[:, b, :], merged[:, q, :], ALU.add))
                after(C_MERGE + m)
            for m in range(4):
                q = slice(2 * m, 2 * m + 2)
                v.tensor_copy(yh[:, q, :], merged[:, q, :]).then_inc(chain, 1)
                links[0] += 1
                dve.wait_ge(chain, links[0])
                tt(yl[:, q, :], merged[:, q, :], f32(yh[:, q, :]), ALU.subtract).then_inc(merged_ready, 1)
            normalise_memory(1, "mem2_g")

            def copy_unit(n, dst):
                full(n)
                u = units.take()
                v.tensor_copy(dst, unit_view(u)).then_inc(unit_free, 1)
                after(n)

            def copy_units(chunk, dst_of):
                for m in range(4):
                    copy_unit(chunk + m, dst_of(m))

            k_dst = lambda m: kT[:, 2 * m:2 * m + 2, :]
            v_dst = lambda m: vm[:, :, 256 * m:256 * (m + 1)]
            copy_units(C_K1, k_dst)
            l0, l1 = sm("lb", 0, 8), sm("lb", 8, 8)
            tt(lbt[:, 0, :], l0, l1, ALU.max).then_inc(lb_steps, 1)
            dve.wait_ge(lb_steps, 1)
            tt(lbt[:, 1, :], l0, lbt[:, 0, :], ALU.subtract).then_inc(lb_steps, 1)
            tt(lbt[:, 2, :], l1, lbt[:, 0, :], ALU.subtract).then_inc(lb_steps, 1)

            copy_units(C_V1, v_dst)
            def attention(base, heads, group, scale, take_out, meanwhile=None, between=None):
                def row_max(h):
                    hh = base + h
                    dve.wait_ge(scores_done, hh + 1)
                    s = psum[:, 4 + hh % SB, :].rearrange("p (t m) -> p t m", t=TT)
                    v.tensor_reduce(nmax[:, hh, :], s, AX_X, ALU.max).then_inc(maxed, 1)
                    dve.wait_ge(maxed, hh + 1)
                    v.tensor_scalar(negm[:, hh, :], nmax[:, hh, :], -scale, None, ALU.mult).then_inc(neg_ready, 1)

                def invert(h):
                    hh = base + h
                    dve.wait_ge(exp_done, hh + 1)
                    v.reciprocal(rsum[:, hh, :], ssum[:, hh, :]).then_inc(rsum_ready, 1)


                def turn(h):
                    hh = base + h
                    if h + 1 < heads:
                        invert(h + 1)
                    if h + SB < heads:
                        row_max(h + SB)
                    if meanwhile:
                        meanwhile(h)
                    dve.wait_ge(copied, hh + 1)
                    dve.wait_ge(unit_free, units.take())
                    v.nop().then_inc(unit_free, 1)
                    if between:
                        between(h)

                def out(g):
                    dve.wait_ge(o_done, base + g + group)
                    take_out(g, units.take()).then_inc(unit_free, 1)

                def early():
                    for h in range(EARLY):
                        row_max(h)
                    invert(0)

                def rest():
                    for h in range(EARLY, SB):
                        row_max(h)
                    in_attention_order(heads, group, turn, out)

                return early, rest

            def cross_out(h, u):
                q = slice(2 * h, 2 * h + 2)
                link(v.tensor_copy(yh[:, q, :], unit_view(u)))
                return tt(yl[:, q, :], unit_view(u), f32(yh[:, q, :]), ALU.subtract)

            residual(C_WO, "x_g")
            after(C_Q1)
            recip(3)
            dve.wait_ge(rstd_ready, 4)
            early, later = attention(0, 4, 1, 1.0 / 16, cross_out)
            for m in range(4):
                if m == 3:
                    early()
                evac_scaled(C_Q1 + m, qT[:, 2 * m:2 * m + 2, :], 3)
            later()
            dve.wait_ge(lb_exp, 1)
            link(tt(lbt[:, 5, :], lbt[:, 3, :], lbt[:, 4, :], ALU.add))
            link(v.reciprocal(lbt[:, 5, :], lbt[:, 5, :]))
            tt(lbt[:, 6, :], lbt[:, 3, :], lbt[:, 5, :], ALU.mult)
            link(tt(lbt[:, 7, :], lbt[:, 4, :], lbt[:, 5, :], ALU.mult))
            dve.wait_ge(s_rt, 16)
            link(v.tensor_copy(router_h[:], router[:]))
            tt(router_l[:], router[:], f32(router_h[:]), ALU.subtract).then_inc(router_split, 1)
            dve.wait_ge(s_cst, 16)
            v.tensor_copy(pick[:], ident[0:16, 0:16])
            residual(C_XO1, "ffn_g")
            after(C_E0)
            split_memory(1, yh, yl)
            recip(4)
            dve.wait_ge(rstd_ready, 5)
            dve.wait_ge(logits_done, 1)
            tt(logitT[0:20, :], psum[0:20, 6, 0:T], rstd[0:20, 0, :], ALU.mult).then_inc(route, 1)
            dve.wait_ge(route, 1)
            v.tensor_scalar(logitT[0:20, :], logitT[0:20, :], sm("r_b")[0:20, :], None, ALU.add).then_inc(logits_ready, 1)
            full(C_E0)
            ug = units.take()
            assert ug == U_MOE_FIRST, (ug, U_MOE_FIRST)
            tt(gs[:, 0], unit_view(ug), two(rstd[:, 0, :]), ALU.mult).then_inc(unit_free, 1)
            full(C_E0 + 1)
            uu = units.take()
            tt(us[:, 0], unit_view(uu), two(rstd[:, 0, :]), ALU.mult).then_inc(unit_free, 1)
            after(C_E0 + 1)

            rn = [1]

            def step(ins):
                ins.then_inc(route, 1)
                rn[0] += 1
                dve.wait_ge(route, rn[0])

            b4 = lambda ap: ap.to_broadcast([P, TT, 4])
            prio = cn("prio", 0, 8).rearrange("p (a b) -> p a b", a=TT)
            dve.wait_ge(ltok_done, 1)
            link(v.tensor_copy(lt[:], psum[:, 5, 0:40].rearrange("p (t n) -> p t n", t=TT)))
            link(v.tensor_reduce(gmx[:], lt[:, :, 0:4], AX_X, ALU.max))
            step(tt(gsub[:], lt[:, :, 0:4], b4(gmx[:]), ALU.subtract))
            after(C_V2)
            step(tt(eqp[:], lt[:, :, 0:4], b4(gmx[:]), ALU.is_equal))
            step(tt(eqp[:], eqp[:], prio, ALU.mult))
            step(v.tensor_reduce(eqm[:], eqp[:], AX_X, ALU.max))
            step(tt(ohg[:], eqp[:], b4(eqm[:]), ALU.is_equal))
            for t in range(TT):
                last = tt(lprod[:, t, :].rearrange("p (g e) -> p g e", g=4),
                          lt[:, t, 4:20].rearrange("p (g e) -> p g e", g=4),
                          ohg[:, t, :].unsqueeze(2).to_broadcast([P, 4, 4]), ALU.mult)
            step(last)
            for t in range(TT):
                last = v.tensor_reduce(lsel[:, t, :], lprod[:, t, :].rearrange("p (g e) -> p e g", g=4), AX_X, ALU.add)
            step(last)
            step(v.tensor_reduce(m1[:], lsel[:], AX_X, ALU.max))
            step(tt(eqp[:], lsel[:], b4(m1[:]), ALU.is_equal))
            step(tt(eqp[:], eqp[:], prio, ALU.mult))
            step(v.tensor_reduce(eqm[:], eqp[:], AX_X, ALU.max))
            step(tt(oh1[:], eqp[:], b4(eqm[:]), ALU.is_equal))
            step(v.tensor_scalar(lsel2[:], oh1[:], NEG, None, ALU.mult))
            step(tt(lsel2[:], lsel2[:], lsel[:], ALU.add))
            step(v.tensor_reduce(m2[:], lsel2[:], AX_X, ALU.max))
            step(tt(dm[:], m2[:], m1[:], ALU.subtract))
            step(tt(eqp[:], lsel2[:], b4(m2[:]), ALU.is_equal))
            step(tt(eqp[:], eqp[:], prio, ALU.mult))
            step(v.tensor_reduce(eqm[:], eqp[:], AX_X, ALU.max))
            step(tt(oh2[:], eqp[:], b4(eqm[:]), ALU.is_equal))
            dve.wait_ge(route_exp, 1)
            step(v.tensor_reduce(gsm[:], gexp[:], AX_X, ALU.add))
            step(v.reciprocal(gval[:], gsm[:]))
            dve.wait_ge(route_exp, 2)
            after(C_V2 + 1)
            step(v.tensor_scalar(den[:], ed[:], 1.0, None, ALU.add))
            step(v.reciprocal(den[:], den[:]))
            step(tt(w1[:], gval[:], den[:], ALU.mult))
            step(tt(w2[:], w1[:], ed[:], ALU.mult))
            step(tt(g4a[:], oh1[:], b4(w1[:]), ALU.mult))
            step(tt(g4b[:], oh2[:], b4(w2[:]), ALU.mult))
            step(tt(g4a[:], g4a[:], g4b[:], ALU.add))
            for t in range(TT):
                last = tt(gate16[:, t, :].rearrange("p (g e) -> p g e", g=4),
                          ohg[:, t, :].unsqueeze(2).to_broadcast([P, 4, 4]),
                          g4a[:, t, :].unsqueeze(1).to_broadcast([P, 4, 4]), ALU.mult)
            last.then_inc(gate16_ready, 1)
            for m in range(3):
                copy_unit(C_V2 + m, v_dst(m))
            dve.wait_ge(gateT_done, 1)
            link(v.tensor_copy(gateT[0], psum[0:16, 6, 0:T]))
            tt(gateT[1], psum[0:16, 6, 0:T], f32(gateT[0]), ALU.subtract).then_inc(gateT_ready, 1)
            copy_unit(C_V2 + 3, v_dst(3))
            for e in range(0, EXPERTS, 2):
                dve.wait_ge(rg_full, e // 2 + 1)
                u = units.take()
                if e == 0:
                    link(tt(us[:, 0], us[:, 0], two(psum[:, u % UNITS, 0:T]), ALU.mult))
                tt(rg[:, e:e + 2, :], unit_view(u), two(rstd[:, 0, :]), ALU.mult).then_inc(unit_free, 1)
            dve.wait_ge(silu_done, 1)
            dve.wait_ge(unit_free, units.n)
            def hidden(b, gate, up, ready):
                link_free(tt(up, gate, up, ALU.mult))
                link_free(v.tensor_copy(act_h[:, b], up))
                tt(act_l[:, b], up, f32(act_h[:, b]), ALU.subtract).then_inc(ready, 1)

            in_loop = [0, 0, 0]

            def link_free(ins):
                ins.then_inc(loop_chain, 1)
                in_loop[0] += 1
                dve.wait_ge(loop_chain, in_loop[1] + in_loop[0])

            hidden(0, gs[:, 0], us[:, 0], act_ready)

            assert units.n == U_MOE, (units.n, U_MOE)

            def expert(t, i):
                c0 = 2 * (C_MOE + 2 + 3 * t)
                u = U_MOE + 2 * t
                b = (t + 1) % 2
                dve.wait_ge(half_done, i * PASS + (c0 + 2))
                tt(gs[:, b], unit_view(u), two(rstd[:, 0, :]), ALU.mult).then_inc(unit_free, 1)
                subtract(c0 + 5, i)
                dve.wait_ge(half_done, i * PASS + (c0 + 4))
                weight = rg[:, t + 1, :] if isinstance(i, int) else work[:, bass.ds(i * (2 * T) + (t + 1) * T, T)]
                tt(us[:, b], unit_view(u + 1), two(weight), ALU.mult).then_inc(unit_free, 1)
                subtract(c0 + 7, i)
                dve.wait_ge(unit_free, i * 4 + (u + 2))
                dve.wait_ge(silu_done, i * 2 + (t + 2))
                hidden(b, gs[:, b], us[:, b], act_ready)
                subtract(c0 + 9, i)

            def loop_steps(first_chunk, count, one):
                passes = (count - 1) // 2
                assert rest.next == 2 * (first_chunk + 2) + 5, (rest.next, first_chunk)
                last = 2 * (first_chunk + 2 + 3 * (count - 1)) + 3
                whole = passes if last < HALVES else passes - 1
                before = in_loop[0]
                with dve.Fori(0, whole) as i:
                    in_loop[1] = i * 4
                    one(0, i)
                    one(1, i)
                in_loop[0], in_loop[1] = before + 4 * whole, 0
                rest.skip_to(2 * (first_chunk + 2) + 5 + PASS * whole)
                return whole

            whole = loop_steps(C_MOE, EXPERTS, expert)
            for t in range(2 * whole, EXPERTS - 1):
                expert(t, 0)
            rest.skip_to(2 * (C_MOE + 3 * EXPERTS) + 3)
            units.take(30)
            for m in range(4):
                if m < 3:
                    dve.wait_ge(sum_done, m + 1)
                else:
                    dve.wait_ge(half_done, 2 * (C_MOE + 3 * EXPERTS))
                q = xT[:, 2 * m:2 * m + 2, :]
                tt(q, psum[:, ACC + m, :].rearrange("p (j t) -> p j t", j=2), q, ALU.add).then_inc(x_new, 1)

            upd[0] += 4
            copy_unit(C_K2, k_dst(0))
            recip(5)
            dve.wait_ge(rstd_ready, 6)
            for m in range(4):
                for k in (2 * m, 2 * m + 1):
                    last = v.scalar_tensor_tensor(xT[:, k, :], xT[:, k, :], sm("f_g", k), rstd[:, 1, :],
                                                  ALU.mult, ALU.mult)
                last.then_inc(x_new, 1)
                upd[0] += 1
                dve.wait_ge(x_new, upd[0])
                gain("pre_mix_g", m)
                if m:
                    copy_unit(C_K2 + m, k_dst(m))
            after(C_WIN2)
            recip(6)
            dve.wait_ge(std_ready, 7)
            v.reciprocal(cols[:, 1, :], cols[:, 0, :]).then_inc(rcol_ready, 1)
            dve.wait_ge(rstd_ready, 7)
            dve.wait_ge(rcol_ready, 1)

            assert units.n == U_WIN2, (units.n, U_WIN2)

            def forget(m):
                f, k = ((ff, kf), (fb, kb))[m // 2]
                dve.wait_ge(f_sig, m + 1)
                for h in (2 * (m % 2), 2 * (m % 2) + 1):
                    c = 4 * (m // 2) + h
                    v.tensor_scalar(f[:, h, :], f[:, h, :], lbt[:, 7, c:c + 1], lbt[:, 6, c:c + 1], ALU.mult, ALU.add)
                    last = v.tensor_scalar(k[:, h, :], k[:, h, :], lbt[:, 7, c:c + 1], None, ALU.mult)
                link(last)

            def take_rows(n, dst):
                full(n)
                u = units.take()
                for t in range(TT):
                    last = v.tensor_scalar(dst[:, t, :], psum[:, u % UNITS, t * 256:(t + 1) * 256],
                                           cols[:, 1, t:t + 1], None, ALU.mult)
                last.then_inc(unit_free, 1)
                after(n)

            def gqa_out(g, u):
                return v.tensor_copy(mix2[:, g // 2, :], psum[:, u % UNITS, 0:T])

            early, later = attention(4, QH, 2, 1.0 / 8, gqa_out, lambda h: h + 2 < 9 and prepare(h + 2),
                                     lambda h: collect(h + 1))
            for m in range(2):
                evac_scaled(C_WIN2 + m, aqk[:, 2 * m:2 * m + 2, :], 6)
            full(C_WIN2 + 2)
            u = units.take()
            tt(aqk[:, 4, :], psum[:, u % UNITS, 0:T], rstd[:, 2, :], ALU.mult)
            for t in range(TT):
                last = v.tensor_scalar(av2[:, t, :], psum[:, u % UNITS, T + t * P:T + (t + 1) * P],
                                       cols[:, 1, t:t + 1], None, ALU.mult)
            last.then_inc(unit_free, 1)
            after(C_WIN2 + 2)
            evac_scaled(C_WIN2 + 3, ff[:, 0:2, :], 6)
            dve.wait_ge(qk_std, 1)
            v.reciprocal(cden[0:10, 1, :], cden[0:10, 0, :]).then_inc(qk_rstd, 1)
            evac_scaled(C_WIN2 + 4, ff[:, 2:4, :], 6)
            for n, j0 in enumerate((0, 2, 4)):
                w = min(2, 5 - j0)
                dve.wait_ge(qk_row, n + 1)
                u = units.take()
                row = psum[:, u % UNITS, 0:w * T].rearrange("p (a t) -> p a t", a=w)
                v.scalar_tensor_tensor(aqn[:, j0:j0 + w, :], row, sm("q_g" if j0 < 4 else "k_g"), aqk[:, j0:j0 + w, :],
                                       ALU.mult, ALU.mult).then_inc(unit_free, 1)
            forget(0)
            evac_scaled(C_WIN2 + 5, fb[:, 0:2, :], 6)
            for n, j0 in enumerate((0, 2, 4)):
                w = min(2, 5 - j0)
                cos, sin = (cn(x, 0, T).unsqueeze(1).to_broadcast([P, w, T]) for x in ("cos", "sin"))
                dve.wait_ge(qk_rot, n + 1)
                u = units.take()
                row = psum[:, u % UNITS, 0:w * T].rearrange("p (a t) -> p a t", a=w)
                if n:
                    dve.wait_ge(roped, n)
                tt(rtmp[:, 0:w, :], row, sin, ALU.mult).then_inc(unit_free, 1)
                link(tt(aqk[:, j0:j0 + w, :], aqn[:, j0:j0 + w, :], cos, ALU.mult))
                dve.wait_ge(unit_free, u + 1)
                tt(aqk[:, j0:j0 + w, :], aqk[:, j0:j0 + w, :], rtmp[:, 0:w, :], ALU.add).then_inc(roped, 1)
            forget(1)
            evac_scaled(C_WIN2 + 6, fb[:, 2:4, :], 6)
            dve.wait_ge(dup_done, 1)
            u = units.take()
            v.tensor_copy(kdup[:], unit_view(u)).then_inc(unit_free, 1)
            forget(2)
            for m in range(2):
                evac_scaled(C_WIN2 + 7 + m, qh[:, 2 * m:2 * m + 2, :], 6)
            forget(3)
            tt(Kc[:], kf[:], kb[:], ALU.add).then_inc(forward_ready, 1)
            dve.wait_ge(forward_ready, 1)
            v.nop().then_inc(forget_ready, 1)
            for m in range(2):
                take_rows(C_WIN2 + 9 + m, v2[:, :, 256 * m:256 * (m + 1)])
            early()
            for m in range(2):
                evac_scaled(C_WIN2 + 11 + m, hgate[:, 2 * m:2 * m + 2, :], 6)

            def prepare(i):
                if i == 0:
                    v.memset(Lf[:], 1.0).then_inc(forward_next, 1)
                    return
                h = 2 ** (i - 1)
                kk, qq = ((Kc, Qc), (Kc2, Qc2))[i % 2]
                dve.wait_ge(forward_next, i)
                if i >= 2:
                    dve.wait_ge(level_done, 2 * (i - 1))
                (fl, fr), (lfl, lfr) = sides(ff, h), sides(Lf, h)
                tt(sides(kk, h)[0], sides(kf, h)[0], lfl, ALU.mult)
                tt(sides(qq, h)[1], sides(qh, h)[1], fr, ALU.mult).then_inc(forward_ready, 1)
                if i == 8:
                    return
                wide = [P, 4 * T // (2 * h), h]
                dve.wait_ge(forward_ready, i + 1)
                link(tt(lfl, lfl, fr[:, :, h - 1:h].to_broadcast(wide), ALU.mult))
                tt(fr, fr, fl[:, :, h - 1:h].to_broadcast(wide), ALU.mult).then_inc(forward_next, 1)

            collected = [0]

            def collect(i):
                if i:
                    dve.wait_ge(unit_free, collected[0])
                for hp in range(2):
                    dve.wait_ge(level_done, 2 * i + hp + 1)
                    u = units.take()
                    got = psum[:, u % UNITS, :].rearrange("p (h c t) -> p h c t", h=2, c=2)
                    at = hp * 4 * T
                    step_c, at = (P, at + P) if i == 8 else (T + P, at)
                    base = AT_flat[:, at:at + 1]
                    dst = bass.AP(base.tensor, base.offset, [base.ap[0], [2 * T, 2], [step_c, 2], [1, P]])
                    wide = [P, 2, 2, P]
                    if i == 0:
                        ins = tt(dst, got, ident.unsqueeze(1).unsqueeze(1).to_broadcast(wide), ALU.mult)
                    elif i < 8:
                        ins = v.copy_predicated(dst, mask[:, i - 1, :].unsqueeze(1).unsqueeze(1).to_broadcast(wide), got)
                    else:
                        ins = v.tensor_copy(dst, got)
                    ins.then_inc(unit_free, 1)
                    collected[0] = u + 1

            dve.wait_ge(s_mask, 16)
            prepare(0)
            prepare(1)
            collect(0)

            later()
            dve.wait_ge(unit_free, units.n)
            v.nop().then_inc(A_ready, 1)
            for m in range(2):
                q = slice(2 * m, 2 * m + 2)
                link(v.tensor_copy(yh[:, q, :], mix2[:, q, :]))
                last = tt(yl[:, q, :], mix2[:, q, :], f32(yh[:, q, :]), ALU.subtract)
            last.then_inc(mix_split, 1)
            dve.wait_ge(hg_act, 2)
            for hp in range(2):
                dve.wait_ge(rec_done, hp + 1)
                u = units.take()
                v.tensor_copy(mix2[:, 4 + 2 * hp:6 + 2 * hp, :], unit_view(u)).then_inc(unit_free, 1)
            dve.wait_ge(rec_std, 1)
            v.reciprocal(cden[0:4, 1, :], cden[0:4, 0, :]).then_inc(rec_rstd, 1)
            for hp in range(2):
                dve.wait_ge(rec_row, hp + 1)
                u = units.take()
                q = mix2[:, 4 + 2 * hp:6 + 2 * hp, :]
                v.scalar_tensor_tensor(q, unit_view(u), sm("hg_g"), q, ALU.mult, ALU.mult).then_inc(unit_free, 1)
                dve.wait_ge(unit_free, u + 1)
                link(tt(q, q, hgate[:, 2 * hp:2 * hp + 2, :], ALU.mult))
                p = slice(4 + 2 * hp, 6 + 2 * hp)
                link(v.tensor_copy(yh[:, p, :], q))
                tt(yl[:, p, :], q, f32(yh[:, p, :]), ALU.subtract).then_inc(rec_ready, 1)

            def post(k, y, gain_name, next_name):
                recip(k)
                dve.wait_ge(rstd_ready, k + 1)
                for m in range(4):
                    link(tt(y[:, 2 * m:2 * m + 2, :], y[:, 2 * m:2 * m + 2, :], two(rstd[:, k % 4, :]), ALU.mult))
                    for c in (2 * m, 2 * m + 1):
                        last = v.scalar_tensor_tensor(xT[:, c, :], y[:, c, :], sm(gain_name, c), xT[:, c, :],
                                                      ALU.mult, ALU.add)
                    last.then_inc(x_new, 1)
                    upd[0] += 1
                    if next_name:
                        dve.wait_ge(x_new, upd[0])
                        gain(next_name, m)

            y_dst = lambda m: yT[:, 2 * m:2 * m + 2, :]
            copy_units(C_WO2, y_dst)
            dve.wait_ge(unit_free, units.n)
            post(7, yT, "post_mix_g", "pre_x_g")
            after(C_Q2)
            recip(8)
            dve.wait_ge(rstd_ready, 9)
            early, later = attention(12, 4, 1, 1.0 / 16, cross_out)
            for m in range(4):
                if m == 3:
                    early()
                evac_scaled(C_Q2 + m, qT[:, 2 * m:2 * m + 2, :], 8)
            later()
            copy_units(C_XO2, y_dst)
            dve.wait_ge(unit_free, units.n)
            post(9, yT, "post_x_g", "pre_ffn_g")
            v.memset(upad2[:, :, :, 0:1], 0.0)
            link(v.memset(upad2[:, :, :, T + 1:T + 2], 0.0))
            after(C_FFN)
            recip(10)
            dve.wait_ge(rstd_ready, 11)

            u_ffn = units.n

            def ffn_step(f, i, at=0):
                c0 = 2 * (C_FFN if f == 0 else C_FFN + 2 + 3 * (f - 1))
                b = f % 2
                for half in range(2):
                    u = u_ffn + 2 * f + half
                    if f == 0:
                        rest.upto(c0 + 2 * half + 3)
                    dve.wait_ge(half_done, i * PASS + (c0 + 2 * half + 2))
                    tt(upad2[:, b, 2 * half:2 * half + 2, 1:T + 1], unit_view(u), two(rstd[:, 2, :]),
                       ALU.mult).then_inc(unit_free, 1)
                    if f == 0:
                        rest.upto(c0 + 2 * half + 5)
                    elif c0 + 2 * half + 5 + at < HALVES:
                        subtract(c0 + 2 * half + 5, i)
                    dve.wait_ge(unit_free, i * 4 + (u + 1))
                    n = 12 * f + 6 * half
                    for tap in (1, 0, 2):
                        for j in range(2):
                            jj = 2 * half + j
                            col = SMALL["ffn_w"] + 16 * f + 4 * jj
                            w = small[:, bass.ds(i * 32 + (col + tap), 1)]
                            x = upad2[:, b, jj, tap:tap + T]
                            if tap == 1:
                                bias = small[:, bass.ds(i * 32 + (col + 3), 1)]
                                ins = v.tensor_scalar(fconv[:, b, jj, :], x, w, bias, ALU.mult, ALU.add)
                            else:
                                dve.wait_ge(fconv_steps, i * 24 + (n - 1))
                                ins = v.scalar_tensor_tensor(fconv[:, b, jj, :], x, w, fconv[:, b, jj, :],
                                                             ALU.mult, ALU.add)
                            ins.then_inc(fconv_steps, 1)
                            n += 1
                dve.wait_ge(fconv_steps, i * 24 + (12 * f + 12))
                dve.wait_ge(fsilu, i * 2 + (f + 1))
                hidden(b, fconv[:, b, 0:2, :], fconv[:, b, 2:4, :], fact_ready)
                if f and c0 + 9 < HALVES:
                    subtract(c0 + 9, i)

            ffn_step(0, 0)
            whole = loop_steps(C_FFN, FSTEPS, lambda t, i: ffn_step(t + 1, i))
            for t in range(2 * whole, FSTEPS - 1):
                ffn_step(t + 1, 0)
            for m in range(4):
                if m < 3:
                    dve.wait_ge(sum_done, 3 + m + 1)
                else:
                    dve.wait_ge(half_done, HALVES)
                v.tensor_copy(yF[:, 2 * m:2 * m + 2, :],
                              psum[:, ACC + m, :].rearrange("p (j t) -> p j t", j=2)).then_inc(y_ready, 1)
            dve.wait_ge(y_ready, 4)
            post(11, yF, "post_ffn_g", None)


def _constants():
    c = np.zeros((P, NCONST), np.float32)
    p = np.arange(P)
    t = np.arange(T)

    def put(name, a, at=0):
        c[:a.shape[0], CONST[name] + at:CONST[name] + at + a.shape[1]] = a

    put("ident", np.eye(P))
    put("ones", np.ones((P, P)))
    for i, w in enumerate(POOL_W):
        put("rcnt", np.broadcast_to(np.float32(1) / np.minimum(t[:PADW] + 1, w).astype(np.float32), (P, PADW)), PADW * i)
    inv = np.power(np.float32(10000.0), -np.arange(16, dtype=np.float32) / np.float32(16)).astype(np.float32)
    ang = np.concatenate([(t // 64).astype(np.float32)[:, None] * inv, (t % 64).astype(np.float32)[:, None] * inv], 1)
    pair = ang[:, (p % 64) // 2].T
    put("cos", np.cos(pair))
    put("sin", np.sin(pair))
    rot = np.zeros((P, P))
    rot[p[1::2], p[0::2]] = -1
    rot[p[0::2], p[1::2]] = 1
    put("rot", rot)
    for j in range(2):
        put("dup", (p[:, None] == 64 * j + p[None, :] % 64).astype(float), 128 * j)
    for j in range(5):
        put("qk_sum", (2 * j + p[:, None] // 64 == np.arange(10)[None, :]).astype(float), 10 * j)
    for h in range(HG):
        put("hg_sum", np.broadcast_to(np.arange(4)[None, :] == h, (P, 4)).astype(float), 4 * h)
    put("prio", np.broadcast_to(np.tile([4.0, 3.0, 2.0, 1.0], 2), (P, 8)))
    x = p[:, None] ^ p[None, :]
    m = np.zeros((P, 8, P), np.int32)
    for i in range(7):
        m[:, i, :] = (x >> i) == 1
    m[:, 7, :] = x == 0
    return c, m


def _tiles(w, rows, c0, width):
    return w.reshape(rows, P, -1)[:, :, c0:c0 + width].transpose(1, 0, 2).reshape(P, rows * width)


def _stream(a):
    s = np.zeros((CHUNKS, 2, P, HW), np.float32)

    def halves(w, c0):
        return [_tiles(w, DK, c0 + P * j, P) for j in range(2)]

    def row_halves(w, c0):
        return [_tiles(w[512 * j:512 * (j + 1)], 4, c0, 256) for j in range(2)]

    def units(at, w, order, c0=0, cut=halves):
        for i, u in enumerate(order):
            s[at + i] = cut(w, c0 + 256 * u)

    units(C_WIN, a["w_in"][0], range(24))
    s[C_POOL, 1] = a["w_pool_grp"][0].transpose(1, 0, 2).reshape(P, 1024)
    for m in range(4):
        s[C_MERGE + m, 0] = _tiles(a["w_a_out"][0], 4, 256 * m, 256)
        s[C_MERGE + m, 1] = _tiles(a["w_c_out"][0], 4, 256 * m, 256)
    for suffix, k, v, q, o in (("", C_K1, C_V1, C_Q1, C_XO1), ("_2", C_K2, C_V2, C_Q2, C_XO2)):
        units(k, a["w_xkv" + suffix][0], range(4))
        units(v, a["w_xkv" + suffix][0], range(4), D, row_halves)
        units(q, a["w_xq" + suffix][0], range(4))
        units(o, a["w_xo" + suffix][0], range(4))
    units(C_WO, a["w_o"][0], range(4))
    units(C_WIN2, a["w_in_2"][0], WIN2_ORDER)
    units(C_WIN2 + WIN2_ORDER.index(9), a["w_in_2"][0], (9, 10), 0, row_halves)
    units(C_WO2, a["w_out_2"][0], range(4))

    def steps(first, at, count, gate, up, down):
        for e in range(count):
            g = first if e == 0 else at + 2 + 3 * (e - 1)
            s[g], s[g + 1] = gate(e), up(e)
            s[at + 3 * count - 1 if e == count - 1 else at + 3 * e + 4] = down(e).reshape(2, P, D)

    steps(C_E0, C_MOE, EXPERTS, lambda e: halves(a["w_e_gate"][0, e], 0), lambda e: halves(a["w_e_up"][0, e], 0),
          lambda e: a["w_e_down"][0, e])
    steps(C_FFN, C_FFN, FSTEPS, lambda f: halves(a["w_up_2"][0], 256 * f), lambda f: halves(a["w_up_2"][0], FF + 256 * f),
          lambda f: a["w_down_2"][0, 256 * f:256 * (f + 1)])
    return s.reshape(HALVES, P, HW)


def _small(a):
    s = np.zeros((P, NSMALL), np.float32)

    def put(name, x, at=0):
        y = np.asarray(x).reshape(-1, P).T
        s[:, SMALL[name] + at:SMALL[name] + at + y.shape[1]] = y

    for name, key in (("mix_g", "norm_mix_g"), ("pool_s", "pool_scale"), ("x_g", "norm_x_g"), ("mem_g", "norm_mem_g"),
                      ("ffn_g", "norm_ffn_g"), ("f_g", "norm_f_g"), ("conv_b", "conv_a_b"), ("ln_g", "ln_a_g"),
                      ("ln_b", "ln_a_b"), ("c_w", "conv_c_w"), ("conv_w", "conv_a_w"), ("pre_mix_g", "pre_mix_g_2"),
                      ("post_mix_g", "post_mix_g_2"), ("pre_x_g", "pre_x_g_2"), ("mem2_g", "mem_norm_g_2"),
                      ("post_x_g", "post_x_g_2"), ("pre_ffn_g", "pre_ffn_g_2"), ("post_ffn_g", "post_ffn_g_2"),
                      ("hg_g", "hg_out_norm_g_2")):
        put(name, a[key])
    for name, key in (("q_g", "q_norm_g_2"), ("k_g", "k_norm_g_2")):
        put(name, np.tile(a[key].reshape(-1), 2))
    put("lb", a["hg_lb_2"].transpose(1, 0, 2))
    s[0:4, SMALL["r_b"]] = a["b_rg"][0]
    s[4:20, SMALL["r_b"]] = a["b_re"][0]
    w, b = a["conv_w_2"][0], a["conv_b_2"][0]
    for f in range(FSTEPS):
        for i in range(4):
            c0 = FF * (i // 2) + 256 * f + P * (i % 2)
            for j in range(3):
                put("ffn_w", w[j, c0:c0 + P], 16 * f + 4 * i + j)
            put("ffn_w", b[c0:c0 + P], 16 * f + 4 * i + 3)
    return s


def _turned(x):
    return np.ascontiguousarray(x[0].T.reshape(DK, P, T).transpose(1, 0, 2))


def kernel(**inputs):
    import concourse.bacc as _bacc
    from concourse.bass_utils import run_bass_kernel_spmd as _run

    a = {k: np.asarray(v) for k, v in inputs.items()}
    const, mask = _constants()
    router = np.concatenate([a["w_rg"][0], a["w_re"][0]], axis=1)
    arrays = {
        "stream": _stream(a),
        "x_t": _turned(a["x"]),
        "mem_t": _turned(a["mem"]),
        "mem2_t": _turned(a["mem_2"]),
        "small": _small(a),
        "const": const,
        "mask": mask,
        "router": np.ascontiguousarray(router.reshape(DK, P, 20).transpose(1, 0, 2)),
    }
    nc = _bacc.Bacc("TRN2", target_bir_lowering=False, num_devices=1)
    args = [nc.dram_tensor(k + "_in", x.shape, mybir.dt.from_np(x.dtype), kind="ExternalInput").ap() for k, x in arrays.items()]
    out = nc.dram_tensor("out_t", (P, DK, T), F32, kind="ExternalOutput").ap()
    build(nc, *args, out)
    r = _run(nc, [{k + "_in": x for k, x in arrays.items()}], core_ids=[0])
    got = r.results[0]["out_t"]
    return np.ascontiguousarray(got.transpose(1, 0, 2).reshape(D, T).T)[None]
```
